# Optimizing a Trainium2 kernel written in Bass

```python
import jax, jax.numpy as jnp
from jax import lax
import numpy as np

D_MODEL = 1024
BATCH = 1
SEQ = 256
DEPTH = 2

EPS = 1e-6
N_BRANCHES = 2

GM_GROUPS = 8
GM_GROUP_CH = D_MODEL // GM_GROUPS
GM_WIDTH = GM_GROUPS * GM_GROUP_CH
GM_CHUNK = 128

MLA_HEADS = 16
QK_NOPE = 64
QK_ROPE = 32
QK_DIM = QK_NOPE + QK_ROPE
V_DIM = 64
Q_LORA = D_MODEL // 2
KV_LORA = D_MODEL // 4
ROPE_THETA = 10000.0
ATT_BLOCK = 128

OFF_U = 0
OFF_V = OFF_U + GM_WIDTH
OFF_CQ = OFF_V + GM_WIDTH
OFF_CKV = OFF_CQ + Q_LORA
OFF_KR = OFF_CKV + KV_LORA
OFF_GATE = OFF_KR + QK_ROPE
D_IN = OFF_GATE + N_BRANCHES * D_MODEL

DENSE_FF = 2816
N_EXPERTS = 8
TOP_K = 2
EXPERT_FF = 2816
NUM_DENSE = (DEPTH + 1) // 2
NUM_MOE = DEPTH // 2

kernel_name = "hybrid_gmlp_mla_gated_moe_block"

def rms_norm(x, g):
    xf = x.astype(jnp.float32)
    y = xf * lax.rsqrt(jnp.mean(xf * xf, axis=-1, keepdims=True) + EPS)
    return (y * g.astype(jnp.float32)).astype(x.dtype)

def layer_norm(x, g, b):
    xf = x.astype(jnp.float32)
    mu = jnp.mean(xf, axis=-1, keepdims=True)
    xc = xf - mu
    y = xc * lax.rsqrt(jnp.mean(xc * xc, axis=-1, keepdims=True) + EPS)
    return (y * g.astype(jnp.float32) + b.astype(jnp.float32)).astype(x.dtype)

def rope_tables(seq_len):
    pos = jnp.arange(seq_len, dtype=jnp.float32)
    inv_freq = ROPE_THETA ** (-jnp.arange(0, QK_ROPE, 2, dtype=jnp.float32) / QK_ROPE)
    ang = pos[:, None] * inv_freq[None, :]
    return jnp.cos(ang), jnp.sin(ang)

def apply_rope(x, cos, sin):
    c = cos[None, :, None, :].astype(x.dtype)
    s = sin[None, :, None, :].astype(x.dtype)
    x1, x2 = jnp.split(x, 2, axis=-1)
    return jnp.concatenate([x1 * c - x2 * s, x2 * c + x1 * s], axis=-1)

def swiglu(h, w_gu, w_down):
    g, u = jnp.split(h @ w_gu, 2, axis=-1)
    return (jax.nn.silu(g) * u) @ w_down

def gmlp_branch(a_u, a_v, v_g, v_b, w_s, b_s):
    B, S, _ = a_u.shape
    u = jax.nn.gelu(a_u)
    v = layer_norm(jax.nn.gelu(a_v), v_g, v_b)
    vc = v.reshape(B, S // GM_CHUNK, GM_CHUNK, GM_GROUPS, GM_GROUP_CH)
    causal = jnp.tril(jnp.ones((GM_CHUNK, GM_CHUNK), dtype=bool))
    ws = jnp.where(causal[None], w_s, jnp.zeros((), w_s.dtype))
    mixed = jnp.einsum('gts,bcsgd->bctgd', ws, vc) + b_s.T[None, None, :, :, None]
    return u * mixed.reshape(B, S, GM_WIDTH)

def causal_block_attention(q, k, v):
    B, S, H, Dq = q.shape
    nb = S // ATT_BLOCK
    scale = 1.0 / float(np.sqrt(Dq))
    qb = q.reshape(B, nb, ATT_BLOCK, H, Dq).transpose(1, 0, 2, 3, 4)
    kpos = jnp.arange(S)

    def one_block(args):
        q_blk, i = args
        qpos = i * ATT_BLOCK + jnp.arange(ATT_BLOCK)
        s = jnp.einsum('bqhd,bkhd->bhqk', q_blk, k, preferred_element_type=jnp.float32) * scale
        s = jnp.where(kpos[None, :] <= qpos[:, None], s, jnp.float32(-1e30))
        p = jax.nn.softmax(s, axis=-1).astype(v.dtype)
        return jnp.einsum('bhqk,bkhd->bqhd', p, v)

    out = lax.map(one_block, (qb, jnp.arange(nb)))
    return out.transpose(1, 0, 2, 3, 4).reshape(B, S, H * v.shape[-1])

def mla_branch(c_q, c_kv, k_r, q_lat_g, w_uq, kv_lat_g, w_ukv, q_norm_g, k_norm_g, cos, sin):
    B, S, _ = c_q.shape
    q = (rms_norm(c_q, q_lat_g) @ w_uq).reshape(B, S, MLA_HEADS, QK_DIM)
    kv = (rms_norm(c_kv, kv_lat_g) @ w_ukv).reshape(B, S, MLA_HEADS, QK_NOPE + V_DIM)
    k_nope, v = kv[..., :QK_NOPE], kv[..., QK_NOPE:]
    k_rope = jnp.broadcast_to(k_r[:, :, None, :], (B, S, MLA_HEADS, QK_ROPE))
    k = jnp.concatenate([k_nope, k_rope], axis=-1)
    q = rms_norm(q, q_norm_g)
    k = rms_norm(k, k_norm_g)
    q = jnp.concatenate([q[..., :QK_NOPE], apply_rope(q[..., QK_NOPE:], cos, sin)], axis=-1)
    k = jnp.concatenate([k[..., :QK_NOPE], apply_rope(k[..., QK_NOPE:], cos, sin)], axis=-1)
    return causal_block_attention(q, k, v)

def moe_swiglu(h, w_router, b_router, w_gu, w_down):
    B, S, D = h.shape
    xf = h.reshape(B * S, D)
    logits = (xf @ w_router).astype(jnp.float32) + b_router.astype(jnp.float32)
    top_vals, top_idx = lax.top_k(logits, TOP_K)
    wts = jax.nn.softmax(top_vals, axis=-1)
    combine = jnp.sum(jax.nn.one_hot(top_idx, N_EXPERTS, dtype=jnp.float32) * wts[..., None], axis=1)
    combine = combine.astype(h.dtype)
    y = jnp.zeros_like(xf)
    for e in range(N_EXPERTS):
        y = y + combine[:, e:e + 1] * swiglu(xf, w_gu[e], w_down[e])
    return y.reshape(B, S, D)

def setup_inputs(seed: int = 0) -> dict:
    key = jax.random.key(seed)
    ks = iter(jax.random.split(key, 32))

    def nrm(shape, fan_in):
        return jax.random.normal(next(ks), shape, jnp.float32) * (fan_in ** -0.5)

    def gain(shape):
        return 1.0 + 0.05 * jax.random.normal(next(ks), shape, jnp.float32)

    L = DEPTH
    return {
        "x": jax.random.normal(next(ks), (BATCH, SEQ, D_MODEL), jnp.float32),
        "mix_norm_g": gain((L, D_MODEL)),
        "w_in": nrm((L, D_MODEL, D_IN), D_MODEL),
        "gm_v_norm_g": gain((L, GM_WIDTH)),
        "gm_v_norm_b": 0.02 * jax.random.normal(next(ks), (L, GM_WIDTH), jnp.float32),
        "gm_w_spatial": nrm((L, GM_GROUPS, GM_CHUNK, GM_CHUNK), GM_CHUNK),
        "gm_b_spatial": gain((L, GM_GROUPS, GM_CHUNK)),
        "gm_w_proj": nrm((L, GM_WIDTH, D_MODEL), GM_WIDTH),
        "mla_q_lat_g": gain((L, Q_LORA)),
        "mla_w_uq": nrm((L, Q_LORA, MLA_HEADS * QK_DIM), Q_LORA),
        "mla_kv_lat_g": gain((L, KV_LORA)),
        "mla_w_ukv": nrm((L, KV_LORA, MLA_HEADS * (QK_NOPE + V_DIM)), KV_LORA),
        "mla_q_norm_g": gain((L, QK_DIM)),
        "mla_k_norm_g": gain((L, QK_DIM)),
        "mla_w_proj": nrm((L, MLA_HEADS * V_DIM, D_MODEL), MLA_HEADS * V_DIM),
        "w_out": nrm((L, D_MODEL, D_MODEL), D_MODEL),
        "ffn_norm_g": gain((L, D_MODEL)),
        "dense_w_gu": nrm((NUM_DENSE, D_MODEL, 2 * DENSE_FF), D_MODEL),
        "dense_w_down": nrm((NUM_DENSE, DENSE_FF, D_MODEL), DENSE_FF),
        "moe_w_router": nrm((NUM_MOE, D_MODEL, N_EXPERTS), D_MODEL),
        "moe_b_router": 0.01 * jax.random.normal(next(ks), (NUM_MOE, N_EXPERTS), jnp.float32),
        "moe_w_gu": nrm((NUM_MOE, N_EXPERTS, D_MODEL, 2 * EXPERT_FF), D_MODEL),
        "moe_w_down": nrm((NUM_MOE, N_EXPERTS, EXPERT_FF, D_MODEL), EXPERT_FF),
    }

def reference(x, mix_norm_g, w_in, gm_v_norm_g, gm_v_norm_b, gm_w_spatial, gm_b_spatial, gm_w_proj,
              mla_q_lat_g, mla_w_uq, mla_kv_lat_g, mla_w_ukv, mla_q_norm_g, mla_k_norm_g, mla_w_proj,
              w_out, ffn_norm_g, dense_w_gu, dense_w_down, moe_w_router, moe_b_router, moe_w_gu, moe_w_down):
    B, S, D = x.shape
    cos, sin = rope_tables(S)
    for l in range(DEPTH):
        h = rms_norm(x, mix_norm_g[l])
        z = h @ w_in[l]
        y_a = gmlp_branch(z[..., OFF_U:OFF_V], z[..., OFF_V:OFF_CQ],
                          gm_v_norm_g[l], gm_v_norm_b[l], gm_w_spatial[l], gm_b_spatial[l]) @ gm_w_proj[l]
        y_b = mla_branch(z[..., OFF_CQ:OFF_CKV], z[..., OFF_CKV:OFF_KR], z[..., OFF_KR:OFF_GATE],
                         mla_q_lat_g[l], mla_w_uq[l], mla_kv_lat_g[l], mla_w_ukv[l],
                         mla_q_norm_g[l], mla_k_norm_g[l], cos, sin) @ mla_w_proj[l]
        gates = jax.nn.sigmoid(z[..., OFF_GATE:].reshape(B, S, N_BRANCHES, D))
        merged = gates[..., 0, :] * y_a + gates[..., 1, :] * y_b
        x = x + merged @ w_out[l]
        h2 = rms_norm(x, ffn_norm_g[l])
        if l % 2 == 0:
            x = x + swiglu(h2, dense_w_gu[l // 2], dense_w_down[l // 2])
        else:
            m = l // 2
            x = x + moe_swiglu(h2, moe_w_router[m], moe_b_router[m], moe_w_gu[m], moe_w_down[m])
    return x


_drawn_inputs = setup_inputs


def setup_inputs(seed=0):
    import zlib

    import numpy as np

    out = dict(_drawn_inputs(seed))
    spreads = {}
    factors = {'gm_v_norm_b': 3.368,
     'mla_q_lat_g': 3.179,
     'mla_q_norm_g': 3.249,
     'mla_k_norm_g': 8.0,
     'moe_b_router': 4.514}
    for name, (base, spread) in spreads.items():
        noise = np.random.default_rng([zlib.crc32(name.encode()), seed]).standard_normal(out[name].shape)
        drawn = base * np.exp(spread * noise) if base else spread * noise
        out[name] = __import__('jax').numpy.asarray(drawn.astype(out[name].dtype))
    for name, factor in factors.items():
        out[name] = (out[name] * factor).astype(out[name].dtype)
    return out
```

```python
from contextlib import ExitStack

import concourse.bass as bass
from concourse import mybir

F32 = mybir.dt.float32
F32R = mybir.dt.float32r
I32 = mybir.dt.int32
U32 = mybir.dt.uint32
ALU = mybir.AluOpType
ACT = mybir.ActivationFunctionType
AX = mybir.AxisListType

P = 128
EPS = 1e-6
RAW, SPLIT, LEAD = 4, 3, 3
CHUNK = 2048
STRIP = 512
GELU_A = 0.044715
GELU_C = 0.7978845608028654
RSQRT_SEED = float(0x5F3759DF)
NEG = -1e30


class Chain:

    def __init__(self, eng, sem, base=0):
        self.eng, self.sem, self.base, self.n = eng, sem, base, 0

    def link(self, ins):
        self.n += 1
        ins.then_inc(self.sem, 1)
        self.eng.wait_ge(self.sem, self.base + self.n)


def decoder_trunk(nc, x, mix_norm_g, w_in, gm_v_norm_g, gm_v_norm_b, gm_w_spatial, gm_b_spatial, gm_w_proj,
                  mla_q_lat_g, mla_w_uq, mla_kv_lat_g, mla_w_ukv, mla_q_norm_g, mla_k_norm_g, mla_w_proj,
                  w_out, ffn_norm_g, dense_w_gu, dense_w_down, moe_w_router, moe_b_router, moe_w_gu,
                  moe_w_down, shape_consts, out):
    _, S, D = x.shape
    L = w_in.shape[0]
    TT = S // P
    KD = D // P
    NG = gm_w_spatial.shape[1]
    QL, KVL = mla_w_uq.shape[1], mla_w_ukv.shape[1]
    DQ = mla_q_norm_g.shape[1]
    H = mla_w_uq.shape[2] // DQ
    DV = mla_w_proj.shape[1] // H
    DN = mla_w_ukv.shape[2] // H - DV
    DR = DQ - DN
    HR = DR // 2
    E = moe_w_gu.shape[1]
    FF = moe_w_down.shape[2]
    KF = FF // P
    assert TT == 2 and D == 1024 and dense_w_down.shape[1] == FF and H * DV == D and 2 * DV == P
    OFF_V, OFF_CQ = D, 2 * D
    OFF_CKV = OFF_CQ + QL
    OFF_GATE = OFF_CKV + KVL + DR
    SCALE = float(DQ) ** -0.5
    KQ, KKV = QL // P, KVL // P
    HC = 256
    GUS = FF // HC
    PAIRS = H // 2
    HPS = STRIP // (DN + DV)

    chunks = []

    def wide(w, c0, width):
        wk = w.rearrange("(k p) n -> p k n", p=P)
        kt = wk.shape[1]
        first = len(chunks)
        for k0 in range(0, kt, 4):
            n = min(4, kt - k0)
            h = n // 2
            chunks.append(([(0, h, wk[:, k0:k0 + h, c0:c0 + width]),
                            (h * width, n - h, wk[:, k0 + h:k0 + n, c0:c0 + width])], n, width))
        return first, len(chunks)

    DOWN_K = [2, 1] * 6 + [2, 2]
    assert sum(DOWN_K) == KF
    GU_CHUNKS = GUS * KD // 4
    PER_EXPERT = GU_CHUNKS + len(DOWN_K)

    def gu_pieces(w_gu, j, k0):
        v = w_gu.rearrange("(k p) n -> p k n", p=P)
        return [v[:, k0:k0 + 4, hh * FF + j * HC:hh * FF + (j + 1) * HC] for hh in range(2)]

    def down_pieces(w_down, d):
        k0, n = sum(DOWN_K[:d]), DOWN_K[d]
        v = w_down.rearrange("(k p) n -> p k n", p=P)
        if n == 2:
            return [v[:, k0, :], v[:, k0 + 1, :]]
        return [v[:, k0, 0:D // 2], v[:, k0, D // 2:D]]

    plan = []
    strip_no = [0]
    strip_at = {}

    def strip(l, what, j, w, c0):
        width = min(STRIP, {"ckv": KVL + DR}.get(what, STRIP))
        a, b = wide(w, c0, width)
        strip_at[l, what, j] = strip_no[0]
        plan.append(("strip", l, what, j, a, b, width, strip_no[0]))
        strip_no[0] += 1

    for l in range(L):
        plan.append(("norm", l, 0))
        strip(l, "cq", 0, w_in[l], OFF_CQ)
        strip(l, "ckv", 0, w_in[l], OFF_CKV)
        plan.append(("latent_norm", l))
        plan.append(("spatial_weights", l))
        strip(l, "v", 0, w_in[l], OFF_V)
        plan.append(("latent_turns", l))
        strip(l, "v", 1, w_in[l], OFF_V + STRIP)
        strip(l, "uq", 0, mla_w_uq[l], 0)
        plan.append(("layer_norm", l))
        for j in range(1, H * DQ // STRIP):
            strip(l, "uq", j, mla_w_uq[l], j * STRIP)
        for j in range(H // HPS):
            strip(l, "ukv", j, mla_w_ukv[l], j * STRIP)
            if j == 0:
                plan.append(("mix_tokens", l))
            if j in (1, 2):
                plan.append(("q_norm", l, j - 1))
        strip(l, "u", 0, w_in[l], 0)
        plan.append(("k_norm", l, 0))
        strip(l, "u", 1, w_in[l], STRIP)
        plan.append(("k_norm", l, 1))
        plan.append(("a_turns", l, 0))
        slots = [("attention", l, s) for s in range(PAIRS + 3)]
        plan.append(slots.pop(0))
        for what, j in (("ga", 0), ("pa", 0), ("ga", 1), ("pa", 1), ("gb", 0), ("pb", 0), ("gb", 1), ("pb", 1)):
            if (what, j) == ("pb", 0):
                plan += slots
                slots = []
            src, c0 = {"ga": (w_in[l], OFF_GATE), "gb": (w_in[l], OFF_GATE + D), "pa": (gm_w_proj[l], 0),
                       "pb": (mla_w_proj[l], 0)}[what]
            strip(l, what, j, src, c0 + j * STRIP)
            if (what, j) == ("ga", 0):
                plan.append(("a_turns", l, 1))
            plan += slots[:2]
            slots = slots[2:]
        plan.append(("merged_turns", l))
        for j in range(2):
            strip(l, "wo", j, w_out[l], j * STRIP)
        plan.append(("norm", l, 1))
        if l % 2 == 0:
            for j in range(GUS):
                a = len(chunks)
                for k0 in range(0, KD, 4):
                    g, u = gu_pieces(dense_w_gu[l // 2], j, k0)
                    chunks.append((("gu", g, u), 4, STRIP))
                strip_at[l, "gu", j] = strip_no[0]
                plan.append(("strip", l, "gu", j, a, len(chunks), STRIP, strip_no[0]))
                strip_no[0] += 1
                if j >= 1:
                    plan.append(("hidden_turn", l, j - 1))
            a = len(chunks)
            for d in range(len(DOWN_K)):
                chunks.append((("down", *down_pieces(dense_w_down[l // 2], d)), DOWN_K[d], D))
            plan.append(("hidden_turn", l, GUS - 1))
            plan.append(("down", l, a, len(chunks), strip_no[0]))
            strip_at[l, "down", 0] = strip_no[0]
            strip_no[0] += 2
    N0 = len(chunks)
    assert N0 % SPLIT == 0 and PER_EXPERT % SPLIT == 0 and PER_EXPERT % RAW == 0

    with ExitStack() as ctx:
        def sb(name, shape, dt=F32, c=ctx):
            return c.enter_context(nc.sbuf_tensor(name, shape, dt))

        def sem(name):
            return ctx.enter_context(nc.semaphore(name))

        ps = ctx.enter_context(nc.psum_tensor("ps", [P, 8, 512], F32))

        raw = sb("raw", [P, RAW, CHUNK])
        w_hi = sb("w_hi", [P, SPLIT, CHUNK], F32R)
        w_lo = sb("w_lo", [P, SPLIT, CHUNK], F32R)
        act_hi = sb("act_hi", [P, KD, S], F32R)
        act_lo = sb("act_lo", [P, KD, S], F32R)
        xres = sb("xres", [P, TT, D])
        CW = shape_consts.shape[1]
        consts = sb("consts", [P, CW])
        o = 0

        def part(n):
            nonlocal o
            o += n
            return consts[:, o - n:o]

        ident, before, ones, iota, bias_mask, cos_sin = (part(n) for n in (P, P, P, P, 2 * P, TT * 2 * HR))
        cos_sin = cos_sin.rearrange("p (t c r) -> p t c r", t=TT, c=2)
        assert o == CW
        row_sizes = [L * KD, L * KD, L * KQ, L * KKV, L * NG]
        ROWS = sum(row_sizes)
        rows = sb("rows", [ROWS, P])
        cols_t = sb("cols_t", [P, ROWS])
        row_at = [sum(row_sizes[:i]) for i in range(5)]
        mix_g, ffn_g, qlat_g, kvlat_g, b_sp = (
            cols_t[:, a:a + n].rearrange("p (l k) -> p l k", l=L) for a, n in zip(row_at, row_sizes))
        q_gain = sb("q_gain", [P, L, DQ])
        k_gain = sb("k_gain", [P, L, DQ])
        small = sb("small", [P, 16])
        rs_a = sb("rs_a", [P, 16])
        rs_t = sb("rs_t", [P, 16])
        rs_y = sb("rs_y", [P, 16], I32)

        mixer = ExitStack()
        t1_hi = sb("t1_hi", [P, KD, S], F32R, mixer)
        t1_lo = sb("t1_lo", [P, KD, S], F32R, mixer)
        bt_hi = sb("bt_hi", [P, KD, S], F32R, mixer)
        bt_lo = sb("bt_lo", [P, KD, S], F32R, mixer)
        vbuf = sb("vbuf", [P, TT, D], F32, mixer)
        tmp = sb("tmp", [P, TT, STRIP], F32, mixer)
        qb = sb("qb", [P, TT, H, DQ], F32, mixer)
        kb = sb("kb", [P, TT, H, DQ], F32, mixer)
        vv = sb("vv", [P, TT, H, DV], F32, mixer)
        ws_t = sb("ws_t", [P, NG, P], F32, mixer)
        qk_t = sb("qk_t", [P, 2, 512], F32, mixer)
        prob = sb("prob", [P, 768], F32, mixer)
        prob_t = sb("prob_t", [P, 768], F32, mixer)
        kr = sb("kr", [P, TT, DR], F32, mixer)
        soft = sb("soft", [P, 3, 4], F32, mixer)
        ws_raw = sb("ws_raw", [P, NG, P], F32, mixer)
        sq = sb("sq", [P, 768], F32, mixer)
        q_sum = sb("q_sum", [P, TT, H], F32, mixer)
        k_sum = sb("k_sum", [P, TT, H], F32, mixer)
        stats = sb("stats", [P, TT, 2, 6], F32, mixer)
        mean_var = sb("mean_var", [P, TT, 2], F32, mixer)
        mixer.close()
        ffn = ExitStack()
        hid_hi = sb("hid_hi", [P, KF, S], F32R, ffn)
        hid_lo = sb("hid_lo", [P, KF, S], F32R, ffn)
        xn = sb("xn", [P, TT, D], F32, ffn)
        xn_hi = sb("xn_hi", [P, TT, D], F32R, ffn)
        xn_lo = sb("xn_lo", [P, TT, D], F32R, ffn)
        hid = sb("hid", [P, 2, TT, HC], F32, ffn)
        sig = sb("sig", [P, TT, HC], F32, ffn)
        y_hi = sb("y_hi", [P, D], F32R, ffn)
        y_lo = sb("y_lo", [P, D], F32R, ffn)
        pick = sb("pick", [P, TT, P], F32R, ffn)
        pick_w = sb("pick_w", [P, TT], F32, ffn)
        put = sb("put", [P, S], F32R, ffn)
        slot_w = sb("slot_w", [P, 1], F32, ffn)
        wr = sb("wr", [P, KD, E], F32, ffn)
        wr_hi = sb("wr_hi", [P, KD, E], F32R, ffn)
        wr_lo = sb("wr_lo", [P, KD, E], F32R, ffn)
        br = sb("br", [P, E], F32, ffn)
        logit = sb("logit", [P, TT, E], F32, ffn)
        top = sb("top", [P, TT, 8], F32, ffn)
        top_i = sb("top_i", [P, TT, 8], U32, ffn)
        top_f = sb("top_f", [P, TT, 8], F32, ffn)
        one_a = sb("one_a", [P, TT, E], F32, ffn)
        one_b = sb("one_b", [P, TT, E], F32, ffn)
        chosen = sb("chosen", [P, TT, E], F32, ffn)
        combine = sb("combine", [P, TT, E], F32, ffn)
        place = sb("place", [P, TT, E], F32, ffn)
        rt = sb("rt", [P, TT, 4], F32, ffn)
        most = sb("most", [P, 2], I32, ffn)
        most_f = sb("most_f", [P, 2], F32, ffn)
        ffn.close()

        raw_landed = [sem(f"raw_landed{i}") for i in range(RAW)]
        raw_landed2 = [sem(f"raw_landed2_{i}") for i in range(RAW)]
        hi_done, lo_done, chunk_used = sem("hi_done"), sem("lo_done"), sem("chunk_used")
        hi_done2, lo_done2, chunk_used2 = sem("hi_done2"), sem("lo_done2"), sem("chunk_used2")
        x_landed, small_landed, out_stored = sem("x_landed"), sem("small_landed"), sem("out_stored")
        rows_landed, rows_turned, gains_ready = sem("rows_landed"), sem("rows_turned"), sem("gains_ready")
        ws_landed, wr_landed = sem("ws_landed"), sem("wr_landed")
        strip_free = [sem("strip_free0"), sem("strip_free1")]
        turn_done, turn_hi = sem("turn_done"), sem("turn_hi")
        turn_free = [sem("turn_free0"), sem("turn_free1")]
        act_own, dve_own = sem("act_own"), sem("dve_own")
        squares_done, root_done, normed_done = sem("squares_done"), sem("root_done"), sem("normed_done")
        latent_normed = sem("latent_normed")
        gelu_sq, gelu_arg, gelu_tanh = sem("gelu_sq"), sem("gelu_arg"), sem("gelu_tanh")
        v_normed, ws_masked, branch_a = sem("v_normed"), sem("ws_masked"), sem("branch_a")
        head_squares, head_sums = sem("head_squares"), sem("head_sums")
        q_ready, k_ready = sem("q_ready"), sem("k_ready")
        scores_done, scores_read, max_ready, exp_done, prob_ready = (
            sem("scores_done"), sem("scores_read"), sem("max_ready"), sem("exp_done"), sem("prob_ready"))
        merged_b, sig_done = sem("merged_b"), sem("sig_done")
        xn_hi_done, xn_lo_done, wr_hi_done, wr_lo_done = (
            sem("xn_hi_done"), sem("xn_lo_done"), sem("wr_hi_done"), sem("wr_lo_done"))
        logits_done, chosen_ready, gap_ready, gap_exp, places_done, counts_ready = (
            sem("logits_done"), sem("chosen_ready"), sem("gap_ready"), sem("gap_exp"), sem("places_done"),
            sem("counts_ready"))
        pass_sems = []
        for q in range(2):
            pass_sems.append({n: sem(f"{n}_{q}") for n in (
                "gu_free0", "gu_free1", "sig_ready", "sig_half", "hturn_done", "hturn_hi", "hturn_free0",
                "hturn_free1", "y_hi_done", "y_split", "g_done", "g_hi", "g_free0", "g_free1", "picked", "over")})

        def raw_view(slot, n, w):
            return raw[:, slot, 0:n * w].rearrange("p (k n) -> p k n", k=n)

        class Ring:

            def __init__(self, n0, landed, hi, lo, used):
                self.n0, self.landed, self.hi, self.lo, self.used = n0, landed, hi, lo, used

            def count(self, e, j):
                return self.n0 + j + PER_EXPERT * e

            def raw_slot(self, j):
                return (self.n0 + j) % RAW

            def split_slot(self, j):
                return (self.n0 + j) % SPLIT

            def load(self, sp, e, j, pieces):
                if self.n0 + j >= RAW or not isinstance(e, int) or e > 0:
                    sp.wait_ge(self.lo, self.count(e, j) - RAW + 1)
                for dst, src in pieces:
                    sp.dma_start(dst, src).then_inc(self.landed[self.raw_slot(j)], 16)

            def split_hi(self, act, e, j, n=CHUNK):
                s = self.raw_slot(j)
                act.wait_ge(self.landed[s], 32 * ((self.n0 + j) // RAW + 1) + 32 * (PER_EXPERT // RAW) * e)
                if self.n0 + j >= SPLIT or not isinstance(e, int) or e > 0:
                    act.wait_ge(self.used, self.count(e, j) - SPLIT + 1)
                nc.scalar.activation(w_hi[:, self.split_slot(j), 0:n], raw[:, s, 0:n], ACT.Copy).then_inc(self.hi, 1)

            def split_lo(self, dve, e, j, n=CHUNK):
                dve.wait_ge(self.hi, self.count(e, j) + 1)
                c = self.split_slot(j)
                nc.vector.tensor_tensor(w_lo[:, c, 0:n], raw[:, self.raw_slot(j), 0:n],
                                        w_hi[:, c, 0:n].bitcast(F32), ALU.subtract).then_inc(self.lo, 1)

            def take(self, pe, e, j):
                pe.wait_ge(self.lo, self.count(e, j) + 1)
                c = self.split_slot(j)
                return w_hi[:, c, :], w_lo[:, c, :]

        ring = Ring(0, raw_landed, hi_done, lo_done, chunk_used)
        size = [n * w for _, n, w in chunks]
        DOWN_SIZE = [n * D for n in DOWN_K]
        expert_size = [CHUNK] * GU_CHUNKS + DOWN_SIZE

        def three(dst, a_hi, a_lo, b_hi, b_lo, start, stop):
            nc.tensor.matmul(dst, a_hi, b_hi, start=start, stop=False)
            nc.tensor.matmul(dst, a_lo, b_hi, start=False, stop=False)
            return nc.tensor.matmul(dst, a_hi, b_lo, start=False, stop=stop)

        def turns_in(step):
            if step[0] == "attention":
                s = step[2]
                return (2 if s < PAIRS else 0) + (2 if 2 <= s < PAIRS + 2 else 0) + (1 if 3 <= s else 0)
            return {"norm": 4, "latent_turns": 3, "spatial_weights": 2, "mix_tokens": 4, "merged_turns": 4,
                    "a_turns": 2, "hidden_turn": 1}.get(step[0], 0)

        turn_at, ws_turn, t = [], [], 0
        prob_turn, qk_turn = {}, {}
        for step in plan:
            if step[0] == "spatial_weights":
                ws_turn.append(t)
            turn_at.append(t)
            if step[0] == "attention":
                s, b = step[2], t + (1 if 3 <= step[2] else 0)
                if 2 <= s < PAIRS + 2:
                    prob_turn[step[1], s - 2] = b
                    b += 2
                if s < PAIRS:
                    qk_turn[step[1], s] = b
            t += turns_in(step)
        ALL_TURNS = t

        def wait_turn_read(eng, b):
            eng.wait_ge(turn_free[b % 2], b // 2 + 1)

        def wait_strip_read(eng, n):
            eng.wait_ge(strip_free[n % 2], n // 2 + 1)

        def is_first(e):
            return isinstance(e, int) and e == 0

        def strips_read(e, j):
            return ((GUS + 1) // 2 if j % 2 == 0 else GUS // 2) * e + j // 2

        def g_done(e, g):
            return 8 * e - 2 + g

        def g_read(e, g):
            return 4 * e - 1 + g // 2

        def layer_over(l):
            return strip_at[l, "down", 0] + 1

        block = ctx.enter_context(nc.Block())

        @block.sync
        def _(sp):
            for t in range(TT):
                sp.dma_start(xres[:, t, :], x[0, t * P:(t + 1) * P, :]).then_inc(x_landed, 16)
            sp.dma_start(consts[:], shape_consts).then_inc(x_landed, 16)
            for i, src in enumerate((mix_norm_g.rearrange("l (k p) -> (l k) p", p=P),
                                     ffn_norm_g.rearrange("l (k p) -> (l k) p", p=P),
                                     mla_q_lat_g.rearrange("l (k p) -> (l k) p", p=P),
                                     mla_kv_lat_g.rearrange("l (k p) -> (l k) p", p=P),
                                     gm_b_spatial.rearrange("l g p -> (l g) p"))):
                sp.dma_start(rows[row_at[i]:row_at[i] + row_sizes[i], :], src).then_inc(rows_landed, 16)

            def static_load(n):
                pieces, k, w = chunks[n]
                slot = n % RAW
                v = raw_view(slot, k, w)
                if pieces[0] == "gu":
                    ring.load(sp, 0, n, [(v[:, :, 0:HC], pieces[1]), (v[:, :, HC:2 * HC], pieces[2])])
                elif pieces[0] == "down":
                    half = k * w // 2
                    ring.load(sp, 0, n, [(raw[:, slot, 0:half], pieces[1]), (raw[:, slot, half:2 * half], pieces[2])])
                else:
                    ring.load(sp, 0, n, [(v[:, c // w:c // w + kk, :], src) for c, kk, src in pieces])

            for n in range(RAW):
                static_load(n)
            for n in range(RAW, N0):
                static_load(n)

            def expert_loads(r, e):
                for j in range(GU_CHUNKS):
                    v = raw_view(r.raw_slot(j), 4, STRIP)
                    g, u = gu_pieces(moe_w_gu[0, e], j // 2, 4 * (j % 2))
                    r.load(sp, e, j, [(v[:, :, 0:HC], g), (v[:, :, HC:2 * HC], u)])
                for d in range(len(DOWN_K)):
                    s = r.raw_slot(GU_CHUNKS + d)
                    half = DOWN_SIZE[d] // 2
                    a, b = down_pieces(moe_w_down[0, e], d)
                    r.load(sp, e, GU_CHUNKS + d, [(raw[:, s, 0:half], a), (raw[:, s, half:2 * half], b)])

            r = Ring(N0, raw_landed, hi_done, lo_done, chunk_used)
            with sp.Fori(0, E) as e:
                expert_loads(r, e)
            sp.wait_ge(counts_ready, 1)
            crowded = sp.value_load(most[0:1, 0:1], min_val=0, max_val=S)
            sp.wait_ge(pass_sems[0]["over"], 1)
            with sp.If(crowded > P):
                r2 = Ring(0, raw_landed2, hi_done2, lo_done2, chunk_used2)
                expert_loads(r2, 0)
                with sp.Fori(1, E) as e:
                    expert_loads(r2, e)
                sp.wait_ge(pass_sems[1]["over"], 1)
            sp.dma_start(out[0].rearrange("(t p) d -> p t d", p=P), xres[:]).then_inc(out_stored, 16)
            sp.wait_ge(out_stored, 16)

        @block.gpsimd
        def _(pool):
            for l in range(L):
                for dst, src in ((q_gain, mla_q_norm_g), (k_gain, mla_k_norm_g)):
                    pool.dma_start(dst[:, l, :], src[l:l + 1, :].to_broadcast([P, DQ])).then_inc(small_landed, 16)
            for l in range(L):
                if l:
                    wait_strip_read(pool, layer_over(l - 1) - 1)
                    wait_strip_read(pool, layer_over(l - 1))
                kf = kb[:].rearrange("p t h d -> p (t h d)")
                pool.dma_start(kf[:, 0:D], gm_v_norm_g[l:l + 1, :].to_broadcast([P, D])).then_inc(ws_landed, 16)
                pool.dma_start(kf[:, D:2 * D], gm_v_norm_b[l:l + 1, :].to_broadcast([P, D])).then_inc(ws_landed, 16)
                pool.dma_start(ws_raw[:], gm_w_spatial[l].rearrange("g t s -> t g s")).then_inc(ws_landed, 16)
                wait_turn_read(pool, ws_turn[l])
                wait_turn_read(pool, ws_turn[l] + 1)
                nc.gpsimd.affine_select(out=ws_t[:], in_=ws_t[:], compare_op=ALU.is_ge, fill=0.0, base=0,
                                        pattern=[[0, NG], [1, P]], channel_multiplier=-1).then_inc(ws_masked, 1)
            wait_strip_read(pool, strip_at[L - 1, "wo", 0])
            wait_strip_read(pool, strip_at[L - 1, "wo", 1])
            with nc.allow_non_contiguous_dma(reason="the router, 32 KiB"):
                pool.dma_start(wr[:], moe_w_router[0].rearrange("(k p) e -> p k e", p=P)).then_inc(wr_landed, 16)
            pool.dma_start(br[:], moe_b_router[0:1, :].to_broadcast([P, E])).then_inc(wr_landed, 16)
            pool.wait_ge(small_landed, 16 * 2 * L)
            pool.wait_ge(wr_landed, 32)

        @block.tensor
        def _(pe):
            def turn_bank(b):
                if b >= 2:
                    wait_turn_read(pe, b - 2)
                return ps[:, 4 + b % 2, :]

            def turn4(b, src):
                bank = turn_bank(b)
                for i in range(4):
                    mm = nc.tensor.transpose(bank[:, i * P:(i + 1) * P], src(i // TT, i % TT), ident)
                mm.then_inc(turn_done, 1)

            def wait_turns_split(b):
                wait_turn_read(pe, b - 1)
                wait_turn_read(pe, b - 2)

            operands = {"cq": (act_hi, act_lo, 0), "ckv": (act_hi, act_lo, 0), "v": (act_hi, act_lo, 0),
                        "u": (act_hi, act_lo, 0), "ga": (act_hi, act_lo, 0), "gb": (act_hi, act_lo, 0),
                        "gu": (act_hi, act_lo, 0), "uq": (t1_hi, t1_lo, 0), "ukv": (t1_hi, t1_lo, KQ),
                        "pa": (t1_hi, t1_lo, 0), "pb": (bt_hi, bt_lo, 0), "wo": (act_hi, act_lo, 0)}
            latents = qb[:].rearrange("p t h d -> p (t h d)")
            CKV0, CKVW = TT * QL, KVL + DR

            pe.wait_ge(x_landed, 48)
            pe.wait_ge(rows_landed, 80)
            nc.tensor.transpose(ps[:, 6, 0:ROWS], rows[:], ident[0:ROWS, 0:ROWS]).then_inc(rows_turned, 1)
            for i, step in enumerate(plan):
                kind, l, b0 = step[0], step[1], turn_at[i]
                if kind == "norm":
                    src = xn if step[2] else vbuf
                    pe.wait_ge(normed_done, 2 * (2 * l + step[2] + 1))
                    for b in range(4):
                        turn4(b0 + b, lambda k, t: src[:, t, (2 * b + k) * P:(2 * b + k + 1) * P])
                elif kind == "spatial_weights":
                    pe.wait_ge(ws_landed, 48 * (l + 1))
                    for b in range(2):
                        bank = turn_bank(b0 + b)
                        for g in range(4):
                            mm = nc.tensor.transpose(bank[:, g * P:(g + 1) * P], ws_raw[:, 4 * b + g, :], ident)
                        mm.then_inc(turn_done, 1)
                elif kind == "latent_turns":
                    pe.wait_ge(latent_normed, l + 1)
                    for b in range(2):
                        turn4(b0 + b, lambda k, t: latents[:, t * QL + (2 * b + k) * P:t * QL + (2 * b + k + 1) * P])
                    turn4(b0 + 2, lambda k, t: latents[:, CKV0 + t * CKVW + k * P:CKV0 + t * CKVW + (k + 1) * P])
                elif kind == "mix_tokens":
                    pe.wait_ge(v_normed, l + 1)
                    pe.wait_ge(ws_masked, l + 1)
                    for b in range(4):
                        bank = turn_bank(b0 + b)
                        for g in range(2):
                            c = (2 * b + g) * P
                            mm = nc.tensor.matmul(bank[:, g * S:(g + 1) * S].rearrange("p (t d) -> p t d", t=TT),
                                                  ws_t[:, 2 * b + g, :], vbuf[:, :, c:c + P], start=True, stop=True)
                        mm.then_inc(turn_done, 1)
                elif kind == "a_turns":
                    j = step[2]
                    pe.wait_ge(branch_a, 2 * l + j + 1)
                    for b in range(2):
                        turn4(b0 + b, lambda k, t: vbuf[:, t, (4 * j + 2 * b + k) * P:(4 * j + 2 * b + k + 1) * P])
                elif kind == "merged_turns":
                    pe.wait_ge(merged_b, 2 * (l + 1))
                    for b in range(4):
                        turn4(b0 + b, lambda k, t: vbuf[:, t, (2 * b + k) * P:(2 * b + k + 1) * P])
                elif kind == "hidden_turn":
                    j = step[2]
                    wait_strip_read(pe, strip_at[l, "gu", j])
                    turn4(b0, lambda k, t: hid[:, j % 2, t, k * P:(k + 1) * P])
                elif kind == "attention":
                    s, b = step[2], b0
                    if s >= 3:
                        n = s - 3
                        wait_turn_read(pe, prob_turn[l, n])
                        wait_turn_read(pe, prob_turn[l, n] + 1)
                        bank = turn_bank(b)
                        for hh in range(2):
                            dst = bank[hh * DV:(hh + 1) * DV, :]
                            v0, v1 = vv[:, 0, 2 * n + hh, :], vv[:, 1, 2 * n + hh, :]
                            t10, t11 = 2 + 2 * hh, 3 + 2 * hh
                            nc.tensor.matmul(dst[:, 0:P], v0, prob_t[:, hh * P:(hh + 1) * P], start=True, stop=True)
                            nc.tensor.matmul(dst[:, P:S], v0, prob_t[:, t10 * P:(t10 + 1) * P], start=True, stop=False)
                            mm = nc.tensor.matmul(dst[:, P:S], v1, prob_t[:, t11 * P:(t11 + 1) * P], start=False, stop=True)
                        mm.then_inc(turn_done, 1)
                        b += 1
                    if 2 <= s < PAIRS + 2:
                        pe.wait_ge(prob_ready, PAIRS * l + s - 1)
                        for blocks in ((0, 1, 2, 3), (4, 5)):
                            bank = turn_bank(b)
                            for q, blk in enumerate(blocks):
                                mm = nc.tensor.transpose(bank[:, q * P:(q + 1) * P], prob[:, blk * P:(blk + 1) * P], ident)
                            mm.then_inc(turn_done, 1)
                            b += 1
                    if 1 <= s < PAIRS + 1:
                        n = PAIRS * l + s - 1
                        wait_turn_read(pe, qk_turn[l, s - 1])
                        wait_turn_read(pe, qk_turn[l, s - 1] + 1)
                        if n:
                            pe.wait_ge(scores_read, n)
                        for hh in range(2):
                            q_t, k_t = qk_t[0:DQ, hh, 0:S], qk_t[0:DQ, hh, S:2 * S]
                            nc.tensor.matmul(ps[:, 6, hh * P:(hh + 1) * P], q_t[:, 0:P], k_t[:, 0:P], start=True, stop=True)
                            mm = nc.tensor.matmul(ps[:, 7, hh * S:(hh + 1) * S], q_t[:, P:S], k_t, start=True, stop=True)
                        mm.then_inc(scores_done, 1)
                    if s < PAIRS:
                        if s == 0:
                            pe.wait_ge(q_ready, TT * (l + 1))
                            pe.wait_ge(k_ready, TT * (l + 1))
                        for hh in range(2):
                            bank = turn_bank(b)
                            for q in range(4):
                                src = (qb, kb)[q // 2]
                                mm = nc.tensor.transpose(bank[0:DQ, q * P:(q + 1) * P], src[:, q % 2, 2 * s + hh, :], ident)
                            mm.then_inc(turn_done, 1)
                            b += 1
                elif kind == "strip":
                    _, _, what, j, a, b, width, n = step
                    hi, lo, k_at = operands[what]
                    if j == 0 and what in ("cq", "uq", "pa", "pb", "wo", "gu"):
                        wait_turns_split(b0)
                    if n >= 2:
                        wait_strip_read(pe, n - 2)
                    total = sum(chunks[c][1] for c in range(a, b))
                    done = 0
                    for c in range(a, b):
                        ch, cl = ring.take(pe, 0, c)
                        kt = chunks[c][1]
                        for t in range(TT):
                            for k in range(kt):
                                kk = k_at + done + k
                                mm = three(ps[:, 2 * (n % 2) + t, 0:width], hi[:, kk, t * P:(t + 1) * P],
                                           lo[:, kk, t * P:(t + 1) * P], ch[:, k * width:(k + 1) * width],
                                           cl[:, k * width:(k + 1) * width], done + k == 0, done + k == total - 1)
                        mm.then_inc(chunk_used, 1)
                        done += kt
                elif kind == "down":
                    a, n = step[2], step[4]
                    wait_turns_split(b0)
                    wait_strip_read(pe, n - 2)
                    wait_strip_read(pe, n - 1)
                    k_at = 0
                    for d, kt in enumerate(DOWN_K):
                        ch, cl = ring.take(pe, 0, a + d)
                        for t in range(TT):
                            for k in range(kt):
                                kk = k_at + k
                                for hf in range(2):
                                    c = k * D + hf * 512
                                    mm = three(ps[:, (2 * n + 2 * t) % 4 + hf, :], hid_hi[:, kk, t * P:(t + 1) * P],
                                               hid_lo[:, kk, t * P:(t + 1) * P], ch[:, c:c + 512], cl[:, c:c + 512],
                                               kk == 0, kk == KF - 1)
                        mm.then_inc(chunk_used, 1)
                        k_at += kt

            wait_turns_split(ALL_TURNS)
            pe.wait_ge(wr_lo_done, 1)
            for t in range(TT):
                for k in range(KD):
                    mm = three(ps[:, 4, t * E:(t + 1) * E], act_hi[:, k, t * P:(t + 1) * P],
                               act_lo[:, k, t * P:(t + 1) * P], wr_hi[:, k, :], wr_lo[:, k, :], k == 0, k == KD - 1)
            mm.then_inc(logits_done, 1)
            pe.wait_ge(chosen_ready, 1)
            nc.tensor.matmul(ps[:, 5, 0:E], before, chosen[:, 0, :], start=True, stop=True)
            nc.tensor.matmul(ps[:, 5, E:2 * E], before, chosen[:, 1, :], start=True, stop=False)
            nc.tensor.matmul(ps[:, 5, E:2 * E], ones, chosen[:, 0, :], start=False, stop=True)
            nc.tensor.matmul(ps[:, 5, 2 * E:3 * E], ones, chosen[:, 0, :], start=True, stop=False)
            nc.tensor.matmul(ps[:, 5, 2 * E:3 * E], ones, chosen[:, 1, :], start=False, stop=True).then_inc(places_done, 1)

            def moe_pass(r, z):
                def gather(half):
                    bank = ps[:, 6 + half, :]
                    for k in range(4):
                        c = (4 * half + k) * P
                        for t in range(TT):
                            nc.tensor.matmul(bank[:, k * P:(k + 1) * P], xn_hi[:, t, c:c + P], pick[:, t, :],
                                             start=t == 0, stop=False)
                            mm = nc.tensor.matmul(bank[:, k * P:(k + 1) * P], xn_lo[:, t, c:c + P], pick[:, t, :],
                                                  start=False, stop=t == TT - 1)
                    mm.then_inc(z["g_done"], 1)

                def scatter(t, g_read):
                    for hf in range(2):
                        pe.wait_ge(z[f"g_free{hf}"], g_read)
                        nc.tensor.matmul(ps[:, 6 + hf, :], put[:, t * P:(t + 1) * P], y_hi[:, hf * 512:(hf + 1) * 512],
                                         start=True, stop=False)
                        nc.tensor.matmul(ps[:, 6 + hf, :], put[:, t * P:(t + 1) * P], y_lo[:, hf * 512:(hf + 1) * 512],
                                         start=False, stop=True).then_inc(z["g_done"], 1)

                def hidden_turn(e, j):
                    pe.wait_ge(z[f"gu_free{j % 2}"], strips_read(e, j) + 1)
                    if j >= 2 or not is_first(e):
                        pe.wait_ge(z[f"hturn_free{j % 2}"], strips_read(e, j))
                    for k in range(2):
                        mm = nc.tensor.transpose(ps[:, 4 + j % 2, k * P:(k + 1) * P], hid[:, j % 2, 0, k * P:(k + 1) * P], ident)
                    mm.then_inc(z["hturn_done"], 1)

                def body(e, last):
                    first = is_first(e)
                    for j in range(GUS):
                        if j >= 2 or not first:
                            pe.wait_ge(z[f"gu_free{j % 2}"], strips_read(e, j))
                        if j == 0:
                            pe.wait_ge(z["g_free0"], 1 if first else g_read(e, 0))
                            pe.wait_ge(z["g_free1"], 1 if first else g_read(e, 0))
                        for c in range(2):
                            ch, cl = r.take(pe, e, 2 * j + c)
                            for k in range(4):
                                kk = 4 * c + k
                                mm = three(ps[:, j % 2, :], act_hi[:, kk, 0:P], act_lo[:, kk, 0:P],
                                           ch[:, k * STRIP:(k + 1) * STRIP], cl[:, k * STRIP:(k + 1) * STRIP],
                                           kk == 0, kk == KD - 1)
                            mm.then_inc(r.used, 1)
                            if c == 0 and j >= 2:
                                hidden_turn(e, j - 2)
                        if not first and j == 1:
                            pe.wait_ge(z["y_split"], e)
                            scatter(0, g_read(e, 0))
                        if not first and j == 3:
                            scatter(1, g_read(e, 2))
                        if j == 5:
                            pe.wait_ge(z["g_free0"], g_read(e, 4))
                            for t in range(TT):
                                mm = nc.tensor.transpose(ps[:, 6, t * P:(t + 1) * P], pick[:, t, :].bitcast(F32), ident)
                            mm.then_inc(z["g_done"], 1)
                            pe.wait_ge(z["g_free1"], g_read(e, 4))
                            for t in range(TT):
                                mm = nc.tensor.matmul(ps[:, 7, 0:1], pick[:, t, :].bitcast(F32), pick_w[:, t:t + 1],
                                                      start=t == 0, stop=t == TT - 1)
                            mm.then_inc(z["g_done"], 1)
                    k_at = 0
                    for d, kt in enumerate(DOWN_K):
                        if d == 0 and not first:
                            pe.wait_ge(z["y_split"], e)
                        ch, cl = r.take(pe, e, GU_CHUNKS + d)
                        s = (k_at + kt - 1) // 2
                        if s > (k_at - 1) // 2 or not k_at:
                            pe.wait_ge(z[f"hturn_free{s % 2}"], strips_read(e, s) + 1)
                        for k in range(kt):
                            kk = k_at + k
                            for hf in range(2):
                                c = k * D + hf * 512
                                mm = three(ps[:, 2 + hf, :], hid_hi[:, kk, 0:P], hid_lo[:, kk, 0:P], ch[:, c:c + 512],
                                           cl[:, c:c + 512], kk == 0, kk == KF - 1)
                        mm.then_inc(r.used, 1)
                        k_at += kt
                        if d == 0:
                            hidden_turn(e, GUS - 2)
                        if d == 2:
                            hidden_turn(e, GUS - 1)
                        if not last and d in (4, 6):
                            if d == 4:
                                pe.wait_ge(z["picked"], e + 2)
                            pe.wait_ge(z[f"g_free{(d - 4) // 2}"], g_read(e, 6))
                            gather((d - 4) // 2)

                pe.wait_ge(z["picked"], 1)
                gather(0)
                gather(1)
                body(0, False)
                with pe.Fori(1, E - 1) as e:
                    body(e, False)
                body(E - 1, True)
                pe.wait_ge(z["y_split"], E)
                scatter(0, g_read(E, 0) - 1)
                scatter(1, g_read(E, 2) - 1)

            pe.wait_ge(xn_lo_done, 1)
            moe_pass(Ring(N0, raw_landed, hi_done, lo_done, chunk_used), pass_sems[0])
            pe.wait_ge(counts_ready, 1)
            crowded = pe.value_load(most[0:1, 0:1], min_val=0, max_val=S)
            with pe.If(crowded > P):
                pe.wait_ge(pass_sems[0]["over"], 1)
                moe_pass(Ring(0, raw_landed2, hi_done2, lo_done2, chunk_used2), pass_sems[1])

        @block.scalar
        def _(act):
            own = Chain(act, act_own)
            latents = qb[:].rearrange("p t h d -> p (t h d)")
            CKV0, CKVW = TT * QL, KVL + DR
            counts = {"split_turns": 0, "head_sums": 0}

            def copy(dst, src, scale=1.0):
                return nc.scalar.activation(dst, src, ACT.Copy, scale=scale)

            def splits(a, b):
                for n in range(a + LEAD, b + LEAD):
                    ring.split_hi(act, 0, n, size[n] if n < N0 else CHUNK)

            def turn_hi_parts(b, hi, k0, scale):
                act.wait_ge(turn_done, b + 1)
                for k in range(2):
                    op = copy(hi[:, k0 + k, :], ps[:, 4 + b % 2, k * S:(k + 1) * S], scale(k0 + k))
                op.then_inc(turn_hi, 1)

            act.wait_ge(x_landed, 48)
            for i, step in enumerate(plan):
                kind, l, b0 = step[0], step[1], turn_at[i]
                if kind == "norm":
                    g = ffn_g if step[2] else mix_g
                    dst = xn if step[2] else vbuf
                    m = 2 * l + step[2]
                    if step[2]:
                        wait_strip_read(act, strip_at[l, "wo", 0])
                        wait_strip_read(act, strip_at[l, "wo", 1])
                    elif l:
                        wait_strip_read(act, layer_over(l - 1) - 1)
                        wait_strip_read(act, layer_over(l - 1))
                    for t in range(TT):
                        nc.scalar.activation(dst[:, t, :], xres[:, t, :], ACT.Square,
                                             accum_out=small[:, t:t + 1]).then_inc(squares_done, 1)
                    if not m:
                        act.wait_ge(rows_turned, 1)
                        copy(cols_t[:], ps[:, 6, 0:ROWS]).then_inc(gains_ready, 1)
                        act.wait_ge(gains_ready, 1)
                    act.wait_ge(root_done, m + 1)
                    for t in range(TT):
                        copy(dst[:, t, :], xres[:, t, :], small[:, 2 + t:3 + t]).then_inc(normed_done, 1)
                    if not m:
                        for n in range(LEAD):
                            ring.split_hi(act, 0, n, size[n])
                    for b in range(4):
                        turn_hi_parts(b0 + b, act_hi, 2 * b, lambda k: g[:, l, k:k + 1])
                elif kind == "spatial_weights":
                    for b in range(2):
                        act.wait_ge(turn_done, b0 + b + 1)
                        copy(ws_t[:, 4 * b:4 * b + 4, :], ps[:, 4 + (b0 + b) % 2, :].rearrange("p (g s) -> p g s", g=4)
                             ).then_inc(turn_free[(b0 + b) % 2], 1)
                elif kind == "latent_turns":
                    for b in range(2):
                        turn_hi_parts(b0 + b, t1_hi, 2 * b, lambda k: qlat_g[:, l, k:k + 1])
                    turn_hi_parts(b0 + 2, t1_hi, KQ, lambda k: kvlat_g[:, l, k - KQ:k - KQ + 1])
                elif kind == "a_turns":
                    for b in range(2):
                        turn_hi_parts(b0 + b, t1_hi, 4 * step[2] + 2 * b, lambda k: 1.0)
                elif kind == "merged_turns":
                    for b in range(4):
                        turn_hi_parts(b0 + b, act_hi, 2 * b, lambda k: 0.5)
                elif kind == "hidden_turn":
                    turn_hi_parts(b0, hid_hi, 2 * step[2], lambda k: 1.0)
                elif kind in ("q_norm", "k_norm"):
                    t = step[2]
                    src, w = (qb, DQ) if kind == "q_norm" else (kb, DN)
                    last = ("uq", H * DQ // STRIP - 1) if kind == "q_norm" else ("ukv", H // HPS - 1)
                    wait_strip_read(act, strip_at[l, last[0], last[1]])
                    for hf in range(2):
                        if counts["head_sums"]:
                            act.wait_ge(head_sums, counts["head_sums"])
                        counts["head_sums"] += 1
                        nc.scalar.activation(sq[:, 0:8 * w].rearrange("p (h d) -> p h d", h=8),
                                             src[:, t, 8 * hf:8 * hf + 8, 0:w], ACT.Square).then_inc(head_squares, 1)
                elif kind == "attention":
                    s, b = step[2], b0
                    if s >= 3:
                        act.wait_ge(turn_done, b + 1)
                        copy(bt_hi[:, s - 3, :], ps[:, 4 + b % 2, 0:S]).then_inc(turn_hi, 1)
                        b += 1
                    if 2 <= s < PAIRS + 2:
                        for c, w in ((0, 512), (512, 256)):
                            act.wait_ge(turn_done, b + 1)
                            copy(prob_t[:, c:c + w], ps[:, 4 + b % 2, 0:w]).then_inc(turn_free[b % 2], 1)
                            b += 1
                    if s < PAIRS:
                        if s >= 1:
                            act.wait_ge(scores_done, PAIRS * l + s)
                        for hh in range(2):
                            act.wait_ge(turn_done, b + 1)
                            copy(qk_t[0:DQ, hh, :], ps[0:DQ, 4 + b % 2, :]).then_inc(turn_free[b % 2], 1)
                            b += 1
                    if 1 <= s < PAIRS + 1:
                        act.wait_ge(max_ready, PAIRS * l + s)
                        for q, (c, w) in enumerate(((0, P), (P, P), (2 * P, S), (2 * P + S, S))):
                            op = nc.scalar.activation(prob[:, c:c + w], prob[:, c:c + w], ACT.Exp,
                                                      bias=soft[:, 0, q:q + 1], accum_out=soft[:, 1, q:q + 1])
                        op.then_inc(exp_done, 1)
                elif kind == "strip":
                    _, _, what, j, a, b, width, n = step
                    splits(a, b)
                    bank = ps[:, 2 * (n % 2):2 * (n % 2) + 2, :]
                    free = strip_free[n % 2]
                    if what in ("wo", "pa", "pb"):
                        continue
                    act.wait_ge(chunk_used, b)
                    if what == "cq":
                        for t in range(TT):
                            own.link(nc.scalar.activation(sq[:, 0:QL], bank[:, t, 0:QL], ACT.Square,
                                                          accum_out=small[:, 4 + t:5 + t]))
                        op = copy(latents[:, 0:TT * QL].rearrange("p (t c) -> p t c", t=TT), bank[:, :, 0:QL])
                    elif what == "ckv":
                        for t in range(TT):
                            own.link(nc.scalar.activation(sq[:, 0:KVL], bank[:, t, 0:KVL], ACT.Square,
                                                          accum_out=small[:, 6 + t:7 + t]))
                            own.link(nc.scalar.activation(sq[:, 0:DR], bank[:, t, KVL:KVL + DR], ACT.Square,
                                                          accum_out=small[:, 12 + t:13 + t]))
                        copy(kr[:, :, :], bank[:, :, KVL:KVL + DR])
                        op = copy(latents[:, CKV0:CKV0 + TT * CKVW].rearrange("p (t c) -> p t c", t=TT),
                                  bank[:, :, 0:CKVW])
                    elif what in ("v", "u"):
                        m = 4 * l + (2 if what == "u" else 0) + j
                        if (what, j) == ("v", 0):
                            if l:
                                act.wait_ge(merged_b, 2 * l)
                        elif (what, j) == ("u", 1):
                            act.wait_ge(branch_a, 2 * l + 1)
                        else:
                            wait_strip_read(act, strip_at[(l, "v", 0) if what == "v" else (l, "v", 1)])
                        nc.scalar.activation(tmp[:], bank, ACT.Square).then_inc(gelu_sq, 1)
                        act.wait_ge(gelu_arg, m + 1)
                        nc.scalar.activation(tmp[:], tmp[:], ACT.Tanh, scale=GELU_A * GELU_C).then_inc(gelu_tanh, 1)
                        continue
                    elif what == "uq":
                        if j == 0:
                            act.wait_ge(turn_done, b0)
                        flat = qb[:].rearrange("p t h d -> p t (h d)")
                        op = copy(flat[:, :, j * STRIP:(j + 1) * STRIP], bank)
                    elif what == "ukv":
                        if j == 0:
                            act.wait_ge(v_normed, l + 1)
                        for t in range(TT):
                            heads = bank[:, t, :].rearrange("p (h c) -> p h c", h=HPS)
                            copy(kb[:, t, HPS * j:HPS * (j + 1), 0:DN], heads[:, :, 0:DN])
                            op = copy(vv[:, t, HPS * j:HPS * (j + 1), :], heads[:, :, DN:DN + DV])
                    elif what in ("ga", "gb"):
                        if what == "ga" and j == 0:
                            act.wait_ge(branch_a, 2 * l + 2)
                        elif what == "gb" and j == 1:
                            act.wait_ge(merged_b, 2 * l + 1)
                        else:
                            wait_strip_read(act, strip_at[l, "pa", 0 if what == "ga" else 1])
                        op = nc.scalar.activation(tmp[:], bank, ACT.Tanh, scale=0.5)
                    elif what == "gu":
                        if j:
                            wait_strip_read(act, n - 1)
                        op = nc.scalar.activation(sig[:], bank[:, :, 0:HC], ACT.Tanh, scale=0.5)
                        free = sig_done
                    op.then_inc(free, 1)
                elif kind == "down":
                    splits(step[2], step[3])

            act.wait_ge(wr_landed, 32)
            copy(wr_hi[:], wr[:]).then_inc(wr_hi_done, 1)
            copy(xn_hi[:], xn[:]).then_inc(xn_hi_done, 1)
            act.wait_ge(gap_ready, 1)
            nc.scalar.activation(rt[:, :, 1], rt[:, :, 0], ACT.Exp).then_inc(gap_exp, 1)

            def moe_pass(r, z):
                def turn_part(e, j):
                    act.wait_ge(z["hturn_done"], GUS * e + j + 1)
                    copy(hid_hi[:, 2 * j:2 * j + 2, 0:P], ps[:, 4 + j % 2, 0:2 * P].rearrange("p (k s) -> p k s", k=2)
                         ).then_inc(z["hturn_hi"], 1)

                def gather_part(e, half):
                    act.wait_ge(z["g_done"], 1 + half if e is None else g_done(e, 6 + half) + 1)
                    for k in range(4):
                        kk = 4 * half + k
                        op = copy(act_hi[:, kk, 0:P], ps[:, 6 + half, k * P:(k + 1) * P], ffn_g[:, L - 1, kk:kk + 1])
                    op.then_inc(z["g_hi"], 1)

                def split(e, c, last):
                    if c < PER_EXPERT:
                        r.split_hi(act, e, c, expert_size[c])
                    elif not last:
                        r.split_hi(act, e + 1, c - PER_EXPERT, expert_size[c - PER_EXPERT])

                def body(e, last):
                    first = is_first(e)
                    for j in range(GUS):
                        split(e, 2 * j + LEAD, last)
                        split(e, 2 * j + 1 + LEAD, last)
                        act.wait_ge(r.used, r.count(e, 2 * j + 2))
                        if j or not first:
                            q = j - 1 if j else GUS - 1
                            act.wait_ge(z[f"gu_free{q % 2}"], strips_read(e if j else e - 1, q) + 1)
                        nc.scalar.activation(sig[:, 0, :], ps[:, j % 2, 0:HC], ACT.Tanh, scale=0.5).then_inc(z["sig_ready"], 1)
                        if j >= 2:
                            turn_part(e, j - 2)
                        if j == 6:
                            act.wait_ge(z["g_done"], g_done(e, 4) + 1)
                            copy(put[:], ps[:, 6, 0:S]).then_inc(z["g_free0"], 1)
                            act.wait_ge(z["g_done"], g_done(e, 5) + 1)
                            copy(slot_w[:], ps[:, 7, 0:1]).then_inc(z["g_free1"], 1)
                    for d in range(len(DOWN_K)):
                        split(e, GU_CHUNKS + d + LEAD, last)
                        if d == 1:
                            turn_part(e, GUS - 2)
                        if d == 3:
                            turn_part(e, GUS - 1)
                        if not last and d in (5, 7):
                            gather_part(e, (d - 5) // 2)
                    act.wait_ge(r.used, r.count(e, PER_EXPERT))
                    act.wait_ge(z["g_free1"], g_read(e, 4) + 1)
                    copy(y_hi[:], ps[:, 2:4, :].rearrange("p a b -> p (a b)"), slot_w[:, 0:1]).then_inc(z["y_hi_done"], 1)

                gather_part(None, 0)
                gather_part(None, 1)
                body(0, False)
                with act.Fori(1, E - 1) as e:
                    body(e, False)
                body(E - 1, True)

            moe_pass(Ring(N0, raw_landed, hi_done, lo_done, chunk_used), pass_sems[0])
            act.wait_ge(counts_ready, 1)
            crowded = act.value_load(most[0:1, 0:1], min_val=0, max_val=S)
            with act.If(crowded > P):
                act.wait_ge(pass_sems[0]["over"], 1)
                r2 = Ring(0, raw_landed2, hi_done2, lo_done2, chunk_used2)
                for c in range(LEAD):
                    r2.split_hi(act, 0, c)
                moe_pass(r2, pass_sems[1])

        @block.vector
        def _(dve):
            own = Chain(dve, dve_own)
            link = own.link
            latents = qb[:].rearrange("p t h d -> p (t h d)")
            CKV0, CKVW = TT * QL, KVL + DR
            counts = {"split_turns": 0, "heads": 0}
            tt, ts, stt = nc.vector.tensor_tensor, nc.vector.tensor_scalar, nc.vector.scalar_tensor_tensor

            def splits(a, b):
                for n in range(a + LEAD, b + LEAD):
                    ring.split_lo(dve, 0, n, size[n] if n < N0 else CHUNK)

            def turn_lo_parts(b, hi, lo, k0, scale):
                counts["split_turns"] += 1
                dve.wait_ge(turn_hi, counts["split_turns"])
                for k in range(2):
                    op = stt(lo[:, k0 + k, :], ps[:, 4 + b % 2, k * S:(k + 1) * S], scale(k0 + k),
                             hi[:, k0 + k, :].bitcast(F32), ALU.mult, ALU.subtract)
                op.then_inc(turn_free[b % 2], 1)

            def root(dst, src, scale, eps, n, last=None):
                a, t_, yi = rs_a[:, 0:n], rs_t[:, 0:n], rs_y[:, 0:n]
                y = yi.bitcast(F32)
                link(ts(a, src, scale, eps, ALU.mult, ALU.add))
                link(ts(yi, a.bitcast(I32), 1, None, ALU.logical_shift_right))
                link(ts(yi, yi, -1.0, RSQRT_SEED, ALU.mult, ALU.add))
                for it in range(3):
                    link(tt(t_, y, y, ALU.mult))
                    link(stt(t_, t_, -0.5, a, ALU.mult, ALU.mult))
                    op = stt(dst if it == 2 else y, t_, 1.5, y, ALU.add, ALU.mult)
                    if it == 2 and last is not None:
                        op.then_inc(last, 1)
                        return
                    link(op)

            def rope(x1, x2, cos, sin, s1, s2, last=None):
                link(tt(s1, x2, sin, ALU.mult))
                link(tt(s2, x1, sin, ALU.mult))
                link(tt(x1, x1, cos, ALU.mult))
                link(tt(x1, x1, s1, ALU.subtract))
                link(tt(x2, x2, cos, ALU.mult))
                op = tt(x2, x2, s2, ALU.add)
                if last is None:
                    link(op)
                else:
                    op.then_inc(last, 1)

            def sum_squares(dst, w):
                counts["heads"] += 1
                dve.wait_ge(head_squares, counts["heads"])
                nc.vector.tensor_reduce(dst, sq[:, 0:8 * w].rearrange("p (h d) -> p h d", h=8), AX.X,
                                        ALU.add).then_inc(head_sums, 1)

            def over(v, n):
                return v.rearrange("p (m o) -> p m o", o=1).to_broadcast([P, v.shape[1], n])

            def each(v, m):
                return v.rearrange("p (o n) -> p o n", o=1).to_broadcast([P, m, v.shape[1]])

            dve.wait_ge(x_landed, 48)
            for i, step in enumerate(plan):
                kind, l, b0 = step[0], step[1], turn_at[i]
                if kind == "norm":
                    g = ffn_g if step[2] else mix_g
                    m = 2 * l + step[2]
                    dve.wait_ge(squares_done, 2 * (m + 1))
                    root(small[:, 2:4], small[:, 0:2], 1.0 / D, EPS, 2, root_done)
                    if not m:
                        dve.wait_ge(gains_ready, 1)
                        for n in range(LEAD):
                            ring.split_lo(dve, 0, n, size[n])
                    for b in range(4):
                        turn_lo_parts(b0 + b, act_hi, act_lo, 2 * b, lambda k: g[:, l, k:k + 1])
                elif kind == "latent_norm":
                    wait_strip_read(dve, strip_at[l, "cq", 0])
                    wait_strip_read(dve, strip_at[l, "ckv", 0])
                    link(ts(small[:, 4:6], small[:, 4:6], 1.0 / QL, None, ALU.mult))
                    link(ts(small[:, 6:8], small[:, 6:8], 1.0 / KVL, None, ALU.mult))
                    root(small[:, 8:12], small[:, 4:8], 1.0, EPS, 4)
                    for t in range(TT):
                        q, c = latents[:, t * QL:(t + 1) * QL], latents[:, CKV0 + t * CKVW:CKV0 + t * CKVW + KVL]
                        ts(q, q, small[:, 8 + t:9 + t], None, ALU.mult)
                        op = ts(c, c, small[:, 10 + t:11 + t], None, ALU.mult)
                    op.then_inc(latent_normed, 1)
                    if not l:
                        dve.wait_ge(small_landed, 16 * 2 * L)
                    for t in range(TT):
                        link(tt(kr[:, t, :], kr[:, t, :], k_gain[:, l, DN:DQ], ALU.mult))
                        rope(kr[:, t, 0:HR], kr[:, t, HR:DR], cos_sin[:, t, 0, :], cos_sin[:, t, 1, :],
                             rs_a[:, 0:HR], rs_t[:, 0:HR])
                elif kind == "latent_turns":
                    for b in range(2):
                        turn_lo_parts(b0 + b, t1_hi, t1_lo, 2 * b, lambda k: qlat_g[:, l, k:k + 1])
                    turn_lo_parts(b0 + 2, t1_hi, t1_lo, KQ, lambda k: kvlat_g[:, l, k - KQ:k - KQ + 1])
                elif kind == "layer_norm":
                    dve.wait_ge(ws_landed, 48 * (l + 1))
                    for t in range(TT):
                        for hf in range(2):
                            op = nc.vector.bn_stats(stats[:, t, hf, :], vbuf[:, t, hf * 512:(hf + 1) * 512])
                    link(op)
                    for t in range(TT):
                        op = nc.vector.bn_aggr(mean_var[:, t, :], stats[:, t, :, :])
                    link(op)
                    root(small[:, 14:16], mean_var[:, :, 1], 1.0, 4 * EPS, 2)
                    kf = kb[:].rearrange("p t h d -> p (t h d)")
                    for t in range(TT):
                        v = vbuf[:, t, :]
                        link(ts(v, v, mean_var[:, t, 0:1], small[:, 14 + t:15 + t], ALU.subtract, ALU.mult))
                        link(tt(v, v, kf[:, 0:D], ALU.mult))
                        op = tt(v, v, kf[:, D:2 * D], ALU.add)
                        if t == 0:
                            link(op)
                    op.then_inc(v_normed, 1)
                elif kind == "mix_tokens":
                    for b in range(4):
                        bb = b0 + b
                        dve.wait_ge(turn_done, bb + 1)
                        for g in range(2):
                            gg = 2 * b + g
                            op = ts(vbuf[:, :, gg * P:(gg + 1) * P],
                                    ps[:, 4 + bb % 2, g * S:(g + 1) * S].rearrange("p (t d) -> p t d", t=TT),
                                    b_sp[:, l, gg:gg + 1], 0.5, ALU.add, ALU.mult)
                        op.then_inc(turn_free[bb % 2], 1)
                elif kind == "a_turns":
                    for b in range(2):
                        bb = b0 + b
                        turn_lo_parts(bb, t1_hi, t1_lo, 4 * step[2] + 2 * b, lambda k: 1.0)
                elif kind == "merged_turns":
                    for b in range(4):
                        turn_lo_parts(b0 + b, act_hi, act_lo, 2 * b, lambda k: 0.5)
                elif kind == "hidden_turn":
                    turn_lo_parts(b0, hid_hi, hid_lo, 2 * step[2], lambda k: 1.0)
                elif kind == "q_norm":
                    t = step[2]
                    for hf in range(2):
                        sum_squares(q_sum[:, t, 8 * hf:8 * hf + 8], DQ)
                    dve.wait_ge(head_sums, counts["heads"])
                    root(q_sum[:, t, :], q_sum[:, t, :], 1.0 / DQ, EPS, H)
                    q = qb[:, t, :, :]
                    link(tt(q, q, over(q_sum[:, t, :], DQ), ALU.mult))
                    link(tt(q, q, each(q_gain[:, l, :], H), ALU.mult))
                    s1, s2 = (prob[:, c:c + H * HR].rearrange("p (h r) -> p h r", h=H) for c in (0, H * HR))
                    rope(q[:, :, DN:DN + HR], q[:, :, DN + HR:DQ], each(cos_sin[:, t, 0, :], H),
                         each(cos_sin[:, t, 1, :], H), s1, s2, q_ready)
                elif kind == "k_norm":
                    t = step[2]
                    for hf in range(2):
                        sum_squares(k_sum[:, t, 8 * hf:8 * hf + 8], DN)
                    dve.wait_ge(head_sums, counts["heads"])
                    link(ts(k_sum[:, t, :], k_sum[:, t, :], small[:, 12 + t:13 + t], None, ALU.add))
                    root(k_sum[:, t, :], k_sum[:, t, :], 1.0 / DQ, EPS, H)
                    k = kb[:, t, :, 0:DN]
                    link(tt(k, k, over(k_sum[:, t, :], DN), ALU.mult))
                    tt(k, k, each(k_gain[:, l, 0:DN], H), ALU.mult)
                    tt(kb[:, t, :, DN:DQ], each(kr[:, t, :], H), over(k_sum[:, t, :], DR), ALU.mult).then_inc(k_ready, 1)
                elif kind == "attention":
                    s, b = step[2], b0
                    if s >= 3:
                        counts["split_turns"] += 1
                        dve.wait_ge(turn_hi, counts["split_turns"])
                        tt(bt_lo[:, s - 3, :], ps[:, 4 + b % 2, 0:S], bt_hi[:, s - 3, :].bitcast(F32),
                           ALU.subtract).then_inc(turn_free[b % 2], 1)
                        b += 1
                    if 1 <= s < PAIRS + 1:
                        n = PAIRS * l + s - 1
                        p0 = prob[:, 0:2 * P].rearrange("p (h k) -> p h k", h=2)
                        p1 = prob[:, 2 * P:2 * P + 2 * S].rearrange("p (h k) -> p h k", h=2)
                        if s >= 2:
                            dve.wait_ge(turn_done, b + 2)
                        elif l or True:
                            dve.wait_ge(q_ready, TT * (l + 1))
                        dve.wait_ge(scores_done, n + 1)
                        stt(p0, ps[:, 6, 0:2 * P].rearrange("p (h k) -> p h k", h=2), SCALE, each(bias_mask[:, P:2 * P], 2),
                            ALU.mult, ALU.add)
                        stt(p1, ps[:, 7, :].rearrange("p (h k) -> p h k", h=2), SCALE, each(bias_mask[:, 0:S], 2),
                            ALU.mult, ALU.add).then_inc(scores_read, 1)
                        dve.wait_ge(scores_read, n + 1)
                        nc.vector.tensor_reduce(soft[:, 2, 0:2], p0, AX.X, ALU.max)
                        link(nc.vector.tensor_reduce(soft[:, 2, 2:4], p1, AX.X, ALU.max))
                        ts(soft[:, 0, :], soft[:, 2, :], -1.0, None, ALU.mult).then_inc(max_ready, 1)
                        dve.wait_ge(exp_done, n + 1)
                        link(nc.vector.reciprocal(soft[:, 2, :], soft[:, 1, :]))
                        tt(p0, p0, over(soft[:, 2, 0:2], P), ALU.mult)
                        tt(p1, p1, over(soft[:, 2, 2:4], S), ALU.mult).then_inc(prob_ready, 1)
                elif kind == "strip":
                    _, _, what, j, a, b, width, n = step
                    splits(a, b)
                    bank = ps[:, 2 * (n % 2):2 * (n % 2) + 2, :]
                    free = strip_free[n % 2]
                    cols = slice(j * STRIP, (j + 1) * STRIP)
                    if what in ("v", "u"):
                        m = 4 * l + (2 if what == "u" else 0) + j
                        dve.wait_ge(gelu_sq, m + 1)
                        stt(tmp[:], tmp[:], 1.0 / GELU_A, bank, ALU.add, ALU.mult).then_inc(gelu_arg, 1)
                        dve.wait_ge(gelu_tanh, m + 1)
                        if what == "v":
                            stt(vbuf[:, :, cols], tmp[:], 1.0, bank, ALU.add, ALU.mult).then_inc(free, 1)
                            wait_strip_read(dve, n)
                        else:
                            stt(tmp[:], tmp[:], 1.0, bank, ALU.add, ALU.mult).then_inc(free, 1)
                            wait_strip_read(dve, n)
                            if j == 0:
                                wait_turn_read(dve, b0 - 1)
                                wait_turn_read(dve, b0 - 2)
                            tt(vbuf[:, :, cols], tmp[:], vbuf[:, :, cols], ALU.mult).then_inc(branch_a, 1)
                    elif what in ("pa", "pb"):
                        wait_strip_read(dve, strip_at[l, "g" + what[1], j])
                        dve.wait_ge(chunk_used, b)
                        if what == "pa":
                            stt(vbuf[:, :, cols], tmp[:], 1.0, bank, ALU.add, ALU.mult).then_inc(free, 1)
                        else:
                            stt(tmp[:], tmp[:], 1.0, bank, ALU.add, ALU.mult).then_inc(free, 1)
                            wait_strip_read(dve, n)
                            wait_strip_read(dve, strip_at[l, "pa", j])
                            tt(vbuf[:, :, cols], vbuf[:, :, cols], tmp[:], ALU.add).then_inc(merged_b, 1)
                    elif what == "wo":
                        dve.wait_ge(chunk_used, b)
                        tt(xres[:, :, cols], xres[:, :, cols], bank, ALU.add).then_inc(free, 1)
                    elif what == "gu":
                        dve.wait_ge(sig_done, j + 1)
                        if j >= 2:
                            dve.wait_ge(turn_done, b0)
                        link(stt(sig[:], sig[:], 1.0, bank[:, :, 0:HC], ALU.add, ALU.mult))
                        stt(hid[:, j % 2, :, :], sig[:], 0.5, bank[:, :, HC:2 * HC], ALU.mult, ALU.mult).then_inc(free, 1)
                elif kind == "down":
                    a, b, n = step[2:5]
                    splits(a, b)
                    dve.wait_ge(chunk_used, b)
                    for t in range(TT):
                        at = (2 * n + 2 * t) % 4
                        tt(xres[:, t, :], xres[:, t, :], ps[:, at:at + 2, :].rearrange("p a b -> p (a b)"),
                           ALU.add).then_inc(strip_free[(n + t) % 2], 1)

            dve.wait_ge(wr_hi_done, 1)
            tt(wr_lo[:], wr[:], wr_hi[:].bitcast(F32), ALU.subtract).then_inc(wr_lo_done, 1)
            dve.wait_ge(xn_hi_done, 1)
            tt(xn_lo[:], xn[:], xn_hi[:].bitcast(F32), ALU.subtract).then_inc(xn_lo_done, 1)
            dve.wait_ge(logits_done, 1)
            link(tt(logit[:], ps[:, 4, 0:TT * E].rearrange("p (t e) -> p t e", t=TT), each(br[:], TT), ALU.add))
            for t in range(TT):
                link(nc.vector.max(top[:, t, :], logit[:, t, :]))
                link(nc.vector.max_index(top_i[:, t, :], top[:, t, :], logit[:, t, :]))
                link(nc.vector.tensor_copy(top_f[:, t, :], top_i[:, t, :]))
                ts(one_a[:, t, :], iota[:, 0:E], top_f[:, t, 0:1], None, ALU.is_equal)
                link(ts(one_b[:, t, :], iota[:, 0:E], top_f[:, t, 1:2], None, ALU.is_equal))
            tt(chosen[:], one_a[:], one_b[:], ALU.add).then_inc(chosen_ready, 1)
            dve.wait_ge(chosen_ready, 1)
            tt(rt[:, :, 0], top[:, :, 1], top[:, :, 0], ALU.subtract).then_inc(gap_ready, 1)
            dve.wait_ge(gap_exp, 1)
            link(ts(rt[:, :, 2], rt[:, :, 1], 1.0, None, ALU.add))
            link(nc.vector.reciprocal(rt[:, :, 3], rt[:, :, 2]))
            link(tt(rt[:, :, 2], rt[:, :, 1], rt[:, :, 3], ALU.mult))
            for t in range(TT):
                link(ts(combine[:, t, :], one_a[:, t, :], rt[:, t, 3:4], None, ALU.mult))
                link(stt(combine[:, t, :], one_b[:, t, :], rt[:, t, 2:3], combine[:, t, :], ALU.mult, ALU.add))
            dve.wait_ge(places_done, 1)
            link(ts(place[:], chosen[:], -4.0 * S, 4.0 * S, ALU.mult, ALU.add))
            link(tt(place[:], place[:], ps[:, 5, 0:TT * E].rearrange("p (t e) -> p t e", t=TT), ALU.add))
            link(nc.vector.tensor_reduce(most_f[:, 0:1], ps[:, 5, TT * E:(TT + 1) * E], AX.X, ALU.max))
            nc.vector.tensor_copy(most[:, 0:1], most_f[:, 0:1]).then_inc(counts_ready, 1)

            def moe_pass(r, z):
                def turn_part(e, j):
                    dve.wait_ge(z["hturn_hi"], GUS * e + j + 1)
                    tt(hid_lo[:, 2 * j:2 * j + 2, 0:P], ps[:, 4 + j % 2, 0:2 * P].rearrange("p (k s) -> p k s", k=2),
                       hid_hi[:, 2 * j:2 * j + 2, 0:P].bitcast(F32), ALU.subtract).then_inc(z[f"hturn_free{j % 2}"], 1)

                def gather_part(e, half):
                    dve.wait_ge(z["g_hi"], 1 + half if e is None else 2 * e + 3 + half)
                    for k in range(4):
                        kk = 4 * half + k
                        op = stt(act_lo[:, kk, 0:P], ps[:, 6 + half, k * P:(k + 1) * P], ffn_g[:, L - 1, kk:kk + 1],
                                 act_hi[:, kk, 0:P].bitcast(F32), ALU.mult, ALU.subtract)
                    op.then_inc(z[f"g_free{half}"], 1)

                def scattered(e, t, missing=0):
                    for hf in range(2):
                        dve.wait_ge(z["g_done"], g_done(e, 2 * t + hf) + 1 - missing)
                        xs = xres[:, t, hf * 512:(hf + 1) * 512]
                        op = tt(xs, xs, ps[:, 6 + hf, :], ALU.add)
                        if missing and t and hf:
                            op.then_inc(z["over"], 1)
                        else:
                            op.then_inc(z[f"g_free{hf}"], 1)

                def pick_tokens(e):
                    for t in range(TT):
                        at = place[:, t, e:e + 1] if isinstance(e, int) else place[:, t, bass.ds(e, 1)]
                        w = combine[:, t, e:e + 1] if isinstance(e, int) else combine[:, t, bass.ds(e, 1)]
                        ts(pick[:, t, :], iota, at, None, ALU.is_equal)
                        op = ts(pick_w[:, t:t + 1], w, 0.0, None, ALU.add)
                    op.then_inc(z["picked"], 1)

                def split(e, c, last):
                    if c < PER_EXPERT:
                        r.split_lo(dve, e, c, expert_size[c])
                    elif not last:
                        r.split_lo(dve, e + 1, c - PER_EXPERT, expert_size[c - PER_EXPERT])

                def body(e, last):
                    first = is_first(e)
                    for j in range(GUS):
                        if not first and j in (2, 4):
                            scattered(e, j // 2 - 1)
                        split(e, 2 * j + LEAD, last)
                        split(e, 2 * j + 1 + LEAD, last)
                        dve.wait_ge(z["sig_ready"], GUS * e + j + 1)
                        if j >= 2:
                            dve.wait_ge(z["hturn_done"], GUS * e + j - 1)
                        stt(sig[:, 0, :], sig[:, 0, :], 1.0, ps[:, j % 2, 0:HC], ALU.add, ALU.mult).then_inc(z["sig_half"], 1)
                        dve.wait_ge(z["sig_half"], GUS * e + j + 1)
                        stt(hid[:, j % 2, 0, :], sig[:, 0, :], 0.5, ps[:, j % 2, HC:2 * HC], ALU.mult,
                            ALU.mult).then_inc(z[f"gu_free{j % 2}"], 1)
                        if j >= 2:
                            turn_part(e, j - 2)
                        if not last and j == 8:
                            dve.wait_ge(z["g_done"], g_done(e, 5) + 1)
                            pick_tokens(e + 1)
                    for d in range(len(DOWN_K)):
                        split(e, GU_CHUNKS + d + LEAD, last)
                        if d == 1:
                            turn_part(e, GUS - 2)
                        if d == 3:
                            turn_part(e, GUS - 1)
                        if not last and d in (5, 7):
                            gather_part(e, (d - 5) // 2)
                    dve.wait_ge(z["y_hi_done"], e + 1)
                    stt(y_lo[:], ps[:, 2:4, :].rearrange("p a b -> p (a b)"), slot_w[:, 0:1], y_hi[:].bitcast(F32),
                        ALU.mult, ALU.subtract).then_inc(z["y_split"], 1)

                pick_tokens(0)
                gather_part(None, 0)
                gather_part(None, 1)
                body(0, False)
                with dve.Fori(1, E - 1) as e:
                    body(e, False)
                body(E - 1, True)
                scattered(E, 0, 2)
                scattered(E, 1, 2)

            moe_pass(Ring(N0, raw_landed, hi_done, lo_done, chunk_used), pass_sems[0])
            dve.wait_ge(counts_ready, 1)
            crowded = dve.value_load(most[0:1, 0:1], min_val=0, max_val=S)
            with dve.If(crowded > P):
                dve.wait_ge(pass_sems[0]["over"], 1)
                link(ts(place[:], place[:], -float(P), None, ALU.add))
                r2 = Ring(0, raw_landed2, hi_done2, lo_done2, chunk_used2)
                for c in range(LEAD):
                    r2.split_lo(dve, 0, c)
                moe_pass(r2, pass_sems[1])


def shape_tables(S, DR, theta):
    import numpy as np
    i = np.arange(P)
    eye = np.eye(P)
    before = (i[:, None] < i[None, :])
    ones = np.ones((P, P))
    iota = np.broadcast_to(i, (P, P))
    mask = np.concatenate([np.zeros((P, P)), np.where(i[None, :] <= i[:, None], 0.0, NEG)], 1)
    pos = np.arange(S, dtype=np.float32)
    inv = np.float32(theta) ** (-np.arange(0, DR, 2, dtype=np.float32) / np.float32(DR))
    ang = pos[:, None] * inv[None, :]
    cs = np.stack([np.cos(ang), np.sin(ang)], 1).reshape(S // P, P, DR).transpose(1, 0, 2).reshape(P, -1)
    return np.ascontiguousarray(np.concatenate([eye, before, ones, iota, mask, cs], 1).astype(np.float32))


_INS = ["x", "mix_norm_g", "w_in", "gm_v_norm_g", "gm_v_norm_b", "gm_w_spatial", "gm_b_spatial", "gm_w_proj",
        "mla_q_lat_g", "mla_w_uq", "mla_kv_lat_g", "mla_w_ukv", "mla_q_norm_g", "mla_k_norm_g", "mla_w_proj",
        "w_out", "ffn_norm_g", "dense_w_gu", "dense_w_down", "moe_w_router", "moe_b_router", "moe_w_gu",
        "moe_w_down"]


def kernel(**inputs):
    import numpy as np
    import concourse.bacc as bacc
    from concourse.bass_utils import run_bass_kernel_spmd

    nc = bacc.Bacc("TRN2", target_bir_lowering=False, num_devices=1)
    arrays, args = {}, []
    for name in _INS:
        a = np.ascontiguousarray(inputs[name])
        arrays[f"in_{name}"] = a
        args.append(nc.dram_tensor(f"in_{name}", a.shape, mybir.dt.from_np(a.dtype), kind="ExternalInput").ap())
    tables = shape_tables(256, 32, 10000.0)
    arrays["shape_consts"] = tables
    args.append(nc.dram_tensor("shape_consts", tables.shape, F32, kind="ExternalInput").ap())
    args.append(nc.dram_tensor("out", (1, 256, 1024), F32, kind="ExternalOutput").ap())
    decoder_trunk(nc, *args)
    r = run_bass_kernel_spmd(nc, [arrays], core_ids=[0])
    return r.results[0]["out"]
```

```python
from contextlib import ExitStack

import concourse.bass as bass
from concourse import mybir

F32 = mybir.dt.float32
F32R = mybir.dt.float32r
I32 = mybir.dt.int32
U32 = mybir.dt.uint32
ALU = mybir.AluOpType
ACT = mybir.ActivationFunctionType
AX = mybir.AxisListType

P = 128
EPS = 1e-6
RAW, SPLIT, LEAD = 4, 3, 3
CHUNK = 2048
STRIP = 512
GELU_A = 0.044715
GELU_C = 0.7978845608028654
RSQRT_SEED = float(0x5F3759DF)
NEG = -1e30


class Chain:

    def __init__(self, eng, sem, base=0):
        self.eng, self.sem, self.base, self.n = eng, sem, base, 0

    def link(self, ins):
        self.n += 1
        ins.then_inc(self.sem, 1)
        self.eng.wait_ge(self.sem, self.base + self.n)


def decoder_trunk(nc, x, mix_norm_g, w_in, gm_v_norm_g, gm_v_norm_b, gm_w_spatial, gm_b_spatial, gm_w_proj,
                  mla_q_lat_g, mla_w_uq, mla_kv_lat_g, mla_w_ukv, mla_q_norm_g, mla_k_norm_g, mla_w_proj,
                  w_out, ffn_norm_g, dense_w_gu, dense_w_down, moe_w_router, moe_b_router, moe_w_gu,
                  moe_w_down, shape_consts, out):
    _, S, D = x.shape
    L = w_in.shape[0]
    TT = S // P
    KD = D // P
    NG = gm_w_spatial.shape[1]
    QL, KVL = mla_w_uq.shape[1], mla_w_ukv.shape[1]
    DQ = mla_q_norm_g.shape[1]
    H = mla_w_uq.shape[2] // DQ
    DV = mla_w_proj.shape[1] // H
    DN = mla_w_ukv.shape[2] // H - DV
    DR = DQ - DN
    HR = DR // 2
    E = moe_w_gu.shape[1]
    FF = moe_w_down.shape[2]
    KF = FF // P
    assert TT == 2 and D == 1024 and dense_w_down.shape[1] == FF and H * DV == D and 2 * DV == P
    OFF_V, OFF_CQ = D, 2 * D
    OFF_CKV = OFF_CQ + QL
    OFF_GATE = OFF_CKV + KVL + DR
    SCALE = float(DQ) ** -0.5
    KQ, KKV = QL // P, KVL // P
    HC = 256
    GUS = FF // HC
    PAIRS = H // 2
    HPS = STRIP // (DN + DV)
    UQS, UKVS = H * DQ // STRIP, H // HPS

    chunks = []

    DOWN_K = [2, 1] * 6 + [2, 2]
    assert sum(DOWN_K) == KF
    GU_CHUNKS = GUS * KD // 4
    PER_EXPERT = GU_CHUNKS + len(DOWN_K)

    def gu_pieces(w_gu, j, k0):
        v = w_gu.rearrange("(k p) n -> p k n", p=P)
        return [v[:, k0:k0 + 4, hh * FF + j * HC:hh * FF + (j + 1) * HC] for hh in range(2)]

    def down_pieces(w_down, d):
        k0, n = sum(DOWN_K[:d]), DOWN_K[d]
        v = w_down.rearrange("(k p) n -> p k n", p=P)
        if n == 2:
            return [v[:, k0, :], v[:, k0 + 1, :]]
        return [v[:, k0, 0:D // 2], v[:, k0, D // 2:D]]

    plan = []
    strip_no = 0
    strip_at, chunk_end = {}, {}

    def mul(l, what, j, k0=0):
        nonlocal strip_no
        w, c0 = {"cq": (w_in, OFF_CQ), "ckv": (w_in, OFF_CKV), "v": (w_in, OFF_V), "u": (w_in, 0),
                 "ga": (w_in, OFF_GATE), "gb": (w_in, OFF_GATE + D), "uq": (mla_w_uq, 0), "ukv": (mla_w_ukv, 0),
                 "pa": (gm_w_proj, 0), "pb": (mla_w_proj, 0), "wo": (w_out, 0), "gu": (None, 0)}[what]
        width = KVL + DR if what == "ckv" else STRIP
        if k0 == 0:
            strip_at[l, what, j] = strip_no
            strip_no += 1
        if what == "gu":
            kt, n = KD, 4
            chunks.append((("gu", *gu_pieces(dense_w_gu[l // 2], j, k0)), n, width))
        else:
            v = w[l].rearrange("(k p) n -> p k n", p=P)[:, :, c0 + j * STRIP:c0 + j * STRIP + width]
            kt = v.shape[1]
            n = min(4, kt - k0)
            h = n // 2
            chunks.append(([(0, h, v[:, k0:k0 + h, :]), (h * width, n - h, v[:, k0 + h:k0 + n, :])], n, width))
        chunk_end[l, what, j] = len(chunks)
        plan.append(("mul", l, what, j, k0, n, k0 + n == kt, width, len(chunks) - 1))

    def evac(l, what, j=0):
        plan.append(("evac", l, what, j))

    for l in range(L):
        def slot(s):
            plan.append(("attention", l, s))

        plan.append(("norm", l, 0))
        plan.append(("norm_turns", l, 0, 0))
        mul(l, "cq", 0)
        plan.append(("norm_turns", l, 0, 1))
        mul(l, "cq", 0, 4)
        evac(l, "cq")
        mul(l, "ckv", 0)
        mul(l, "ckv", 0, 4)
        evac(l, "ckv")
        plan.append(("latent_norm", l))
        mul(l, "v", 0)
        plan.append(("spatial_weights", l))
        plan.append(("latent_turns", l))
        mul(l, "v", 0, 4)
        evac(l, "v", 0)
        for j in range(UQS):
            mul(l, "uq", j)
            evac(l, "uq", j)
        plan.append(("q_norm", l, 0))
        for j in range(UKVS):
            mul(l, "ukv", j)
            evac(l, "ukv", j)
            if j == UKVS // 4:
                plan.append(("q_norm", l, 1))
            if j == UKVS // 2:
                plan.append(("rotary_key", l))
        plan.append(("k_norm", l, 0))
        mul(l, "v", 1)
        plan.append(("k_norm", l, 1))
        mul(l, "v", 1, 4)
        evac(l, "v", 1)
        mul(l, "gb", 0)
        slot(0)
        mul(l, "gb", 0, 4)
        evac(l, "gb", 0)
        slot(1)
        plan.append(("layer_stats", l))
        mul(l, "u", 0)
        slot(2)
        plan.append(("layer_norm", l, 0))
        mul(l, "u", 0, 4)
        evac(l, "u", 0)
        plan.append(("layer_norm", l, 1))
        mul(l, "u", 1)
        slot(3)
        plan.append(("mix_tokens", l))
        plan.append(("branch", l, 0))
        mul(l, "u", 1, 4)
        slot(4)
        evac(l, "u", 1)
        plan.append(("branch", l, 1))
        plan.append(("a_turns", l, 0))
        mul(l, "ga", 0)
        slot(5)
        plan.append(("a_turns", l, 1))
        mul(l, "ga", 0, 4)
        evac(l, "ga", 0)
        slot(6)
        mul(l, "pa", 0)
        slot(7)
        mul(l, "pa", 0, 4)
        evac(l, "pa", 0)
        slot(8)
        mul(l, "gb", 1)
        slot(9)
        mul(l, "gb", 1, 4)
        evac(l, "gb", 1)
        slot(10)
        for what, j in (("ga", 1), ("pa", 1), ("pb", 0)):
            mul(l, what, j)
            mul(l, what, j, 4)
            evac(l, what, j)
        mul(l, "pb", 1)
        plan.append(("merged_turns", l, 0))
        mul(l, "pb", 1, 4)
        evac(l, "pb", 1)
        mul(l, "wo", 0)
        plan.append(("merged_turns", l, 1))
        mul(l, "wo", 1)
        mul(l, "wo", 0, 4)
        evac(l, "wo", 0)
        plan.append(("squares", l, 0))
        mul(l, "wo", 1, 4)
        evac(l, "wo", 1)
        plan.append(("squares", l, 1))
        plan.append(("norm", l, 1))
        plan.append(("norm_turns", l, 1, 0))
        if l % 2:
            plan.append(("norm_turns", l, 1, 1))
        else:
            for j in range(GUS):
                mul(l, "gu", j)
                if j == 0:
                    plan.append(("norm_turns", l, 1, 1))
                mul(l, "gu", j, 4)
                evac(l, "gu", j)
                if j >= 1:
                    plan.append(("hidden_turn", l, j - 1))
            a = len(chunks)
            for d in range(len(DOWN_K)):
                chunks.append((("down", *down_pieces(dense_w_down[l // 2], d)), DOWN_K[d], D))
            plan.append(("hidden_turn", l, GUS - 1))
            plan.append(("down", l, a, len(chunks), strip_no))
            strip_at[l, "down", 0] = strip_no
            strip_no += 2
    assert PAIRS + 3 == 11
    N0 = len(chunks)
    assert N0 % SPLIT == 0 and PER_EXPERT % SPLIT == 0 and PER_EXPERT % RAW == 0

    with ExitStack() as ctx:
        def sb(name, shape, dt=F32, c=ctx):
            return c.enter_context(nc.sbuf_tensor(name, shape, dt))

        def sem(name):
            return ctx.enter_context(nc.semaphore(name))

        ps = ctx.enter_context(nc.psum_tensor("ps", [P, 8, 512], F32))

        raw = sb("raw", [P, RAW, CHUNK])
        w_hi = sb("w_hi", [P, SPLIT, CHUNK], F32R)
        w_lo = sb("w_lo", [P, SPLIT, CHUNK], F32R)
        act_hi = sb("act_hi", [P, KD, S], F32R)
        act_lo = sb("act_lo", [P, KD, S], F32R)
        xres = sb("xres", [P, TT, D])
        CW = shape_consts.shape[1]
        consts = sb("consts", [P, CW])
        o = 0

        def part(n):
            nonlocal o
            o += n
            return consts[:, o - n:o]

        ident, before, ones, iota, bias_mask, cos_sin = (part(n) for n in (P, P, P, P, 2 * P, TT * 2 * HR))
        cos_sin = cos_sin.rearrange("p (t c r) -> p t c r", t=TT, c=2)
        assert o == CW
        row_sizes = [L * KD, L * KD, L * KQ, L * KKV, L * NG]
        ROWS = sum(row_sizes)
        rows = sb("rows", [ROWS, P])
        cols_t = sb("cols_t", [P, ROWS])
        row_at = [sum(row_sizes[:i]) for i in range(5)]
        mix_g, ffn_g, qlat_g, kvlat_g, b_sp = (
            cols_t[:, a:a + n].rearrange("p (l k) -> p l k", l=L) for a, n in zip(row_at, row_sizes))
        q_gain = sb("q_gain", [P, L, DQ])
        k_gain = sb("k_gain", [P, L, DQ])
        qk_gain = sb("qk_gain", [P, L])
        gain_q = sb("gain_q", [P, L])
        gain_k = sb("gain_k", [P, L])
        square_sum = sb("square_sum", [P, 2, TT])
        small = sb("small", [P, 16])
        rs_a = sb("rs_a", [P, 16])
        rs_t = sb("rs_t", [P, 16])
        rs_y = sb("rs_y", [P, 16], I32)

        mixer = ExitStack()
        ln_memory = ExitStack()
        ln_rows = sb("ln_rows", [P, 2, D], F32, ln_memory)
        ln_memory.close()
        t1_hi = sb("t1_hi", [P, KD, S], F32R, mixer)
        t1_lo = sb("t1_lo", [P, KD, S], F32R, mixer)
        bt_hi = sb("bt_hi", [P, KD, S], F32R, mixer)
        bt_lo = sb("bt_lo", [P, KD, S], F32R, mixer)
        vbuf = sb("vbuf", [P, TT, D], F32, mixer)
        tmp = sb("tmp", [P, TT, STRIP], F32, mixer)
        qb = sb("qb", [P, TT, H, DQ], F32, mixer)
        kb = sb("kb", [P, TT, H, DQ], F32, mixer)
        vv = sb("vv", [P, TT, H, DV], F32, mixer)
        ws_t = sb("ws_t", [P, NG, P], F32, mixer)
        qk_t = sb("qk_t", [P, 2, 512], F32, mixer)
        prob = sb("prob", [P, 768], F32, mixer)
        prob_t = sb("prob_t", [P, 768], F32, mixer)
        kr = sb("kr", [P, TT, DR], F32, mixer)
        soft = sb("soft", [P, 3, 4], F32, mixer)
        ws_raw = sb("ws_raw", [P, NG, P], F32, mixer)
        sq = sb("sq", [P, 768], F32, mixer)
        q_sum = sb("q_sum", [P, TT, H], F32, mixer)
        k_sum = sb("k_sum", [P, TT, H], F32, mixer)
        stats = sb("stats", [P, TT, 2, 6], F32, mixer)
        mean_var = sb("mean_var", [P, TT, 2], F32, mixer)
        mixer.close()
        gate_b = [ws_raw[:].rearrange("p g t -> p (g t)").rearrange("p (t n) -> p t n", t=TT),
                  ws_t[:].rearrange("p g t -> p (g t)").rearrange("p (t n) -> p t n", t=TT)]
        probs = [prob, sq]
        ffn = ExitStack()
        hid_hi = sb("hid_hi", [P, KF, S], F32R, ffn)
        hid_lo = sb("hid_lo", [P, KF, S], F32R, ffn)
        xn = sb("xn", [P, TT, D], F32, ffn)
        xn_hi = sb("xn_hi", [P, TT, D], F32R, ffn)
        xn_lo = sb("xn_lo", [P, TT, D], F32R, ffn)
        hid = sb("hid", [P, 2, TT, HC], F32, ffn)
        sig = sb("sig", [P, TT, HC], F32, ffn)
        y_hi = sb("y_hi", [P, D], F32R, ffn)
        y_lo = sb("y_lo", [P, D], F32R, ffn)
        pick = sb("pick", [P, TT, P], F32R, ffn)
        pick_w = sb("pick_w", [P, TT], F32, ffn)
        put = sb("put", [P, S], F32R, ffn)
        slot_w = sb("slot_w", [P, 1], F32, ffn)
        wr = sb("wr", [P, KD, E], F32, ffn)
        wr_hi = sb("wr_hi", [P, KD, E], F32R, ffn)
        wr_lo = sb("wr_lo", [P, KD, E], F32R, ffn)
        br = sb("br", [P, E], F32, ffn)
        logit = sb("logit", [P, TT, E], F32, ffn)
        top = sb("top", [P, TT, 8], F32, ffn)
        top_i = sb("top_i", [P, TT, 8], U32, ffn)
        top_f = sb("top_f", [P, TT, 8], F32, ffn)
        one_a = sb("one_a", [P, TT, E], F32, ffn)
        one_b = sb("one_b", [P, TT, E], F32, ffn)
        chosen = sb("chosen", [P, TT, E], F32, ffn)
        combine = sb("combine", [P, TT, E], F32, ffn)
        place = sb("place", [P, TT, E], F32, ffn)
        rt = sb("rt", [P, TT, 4], F32, ffn)
        most = sb("most", [P, 2], I32, ffn)
        most_f = sb("most_f", [P, 2], F32, ffn)
        ffn.close()

        raw_landed = [sem(f"raw_landed{i}") for i in range(RAW)]
        raw_landed2 = [sem(f"raw_landed2_{i}") for i in range(RAW)]
        hi_done, lo_done, chunk_used = sem("hi_done"), sem("lo_done"), sem("chunk_used")
        hi_done2, lo_done2, chunk_used2 = sem("hi_done2"), sem("lo_done2"), sem("chunk_used2")
        x_landed, small_landed, out_stored = sem("x_landed"), sem("small_landed"), sem("out_stored")
        rows_landed, rows_turned, gains_ready = sem("rows_landed"), sem("rows_turned"), sem("gains_ready")
        ws_landed, ln_landed, wr_landed, qk_gain_ready = sem("ws_landed"), sem("ln_landed"), sem("wr_landed"), sem("qk_gain_ready")
        strip_free = [sem("strip_free0"), sem("strip_free1")]
        turn_done, turn_hi = sem("turn_done"), sem("turn_hi")
        turn_free = [sem("turn_free0"), sem("turn_free1")]
        act_own, dve_own = sem("act_own"), sem("dve_own")
        squares_done, root_done = sem("squares_done"), sem("root_done")
        normed0_done, normed1_done = sem("normed0_done"), sem("normed1_done")
        latent_normed = sem("latent_normed")
        gelu_sq, gelu_arg, gelu_tanh = sem("gelu_sq"), sem("gelu_arg"), sem("gelu_tanh")
        v_normed, ws_masked, branch_a = sem("v_normed"), sem("ws_masked"), sem("branch_a")
        head_squares, head_sums = sem("head_squares"), sem("head_sums")
        q_ready, k_ready = sem("q_ready"), sem("k_ready")
        scores_done, scores_read, max_ready, exp_done, prob_ready = (
            sem("scores_done"), sem("scores_read"), sem("max_ready"), sem("exp_done"), sem("prob_ready"))
        merged_b, sig_done = sem("merged_b"), sem("sig_done")
        xn_hi_done, xn_lo_done, wr_hi_done, wr_lo_done = (
            sem("xn_hi_done"), sem("xn_lo_done"), sem("wr_hi_done"), sem("wr_lo_done"))
        logits_done, chosen_ready, gap_ready, gap_exp, places_done, counts_ready = (
            sem("logits_done"), sem("chosen_ready"), sem("gap_ready"), sem("gap_exp"), sem("places_done"),
            sem("counts_ready"))
        pass_sems = []
        for q in range(2):
            pass_sems.append({n: sem(f"{n}_{q}") for n in (
                "gu_free0", "gu_free1", "sig_ready", "sig_half", "hturn_done", "hturn_hi", "hturn_free0",
                "hturn_free1", "y_hi_done", "y_split", "g_done", "g_hi", "g_free0", "g_free1", "picked", "over")})

        def raw_view(slot, n, w):
            return raw[:, slot, 0:n * w].rearrange("p (k n) -> p k n", k=n)

        class Ring:

            def __init__(self, n0, landed, hi, lo, used):
                self.n0, self.landed, self.hi, self.lo, self.used = n0, landed, hi, lo, used

            def count(self, e, j):
                return self.n0 + j + PER_EXPERT * e

            def raw_slot(self, j):
                return (self.n0 + j) % RAW

            def split_slot(self, j):
                return (self.n0 + j) % SPLIT

            def load(self, sp, e, j, pieces):
                if self.n0 + j >= RAW or not isinstance(e, int) or e > 0:
                    sp.wait_ge(self.lo, self.count(e, j) - RAW + 1)
                for dst, src in pieces:
                    sp.dma_start(dst, src).then_inc(self.landed[self.raw_slot(j)], 16)

            def split_hi(self, act, e, j, n=CHUNK):
                s = self.raw_slot(j)
                act.wait_ge(self.landed[s], 32 * ((self.n0 + j) // RAW + 1) + 32 * (PER_EXPERT // RAW) * e)
                if self.n0 + j >= SPLIT or not isinstance(e, int) or e > 0:
                    act.wait_ge(self.used, self.count(e, j) - SPLIT + 1)
                nc.scalar.activation(w_hi[:, self.split_slot(j), 0:n], raw[:, s, 0:n], ACT.Copy).then_inc(self.hi, 1)

            def split_lo(self, dve, e, j, n=CHUNK):
                dve.wait_ge(self.hi, self.count(e, j) + 1)
                c = self.split_slot(j)
                nc.vector.tensor_tensor(w_lo[:, c, 0:n], raw[:, self.raw_slot(j), 0:n],
                                        w_hi[:, c, 0:n].bitcast(F32), ALU.subtract).then_inc(self.lo, 1)

            def take(self, pe, e, j):
                pe.wait_ge(self.lo, self.count(e, j) + 1)
                c = self.split_slot(j)
                return w_hi[:, c, :], w_lo[:, c, :]

        ring = Ring(0, raw_landed, hi_done, lo_done, chunk_used)
        size = [n * w for _, n, w in chunks]
        DOWN_SIZE = [n * D for n in DOWN_K]
        expert_size = [CHUNK] * GU_CHUNKS + DOWN_SIZE

        def three(dst, a_hi, a_lo, b_hi, b_lo, start, stop):
            nc.tensor.matmul(dst, a_hi, b_hi, start=start, stop=False)
            nc.tensor.matmul(dst, a_lo, b_hi, start=False, stop=False)
            return nc.tensor.matmul(dst, a_hi, b_lo, start=False, stop=stop)

        def turns_in(step):
            if step[0] == "attention":
                s = step[2]
                return (2 if s < PAIRS else 0) + (2 if 2 <= s < PAIRS + 2 else 0) + (1 if 3 <= s else 0)
            return {"norm_turns": 2, "latent_turns": 3, "spatial_weights": 2, "mix_tokens": 4, "merged_turns": 2,
                    "a_turns": 2, "hidden_turn": 1}.get(step[0], 0)

        turn_at, ws_turn, t = [], [], 0
        last_turn = {}
        prob_turn, qk_turn = {}, {}
        for step in plan:
            if step[0] == "spatial_weights":
                ws_turn.append(t)
            turn_at.append(t)
            if step[0] == "attention":
                s, b = step[2], t + (1 if 3 <= step[2] else 0)
                if 2 <= s < PAIRS + 2:
                    prob_turn[step[1], s - 2] = b
                    b += 2
                if s < PAIRS:
                    qk_turn[step[1], s] = b
            t += turns_in(step)
            if turns_in(step):
                last_turn[step] = t - 1
        ALL_TURNS = t

        def wait_turn_read(eng, b):
            eng.wait_ge(turn_free[b % 2], b // 2 + 1)

        def operand_turns(l, what, k0):
            half = k0 // 4
            return {"cq": lambda: last_turn["norm_turns", l, 0, half],
                    "gu": lambda: last_turn["norm_turns", l, 1, half],
                    "uq": lambda: last_turn["latent_turns", l] - 1,
                    "ukv": lambda: last_turn["latent_turns", l],
                    "pa": lambda: last_turn["a_turns", l, half],
                    "pb": lambda: turn_at[plan.index(("attention", l, 4 * half + 3 + 3))],
                    "wo": lambda: last_turn["merged_turns", l, half]}.get(what, lambda: None)()

        def wait_strip_read(eng, n):
            eng.wait_ge(strip_free[n % 2], n // 2 + 1)

        def is_first(e):
            return isinstance(e, int) and e == 0

        def strips_read(e, j):
            return ((GUS + 1) // 2 if j % 2 == 0 else GUS // 2) * e + j // 2

        def g_done(e, g):
            return 8 * e - 2 + g

        def g_read(e, g):
            return 4 * e - 1 + g // 2

        def layer_over(l):
            return strip_at[l, "down", 0] + 1

        block = ctx.enter_context(nc.Block())

        @block.sync
        def _(sp):
            for t in range(TT):
                sp.dma_start(xres[:, t, :], x[0, t * P:(t + 1) * P, :]).then_inc(x_landed, 16)
            sp.dma_start(consts[:], shape_consts).then_inc(x_landed, 16)
            for i, src in enumerate((mix_norm_g.rearrange("l (k p) -> (l k) p", p=P),
                                     ffn_norm_g.rearrange("l (k p) -> (l k) p", p=P),
                                     mla_q_lat_g.rearrange("l (k p) -> (l k) p", p=P),
                                     mla_kv_lat_g.rearrange("l (k p) -> (l k) p", p=P),
                                     gm_b_spatial.rearrange("l g p -> (l g) p"))):
                sp.dma_start(rows[row_at[i]:row_at[i] + row_sizes[i], :], src).then_inc(rows_landed, 16)

            def static_load(n):
                pieces, k, w = chunks[n]
                slot = n % RAW
                v = raw_view(slot, k, w)
                if pieces[0] == "gu":
                    ring.load(sp, 0, n, [(v[:, :, 0:HC], pieces[1]), (v[:, :, HC:2 * HC], pieces[2])])
                elif pieces[0] == "down":
                    half = k * w // 2
                    ring.load(sp, 0, n, [(raw[:, slot, 0:half], pieces[1]), (raw[:, slot, half:2 * half], pieces[2])])
                else:
                    ring.load(sp, 0, n, [(v[:, c // w:c // w + kk, :], src) for c, kk, src in pieces])

            for n in range(RAW):
                static_load(n)
            for n in range(RAW, N0):
                static_load(n)

            def expert_loads(r, e):
                for j in range(GU_CHUNKS):
                    v = raw_view(r.raw_slot(j), 4, STRIP)
                    g, u = gu_pieces(moe_w_gu[0, e], j // 2, 4 * (j % 2))
                    r.load(sp, e, j, [(v[:, :, 0:HC], g), (v[:, :, HC:2 * HC], u)])
                for d in range(len(DOWN_K)):
                    s = r.raw_slot(GU_CHUNKS + d)
                    half = DOWN_SIZE[d] // 2
                    a, b = down_pieces(moe_w_down[0, e], d)
                    r.load(sp, e, GU_CHUNKS + d, [(raw[:, s, 0:half], a), (raw[:, s, half:2 * half], b)])

            r = Ring(N0, raw_landed, hi_done, lo_done, chunk_used)
            with sp.Fori(0, E) as e:
                expert_loads(r, e)
            sp.wait_ge(counts_ready, 1)
            crowded = sp.value_load(most[0:1, 0:1], min_val=0, max_val=S)
            sp.wait_ge(pass_sems[0]["over"], 1)
            with sp.If(crowded > P):
                r2 = Ring(0, raw_landed2, hi_done2, lo_done2, chunk_used2)
                expert_loads(r2, 0)
                with sp.Fori(1, E) as e:
                    expert_loads(r2, e)
                sp.wait_ge(pass_sems[1]["over"], 1)
            sp.dma_start(out[0].rearrange("(t p) d -> p t d", p=P), xres[:]).then_inc(out_stored, 16)
            sp.wait_ge(out_stored, 16)

        @block.gpsimd
        def _(pool):
            for l in range(L):
                for dst, src in ((q_gain, mla_q_norm_g), (k_gain, mla_k_norm_g)):
                    pool.dma_start(dst[:, l, :], src[l:l + 1, :].to_broadcast([P, DQ])).then_inc(small_landed, 16)
            with nc.allow_non_contiguous_dma(reason="gains as columns, 256 bytes each"):
                for l in range(L):
                    for dst, src in ((gain_q, mla_q_norm_g), (gain_k, mla_k_norm_g)):
                        pool.dma_start(dst[0:DN, l:l + 1], src[l:l + 1, 0:DN].rearrange("o d -> d o")
                                       ).then_inc(small_landed, 16)
            for l in range(L):
                if l:
                    wait_strip_read(pool, layer_over(l - 1) - 1)
                    wait_strip_read(pool, layer_over(l - 1))
                pool.dma_start(ws_raw[:], gm_w_spatial[l].rearrange("g t s -> t g s")).then_inc(ws_landed, 16)
                wait_turn_read(pool, ws_turn[l])
                wait_turn_read(pool, ws_turn[l] + 1)
                nc.gpsimd.affine_select(out=ws_t[:], in_=ws_t[:], compare_op=ALU.is_ge, fill=0.0, base=0,
                                        pattern=[[0, NG], [1, P]], channel_multiplier=-1).then_inc(ws_masked, 1)
                pool.wait_ge(chunk_used, chunk_end[l, "ukv", UKVS - 1])
                pool.dma_start(ln_rows[:, 0, :], gm_v_norm_g[l:l + 1, :].to_broadcast([P, D])).then_inc(ln_landed, 16)
                pool.dma_start(ln_rows[:, 1, :], gm_v_norm_b[l:l + 1, :].to_broadcast([P, D])).then_inc(ln_landed, 16)
            wait_strip_read(pool, strip_at[L - 1, "wo", 0])
            wait_strip_read(pool, strip_at[L - 1, "wo", 1])
            with nc.allow_non_contiguous_dma(reason="the router, 32 KiB"):
                pool.dma_start(wr[:], moe_w_router[0].rearrange("(k p) e -> p k e", p=P)).then_inc(wr_landed, 16)
            pool.dma_start(br[:], moe_b_router[0:1, :].to_broadcast([P, E])).then_inc(wr_landed, 16)
            pool.wait_ge(small_landed, 16 * 4 * L)
            pool.wait_ge(wr_landed, 32)

        @block.tensor
        def _(pe):
            def turn_bank(b):
                if b >= 2:
                    wait_turn_read(pe, b - 2)
                return ps[:, 4 + b % 2, :]

            def turn4(b, src):
                bank = turn_bank(b)
                for i in range(4):
                    mm = nc.tensor.transpose(bank[:, i * P:(i + 1) * P], src(i // TT, i % TT), ident)
                mm.then_inc(turn_done, 1)

            def wait_turns_split(b):
                wait_turn_read(pe, b - 1)
                wait_turn_read(pe, b - 2)

            operands = {"cq": (act_hi, act_lo, 0), "ckv": (act_hi, act_lo, 0), "v": (act_hi, act_lo, 0),
                        "u": (act_hi, act_lo, 0), "ga": (act_hi, act_lo, 0), "gb": (act_hi, act_lo, 0),
                        "gu": (act_hi, act_lo, 0), "uq": (t1_hi, t1_lo, 0), "ukv": (t1_hi, t1_lo, KQ),
                        "pa": (t1_hi, t1_lo, 0), "pb": (bt_hi, bt_lo, 0), "wo": (act_hi, act_lo, 0)}
            latents = qb[:].rearrange("p t h d -> p (t h d)")
            CKV0, CKVW = TT * QL, KVL + DR

            pe.wait_ge(x_landed, 48)
            pe.wait_ge(rows_landed, 80)
            nc.tensor.transpose(ps[:, 6, 0:ROWS], rows[:], ident[0:ROWS, 0:ROWS]).then_inc(rows_turned, 1)
            for i, step in enumerate(plan):
                kind, l, b0 = step[0], step[1], turn_at[i]
                if kind == "norm_turns":
                    m, half = 2 * l + step[2], step[3]
                    src = xn if step[2] else vbuf
                    pe.wait_ge(normed0_done, 2 * m + half + 1)
                    pe.wait_ge(normed1_done, 2 * m + half + 1)
                    for b in range(2):
                        c = 4 * half + 2 * b
                        turn4(b0 + b, lambda k, t: src[:, t, (c + k) * P:(c + k + 1) * P])
                elif kind == "spatial_weights":
                    pe.wait_ge(ws_landed, 16 * (l + 1))
                    for b in range(2):
                        bank = turn_bank(b0 + b)
                        for g in range(4):
                            mm = nc.tensor.transpose(bank[:, g * P:(g + 1) * P], ws_raw[:, 4 * b + g, :], ident)
                        mm.then_inc(turn_done, 1)
                elif kind == "latent_turns":
                    pe.wait_ge(latent_normed, l + 1)
                    for b in range(2):
                        turn4(b0 + b, lambda k, t: latents[:, t * QL + (2 * b + k) * P:t * QL + (2 * b + k + 1) * P])
                    turn4(b0 + 2, lambda k, t: latents[:, CKV0 + t * CKVW + k * P:CKV0 + t * CKVW + (k + 1) * P])
                elif kind == "mix_tokens":
                    pe.wait_ge(v_normed, TT * (l + 1))
                    pe.wait_ge(ws_masked, l + 1)
                    for b in range(4):
                        bank = turn_bank(b0 + b)
                        for g in range(2):
                            c = (2 * b + g) * P
                            mm = nc.tensor.matmul(bank[:, g * S:(g + 1) * S].rearrange("p (t d) -> p t d", t=TT),
                                                  ws_t[:, 2 * b + g, :], vbuf[:, :, c:c + P], start=True, stop=True)
                        mm.then_inc(turn_done, 1)
                elif kind == "a_turns":
                    j = step[2]
                    pe.wait_ge(branch_a, 2 * l + j + 1)
                    for b in range(2):
                        turn4(b0 + b, lambda k, t: vbuf[:, t, (4 * j + 2 * b + k) * P:(4 * j + 2 * b + k + 1) * P])
                elif kind == "merged_turns":
                    half = step[2]
                    pe.wait_ge(merged_b, 2 * l + half + 1)
                    for b in range(2):
                        c = 4 * half + 2 * b
                        turn4(b0 + b, lambda k, t: vbuf[:, t, (c + k) * P:(c + k + 1) * P])
                elif kind == "hidden_turn":
                    j = step[2]
                    wait_strip_read(pe, strip_at[l, "gu", j])
                    turn4(b0, lambda k, t: hid[:, j % 2, t, k * P:(k + 1) * P])
                elif kind == "attention":
                    s, b = step[2], b0
                    if s >= 3:
                        n = s - 3
                        wait_turn_read(pe, prob_turn[l, n])
                        wait_turn_read(pe, prob_turn[l, n] + 1)
                        bank = turn_bank(b)
                        for hh in range(2):
                            dst = bank[hh * DV:(hh + 1) * DV, :]
                            v0, v1 = vv[:, 0, 2 * n + hh, :], vv[:, 1, 2 * n + hh, :]
                            t10, t11 = 2 + 2 * hh, 3 + 2 * hh
                            nc.tensor.matmul(dst[:, 0:P], v0, prob_t[:, hh * P:(hh + 1) * P], start=True, stop=True)
                            nc.tensor.matmul(dst[:, P:S], v0, prob_t[:, t10 * P:(t10 + 1) * P], start=True, stop=False)
                            mm = nc.tensor.matmul(dst[:, P:S], v1, prob_t[:, t11 * P:(t11 + 1) * P], start=False, stop=True)
                        mm.then_inc(turn_done, 1)
                        b += 1
                    if 1 <= s < PAIRS + 1:
                        n = PAIRS * l + s - 1
                        wait_turn_read(pe, qk_turn[l, s - 1])
                        wait_turn_read(pe, qk_turn[l, s - 1] + 1)
                        if n:
                            pe.wait_ge(scores_read, n)
                        for hh in range(2):
                            q_t, k_t = qk_t[0:DQ, hh, 0:S], qk_t[0:DQ, hh, S:2 * S]
                            nc.tensor.matmul(ps[:, 6, hh * P:(hh + 1) * P], q_t[:, 0:P], k_t[:, 0:P], start=True, stop=True)
                            mm = nc.tensor.matmul(ps[:, 7, hh * S:(hh + 1) * S], q_t[:, P:S], k_t, start=True, stop=True)
                        mm.then_inc(scores_done, 1)
                    if 2 <= s < PAIRS + 2:
                        pe.wait_ge(prob_ready, PAIRS * l + s - 1)
                        for blocks in ((0, 1, 2, 3), (4, 5)):
                            bank = turn_bank(b)
                            for q, blk in enumerate(blocks):
                                mm = nc.tensor.transpose(bank[:, q * P:(q + 1) * P], probs[s % 2][:, blk * P:(blk + 1) * P], ident)
                            mm.then_inc(turn_done, 1)
                            b += 1
                    if s < PAIRS:
                        if s == 0:
                            pe.wait_ge(q_ready, TT * (l + 1))
                            pe.wait_ge(k_ready, TT * (l + 1))
                        for hh in range(2):
                            bank = turn_bank(b)
                            for q in range(4):
                                src = (qb, kb)[q // 2]
                                mm = nc.tensor.transpose(bank[0:DQ, q * P:(q + 1) * P], src[:, q % 2, 2 * s + hh, :], ident)
                            mm.then_inc(turn_done, 1)
                            b += 1
                elif kind == "mul":
                    _, _, what, j, k0, kt, ends, width, c = step
                    hi, lo, k_at = operands[what]
                    n = strip_at[l, what, j]
                    turned = operand_turns(l, what, k0)
                    if j == 0 and turned is not None:
                        wait_turns_split(turned + 1)
                    if n >= 2 and k0 == 0:
                        wait_strip_read(pe, n - 2)
                    ch, cl = ring.take(pe, 0, c)
                    for t in range(TT):
                        for k in range(kt):
                            kk = k_at + k0 + k
                            mm = three(ps[:, 2 * (n % 2) + t, 0:width], hi[:, kk, t * P:(t + 1) * P],
                                       lo[:, kk, t * P:(t + 1) * P], ch[:, k * width:(k + 1) * width],
                                       cl[:, k * width:(k + 1) * width], k0 + k == 0, ends and k == kt - 1)
                    mm.then_inc(chunk_used, 1)
                elif kind == "down":
                    a, n = step[2], step[4]
                    wait_turns_split(b0)
                    wait_strip_read(pe, n - 2)
                    wait_strip_read(pe, n - 1)
                    k_at = 0
                    for d, kt in enumerate(DOWN_K):
                        ch, cl = ring.take(pe, 0, a + d)
                        for t in range(TT):
                            for k in range(kt):
                                kk = k_at + k
                                for hf in range(2):
                                    c = k * D + hf * 512
                                    mm = three(ps[:, (2 * n + 2 * t) % 4 + hf, :], hid_hi[:, kk, t * P:(t + 1) * P],
                                               hid_lo[:, kk, t * P:(t + 1) * P], ch[:, c:c + 512], cl[:, c:c + 512],
                                               kk == 0, kk == KF - 1)
                        mm.then_inc(chunk_used, 1)
                        k_at += kt

            wait_turns_split(ALL_TURNS)
            pe.wait_ge(wr_lo_done, 1)
            for t in range(TT):
                for k in range(KD):
                    mm = three(ps[:, 4, t * E:(t + 1) * E], act_hi[:, k, t * P:(t + 1) * P],
                               act_lo[:, k, t * P:(t + 1) * P], wr_hi[:, k, :], wr_lo[:, k, :], k == 0, k == KD - 1)
            mm.then_inc(logits_done, 1)
            pe.wait_ge(chosen_ready, 1)
            nc.tensor.matmul(ps[:, 5, 0:E], before, chosen[:, 0, :], start=True, stop=True)
            nc.tensor.matmul(ps[:, 5, E:2 * E], before, chosen[:, 1, :], start=True, stop=False)
            nc.tensor.matmul(ps[:, 5, E:2 * E], ones, chosen[:, 0, :], start=False, stop=True)
            nc.tensor.matmul(ps[:, 5, 2 * E:3 * E], ones, chosen[:, 0, :], start=True, stop=False)
            nc.tensor.matmul(ps[:, 5, 2 * E:3 * E], ones, chosen[:, 1, :], start=False, stop=True).then_inc(places_done, 1)

            def moe_pass(r, z):
                def gather(half):
                    bank = ps[:, 6 + half, :]
                    for k in range(4):
                        c = (4 * half + k) * P
                        for t in range(TT):
                            nc.tensor.matmul(bank[:, k * P:(k + 1) * P], xn_hi[:, t, c:c + P], pick[:, t, :],
                                             start=t == 0, stop=False)
                            mm = nc.tensor.matmul(bank[:, k * P:(k + 1) * P], xn_lo[:, t, c:c + P], pick[:, t, :],
                                                  start=False, stop=t == TT - 1)
                    mm.then_inc(z["g_done"], 1)

                def scatter(t, g_read):
                    for hf in range(2):
                        pe.wait_ge(z[f"g_free{hf}"], g_read)
                        nc.tensor.matmul(ps[:, 6 + hf, :], put[:, t * P:(t + 1) * P], y_hi[:, hf * 512:(hf + 1) * 512],
                                         start=True, stop=False)
                        nc.tensor.matmul(ps[:, 6 + hf, :], put[:, t * P:(t + 1) * P], y_lo[:, hf * 512:(hf + 1) * 512],
                                         start=False, stop=True).then_inc(z["g_done"], 1)

                def hidden_turn(e, j):
                    pe.wait_ge(z[f"gu_free{j % 2}"], strips_read(e, j) + 1)
                    if j >= 2 or not is_first(e):
                        pe.wait_ge(z[f"hturn_free{j % 2}"], strips_read(e, j))
                    for k in range(2):
                        mm = nc.tensor.transpose(ps[:, 4 + j % 2, k * P:(k + 1) * P], hid[:, j % 2, 0, k * P:(k + 1) * P], ident)
                    mm.then_inc(z["hturn_done"], 1)

                def body(e, last):
                    first = is_first(e)
                    for j in range(GUS):
                        if j >= 2 or not first:
                            pe.wait_ge(z[f"gu_free{j % 2}"], strips_read(e, j))
                        if j == 0:
                            pe.wait_ge(z["g_free0"], 1 if first else g_read(e, 0))
                            pe.wait_ge(z["g_free1"], 1 if first else g_read(e, 0))
                        for c in range(2):
                            ch, cl = r.take(pe, e, 2 * j + c)
                            for k in range(4):
                                kk = 4 * c + k
                                mm = three(ps[:, j % 2, :], act_hi[:, kk, 0:P], act_lo[:, kk, 0:P],
                                           ch[:, k * STRIP:(k + 1) * STRIP], cl[:, k * STRIP:(k + 1) * STRIP],
                                           kk == 0, kk == KD - 1)
                            mm.then_inc(r.used, 1)
                            if c == 0 and j >= 2:
                                hidden_turn(e, j - 2)
                        if not first and j == 1:
                            pe.wait_ge(z["y_split"], e)
                            scatter(0, g_read(e, 0))
                        if not first and j == 3:
                            scatter(1, g_read(e, 2))
                        if j == 5:
                            pe.wait_ge(z["g_free0"], g_read(e, 4))
                            for t in range(TT):
                                mm = nc.tensor.transpose(ps[:, 6, t * P:(t + 1) * P], pick[:, t, :].bitcast(F32), ident)
                            mm.then_inc(z["g_done"], 1)
                            pe.wait_ge(z["g_free1"], g_read(e, 4))
                            for t in range(TT):
                                mm = nc.tensor.matmul(ps[:, 7, 0:1], pick[:, t, :].bitcast(F32), pick_w[:, t:t + 1],
                                                      start=t == 0, stop=t == TT - 1)
                            mm.then_inc(z["g_done"], 1)
                    k_at = 0
                    for d, kt in enumerate(DOWN_K):
                        if d == 0 and not first:
                            pe.wait_ge(z["y_split"], e)
                        ch, cl = r.take(pe, e, GU_CHUNKS + d)
                        s = (k_at + kt - 1) // 2
                        if s > (k_at - 1) // 2 or not k_at:
                            pe.wait_ge(z[f"hturn_free{s % 2}"], strips_read(e, s) + 1)
                        for k in range(kt):
                            kk = k_at + k
                            for hf in range(2):
                                c = k * D + hf * 512
                                mm = three(ps[:, 2 + hf, :], hid_hi[:, kk, 0:P], hid_lo[:, kk, 0:P], ch[:, c:c + 512],
                                           cl[:, c:c + 512], kk == 0, kk == KF - 1)
                        mm.then_inc(r.used, 1)
                        k_at += kt
                        if d == 0:
                            hidden_turn(e, GUS - 2)
                        if d == 2:
                            hidden_turn(e, GUS - 1)
                        if not last and d in (4, 6):
                            if d == 4:
                                pe.wait_ge(z["picked"], e + 2)
                            pe.wait_ge(z[f"g_free{(d - 4) // 2}"], g_read(e, 6))
                            gather((d - 4) // 2)

                pe.wait_ge(z["picked"], 1)
                gather(0)
                gather(1)
                body(0, False)
                with pe.Fori(1, E - 1) as e:
                    body(e, False)
                body(E - 1, True)
                pe.wait_ge(z["y_split"], E)
                scatter(0, g_read(E, 0) - 1)
                scatter(1, g_read(E, 2) - 1)

            pe.wait_ge(xn_lo_done, 1)
            moe_pass(Ring(N0, raw_landed, hi_done, lo_done, chunk_used), pass_sems[0])
            pe.wait_ge(counts_ready, 1)
            crowded = pe.value_load(most[0:1, 0:1], min_val=0, max_val=S)
            with pe.If(crowded > P):
                pe.wait_ge(pass_sems[0]["over"], 1)
                moe_pass(Ring(0, raw_landed2, hi_done2, lo_done2, chunk_used2), pass_sems[1])

        @block.scalar
        def _(act):
            own = Chain(act, act_own)
            latents = qb[:].rearrange("p t h d -> p (t h d)")
            CKV0, CKVW = TT * QL, KVL + DR
            counts = {"split_turns": 0, "head_sums": 0}

            def copy(dst, src, scale=1.0):
                return nc.scalar.activation(dst, src, ACT.Copy, scale=scale)

            def splits(a, b):
                for n in range(a + LEAD, b + LEAD):
                    ring.split_hi(act, 0, n, size[n] if n < N0 else CHUNK)

            def turn_hi_parts(b, hi, k0, scale):
                act.wait_ge(turn_done, b + 1)
                for k in range(2):
                    op = copy(hi[:, k0 + k, :], ps[:, 4 + b % 2, k * S:(k + 1) * S], scale(k0 + k))
                op.then_inc(turn_hi, 1)

            act.wait_ge(x_landed, 48)
            for i, step in enumerate(plan):
                kind, l, b0 = step[0], step[1], turn_at[i]
                if kind == "squares":
                    half = step[2]
                    cols = slice(half * STRIP, (half + 1) * STRIP)
                    wait_strip_read(act, strip_at[l, "wo", half])
                    for t in range(TT):
                        nc.scalar.activation(xn[:, t, cols], xres[:, t, cols], ACT.Square,
                                             accum_out=square_sum[:, half, t:t + 1]).then_inc(squares_done, 1)
                elif kind == "norm":
                    dst = xn if step[2] else vbuf
                    m = 2 * l + step[2]
                    if not step[2]:
                        for t in range(TT):
                            if l:
                                wait_strip_read(act, layer_over(l - 1) - 1 + t)
                            nc.scalar.activation(dst[:, t, :], xres[:, t, :], ACT.Square,
                                                 accum_out=square_sum[:, 0, t:t + 1]).then_inc(squares_done, 1)
                    if not m:
                        act.wait_ge(rows_turned, 1)
                        copy(cols_t[:], ps[:, 6, 0:ROWS]).then_inc(gains_ready, 1)
                        act.wait_ge(gains_ready, 1)
                    act.wait_ge(root_done, m + 1)
                    for half in range(2):
                        cols = slice(half * STRIP, (half + 1) * STRIP)
                        copy(dst[:, 0, cols], xres[:, 0, cols], small[:, 2:3]).then_inc(normed0_done, 1)
                    if not m:
                        ring.split_hi(act, 0, 0, size[0])
                elif kind == "norm_turns":
                    g = ffn_g if step[2] else mix_g
                    for b in range(2):
                        turn_hi_parts(b0 + b, act_hi, 4 * step[3] + 2 * b, lambda k: g[:, l, k:k + 1])
                    if (l, step[2], step[3]) == (0, 0, 0):
                        for n in range(1, LEAD):
                            ring.split_hi(act, 0, n, size[n])
                elif kind == "spatial_weights":
                    for b in range(2):
                        act.wait_ge(turn_done, b0 + b + 1)
                        copy(ws_t[:, 4 * b:4 * b + 4, :], ps[:, 4 + (b0 + b) % 2, :].rearrange("p (g s) -> p g s", g=4)
                             ).then_inc(turn_free[(b0 + b) % 2], 1)
                elif kind == "latent_turns":
                    for b in range(2):
                        turn_hi_parts(b0 + b, t1_hi, 2 * b, lambda k: qlat_g[:, l, k:k + 1])
                    turn_hi_parts(b0 + 2, t1_hi, KQ, lambda k: kvlat_g[:, l, k - KQ:k - KQ + 1])
                elif kind == "a_turns":
                    for b in range(2):
                        turn_hi_parts(b0 + b, t1_hi, 4 * step[2] + 2 * b, lambda k: 1.0)
                elif kind == "merged_turns":
                    for b in range(2):
                        turn_hi_parts(b0 + b, act_hi, 4 * step[2] + 2 * b, lambda k: 0.5)
                elif kind == "hidden_turn":
                    turn_hi_parts(b0, hid_hi, 2 * step[2], lambda k: 1.0)
                elif kind in ("q_norm", "k_norm"):
                    t = step[2]
                    src, w = (qb, DQ) if kind == "q_norm" else (kb, DN)
                    last = ("uq", H * DQ // STRIP - 1) if kind == "q_norm" else ("ukv", H // HPS - 1)
                    wait_strip_read(act, strip_at[l, last[0], last[1]])
                    for hf in range(2):
                        if counts["head_sums"]:
                            act.wait_ge(head_sums, counts["head_sums"])
                        counts["head_sums"] += 1
                        nc.scalar.activation(sq[:, 0:8 * w].rearrange("p (h d) -> p h d", h=8),
                                             src[:, t, 8 * hf:8 * hf + 8, 0:w], ACT.Square).then_inc(head_squares, 1)
                elif kind == "attention":
                    s, b = step[2], b0
                    if s >= 3:
                        act.wait_ge(turn_done, b + 1)
                        copy(bt_hi[:, s - 3, :], ps[:, 4 + b % 2, 0:S]).then_inc(turn_hi, 1)
                        b += 1
                    if 2 <= s < PAIRS + 2:
                        for c, w in ((0, 512), (512, 256)):
                            act.wait_ge(turn_done, b + 1)
                            copy(prob_t[:, c:c + w], ps[:, 4 + b % 2, 0:w]).then_inc(turn_free[b % 2], 1)
                            b += 1
                    if s < PAIRS:
                        if s >= 1:
                            act.wait_ge(scores_done, PAIRS * l + s)
                        for hh in range(2):
                            act.wait_ge(turn_done, b + 1)
                            if not l and not s and not hh:
                                act.wait_ge(qk_gain_ready, 1)
                            copy(qk_t[0:DQ, hh, 0:S], ps[0:DQ, 4 + b % 2, 0:S], qk_gain[0:DQ, l:l + 1])
                            copy(qk_t[0:DQ, hh, S:2 * S], ps[0:DQ, 4 + b % 2, S:2 * S]).then_inc(turn_free[b % 2], 1)
                            b += 1
                    if 1 <= s < PAIRS + 1:
                        act.wait_ge(max_ready, PAIRS * l + s)
                        pr = probs[(s - 1) % 2]
                        for q, (c, w) in enumerate(((0, P), (P, P), (2 * P, S), (2 * P + S, S))):
                            op = nc.scalar.activation(pr[:, c:c + w], pr[:, c:c + w], ACT.Exp,
                                                      bias=soft[:, 0, q:q + 1], accum_out=soft[:, 1, q:q + 1])
                        op.then_inc(exp_done, 1)
                elif kind == "mul":
                    splits(step[-1], step[-1] + 1)
                elif kind == "evac":
                    _, _, what, j = step
                    n, end = strip_at[l, what, j], chunk_end[l, what, j]
                    bank = ps[:, 2 * (n % 2):2 * (n % 2) + 2, :]
                    free = strip_free[n % 2]
                    if what in ("wo", "pa", "pb"):
                        continue
                    act.wait_ge(chunk_used, end)
                    if what == "cq":
                        for t in range(TT):
                            own.link(nc.scalar.activation(sq[:, 0:QL], bank[:, t, 0:QL], ACT.Square,
                                                          accum_out=small[:, 4 + t:5 + t]))
                        op = copy(latents[:, 0:TT * QL].rearrange("p (t c) -> p t c", t=TT), bank[:, :, 0:QL])
                    elif what == "ckv":
                        for t in range(TT):
                            own.link(nc.scalar.activation(sq[:, 0:KVL], bank[:, t, 0:KVL], ACT.Square,
                                                          accum_out=small[:, 6 + t:7 + t]))
                            own.link(nc.scalar.activation(sq[:, 0:DR], bank[:, t, KVL:KVL + DR], ACT.Square,
                                                          accum_out=small[:, 12 + t:13 + t]))
                        copy(kr[:, :, :], bank[:, :, KVL:KVL + DR])
                        op = copy(latents[:, CKV0:CKV0 + TT * CKVW].rearrange("p (t c) -> p t c", t=TT),
                                  bank[:, :, 0:CKVW])
                    elif what in ("v", "u"):
                        m = 4 * l + (2 if what == "u" else 0) + j
                        if (what, j) == ("v", 0):
                            if l:
                                wait_strip_read(act, strip_at[l - 1, "pa", 1])
                        elif (what, j) == ("u", 1):
                            act.wait_ge(branch_a, 2 * l + 1)
                        else:
                            wait_strip_read(act, strip_at[(l, "v", 0) if what == "v" else (l, "v", 1)])
                        nc.scalar.activation(tmp[:], bank, ACT.Square).then_inc(gelu_sq, 1)
                        act.wait_ge(gelu_arg, m + 1)
                        nc.scalar.activation(tmp[:], tmp[:], ACT.Tanh, scale=GELU_A * GELU_C).then_inc(gelu_tanh, 1)
                        continue
                    elif what == "uq":
                        if j == 0:
                            act.wait_ge(turn_done, last_turn["latent_turns", l] + 1)
                        flat = qb[:].rearrange("p t h d -> p t (h d)")
                        op = copy(flat[:, :, j * STRIP:(j + 1) * STRIP], bank)
                    elif what == "ukv":
                        for t in range(TT):
                            heads = bank[:, t, :].rearrange("p (h c) -> p h c", h=HPS)
                            copy(kb[:, t, HPS * j:HPS * (j + 1), 0:DN], heads[:, :, 0:DN])
                            op = copy(vv[:, t, HPS * j:HPS * (j + 1), :], heads[:, :, DN:DN + DV])
                    elif what in ("ga", "gb"):
                        dst = tmp[:] if what == "ga" else gate_b[j]
                        if what == "ga" and j == 0:
                            act.wait_ge(branch_a, 2 * l + 2)
                        elif what == "ga":
                            wait_strip_read(act, strip_at[l, "pa", 0])
                        elif j:
                            act.wait_ge(turn_done, last_turn["mix_tokens", l] + 1)
                        op = nc.scalar.activation(dst, bank, ACT.Tanh, scale=0.5)
                    elif what == "gu":
                        if j:
                            wait_strip_read(act, n - 1)
                        op = nc.scalar.activation(sig[:], bank[:, :, 0:HC], ACT.Tanh, scale=0.5)
                        free = sig_done
                    op.then_inc(free, 1)
                elif kind == "down":
                    splits(step[2], step[3])

            act.wait_ge(wr_landed, 32)
            copy(wr_hi[:], wr[:]).then_inc(wr_hi_done, 1)
            copy(xn_hi[:], xn[:]).then_inc(xn_hi_done, 1)
            act.wait_ge(gap_ready, 1)
            nc.scalar.activation(rt[:, :, 1], rt[:, :, 0], ACT.Exp).then_inc(gap_exp, 1)

            def moe_pass(r, z):
                def turn_part(e, j):
                    act.wait_ge(z["hturn_done"], GUS * e + j + 1)
                    copy(hid_hi[:, 2 * j:2 * j + 2, 0:P], ps[:, 4 + j % 2, 0:2 * P].rearrange("p (k s) -> p k s", k=2)
                         ).then_inc(z["hturn_hi"], 1)

                def gather_part(e, half):
                    act.wait_ge(z["g_done"], 1 + half if e is None else g_done(e, 6 + half) + 1)
                    for k in range(4):
                        kk = 4 * half + k
                        op = copy(act_hi[:, kk, 0:P], ps[:, 6 + half, k * P:(k + 1) * P], ffn_g[:, L - 1, kk:kk + 1])
                    op.then_inc(z["g_hi"], 1)

                def split(e, c, last):
                    if c < PER_EXPERT:
                        r.split_hi(act, e, c, expert_size[c])
                    elif not last:
                        r.split_hi(act, e + 1, c - PER_EXPERT, expert_size[c - PER_EXPERT])

                def body(e, last):
                    first = is_first(e)
                    for j in range(GUS):
                        split(e, 2 * j + LEAD, last)
                        split(e, 2 * j + 1 + LEAD, last)
                        act.wait_ge(r.used, r.count(e, 2 * j + 2))
                        if j or not first:
                            q = j - 1 if j else GUS - 1
                            act.wait_ge(z[f"gu_free{q % 2}"], strips_read(e if j else e - 1, q) + 1)
                        nc.scalar.activation(sig[:, 0, :], ps[:, j % 2, 0:HC], ACT.Tanh, scale=0.5).then_inc(z["sig_ready"], 1)
                        if j >= 2:
                            turn_part(e, j - 2)
                        if j == 6:
                            act.wait_ge(z["g_done"], g_done(e, 4) + 1)
                            copy(put[:], ps[:, 6, 0:S]).then_inc(z["g_free0"], 1)
                            act.wait_ge(z["g_done"], g_done(e, 5) + 1)
                            copy(slot_w[:], ps[:, 7, 0:1]).then_inc(z["g_free1"], 1)
                    for d in range(len(DOWN_K)):
                        split(e, GU_CHUNKS + d + LEAD, last)
                        if d == 1:
                            turn_part(e, GUS - 2)
                        if d == 3:
                            turn_part(e, GUS - 1)
                        if not last and d in (5, 7):
                            gather_part(e, (d - 5) // 2)
                    act.wait_ge(r.used, r.count(e, PER_EXPERT))
                    act.wait_ge(z["g_free1"], g_read(e, 4) + 1)
                    copy(y_hi[:], ps[:, 2:4, :].rearrange("p a b -> p (a b)"), slot_w[:, 0:1]).then_inc(z["y_hi_done"], 1)

                gather_part(None, 0)
                gather_part(None, 1)
                body(0, False)
                with act.Fori(1, E - 1) as e:
                    body(e, False)
                body(E - 1, True)

            moe_pass(Ring(N0, raw_landed, hi_done, lo_done, chunk_used), pass_sems[0])
            act.wait_ge(counts_ready, 1)
            crowded = act.value_load(most[0:1, 0:1], min_val=0, max_val=S)
            with act.If(crowded > P):
                act.wait_ge(pass_sems[0]["over"], 1)
                r2 = Ring(0, raw_landed2, hi_done2, lo_done2, chunk_used2)
                for c in range(LEAD):
                    r2.split_hi(act, 0, c)
                moe_pass(r2, pass_sems[1])

        @block.vector
        def _(dve):
            own = Chain(dve, dve_own)
            link = own.link
            latents = qb[:].rearrange("p t h d -> p (t h d)")
            CKV0, CKVW = TT * QL, KVL + DR
            counts = {"split_turns": 0, "heads": 0}
            tt, ts, stt = nc.vector.tensor_tensor, nc.vector.tensor_scalar, nc.vector.scalar_tensor_tensor

            def splits(a, b):
                for n in range(a + LEAD, b + LEAD):
                    ring.split_lo(dve, 0, n, size[n] if n < N0 else CHUNK)

            def turn_lo_parts(b, hi, lo, k0, scale):
                counts["split_turns"] += 1
                dve.wait_ge(turn_hi, counts["split_turns"])
                for k in range(2):
                    op = stt(lo[:, k0 + k, :], ps[:, 4 + b % 2, k * S:(k + 1) * S], scale(k0 + k),
                             hi[:, k0 + k, :].bitcast(F32), ALU.mult, ALU.subtract)
                op.then_inc(turn_free[b % 2], 1)

            def root(dst, src, scale, eps, n, last=None):
                a, t_, yi = rs_a[:, 0:n], rs_t[:, 0:n], rs_y[:, 0:n]
                y = yi.bitcast(F32)
                link(ts(a, src, scale, eps, ALU.mult, ALU.add))
                link(ts(yi, a.bitcast(I32), 1, None, ALU.logical_shift_right))
                link(ts(yi, yi, -1.0, RSQRT_SEED, ALU.mult, ALU.add))
                for it in range(3):
                    link(tt(t_, y, y, ALU.mult))
                    link(stt(t_, t_, -0.5, a, ALU.mult, ALU.mult))
                    op = stt(dst if it == 2 else y, t_, 1.5, y, ALU.add, ALU.mult)
                    if it == 2 and last is not None:
                        op.then_inc(last, 1)
                        return
                    link(op)

            def rope(x1, x2, cos, sin, s1, s2, last=None):
                link(tt(s1, x2, sin, ALU.mult))
                link(tt(s2, x1, sin, ALU.mult))
                link(tt(x1, x1, cos, ALU.mult))
                link(tt(x1, x1, s1, ALU.subtract))
                link(tt(x2, x2, cos, ALU.mult))
                op = tt(x2, x2, s2, ALU.add)
                if last is None:
                    link(op)
                else:
                    op.then_inc(last, 1)

            def sum_squares(dst, w):
                counts["heads"] += 1
                dve.wait_ge(head_squares, counts["heads"])
                nc.vector.tensor_reduce(dst, sq[:, 0:8 * w].rearrange("p (h d) -> p h d", h=8), AX.X,
                                        ALU.add).then_inc(head_sums, 1)

            def over(v, n):
                return v.rearrange("p (m o) -> p m o", o=1).to_broadcast([P, v.shape[1], n])

            def each(v, m):
                return v.rearrange("p (o n) -> p o n", o=1).to_broadcast([P, m, v.shape[1]])

            dve.wait_ge(x_landed, 48)
            for i, step in enumerate(plan):
                kind, l, b0 = step[0], step[1], turn_at[i]
                if kind == "norm":
                    dst = xn if step[2] else vbuf
                    m = 2 * l + step[2]
                    dve.wait_ge(squares_done, 6 * l + (6 if step[2] else 2))
                    if step[2]:
                        link(tt(square_sum[:, 0, :], square_sum[:, 0, :], square_sum[:, 1, :], ALU.add))
                    root(small[:, 2:4], square_sum[:, 0, :], 1.0 / D, EPS, 2, root_done)
                    dve.wait_ge(root_done, m + 1)
                    for half in range(2):
                        cols = slice(half * STRIP, (half + 1) * STRIP)
                        ts(dst[:, 1, cols], xres[:, 1, cols], small[:, 3:4], None, ALU.mult).then_inc(normed1_done, 1)
                    if not m:
                        dve.wait_ge(gains_ready, 1)
                        ring.split_lo(dve, 0, 0, size[0])
                elif kind == "norm_turns":
                    g = ffn_g if step[2] else mix_g
                    for b in range(2):
                        turn_lo_parts(b0 + b, act_hi, act_lo, 4 * step[3] + 2 * b, lambda k: g[:, l, k:k + 1])
                    if (l, step[2], step[3]) == (0, 0, 0):
                        for n in range(1, LEAD):
                            ring.split_lo(dve, 0, n, size[n])
                elif kind == "latent_norm":
                    wait_strip_read(dve, strip_at[l, "cq", 0])
                    wait_strip_read(dve, strip_at[l, "ckv", 0])
                    link(ts(small[:, 4:6], small[:, 4:6], 1.0 / QL, None, ALU.mult))
                    link(ts(small[:, 6:8], small[:, 6:8], 1.0 / KVL, None, ALU.mult))
                    root(small[:, 8:12], small[:, 4:8], 1.0, EPS, 4)
                    for t in range(TT):
                        q, c = latents[:, t * QL:(t + 1) * QL], latents[:, CKV0 + t * CKVW:CKV0 + t * CKVW + KVL]
                        ts(q, q, small[:, 8 + t:9 + t], None, ALU.mult)
                        op = ts(c, c, small[:, 10 + t:11 + t], None, ALU.mult)
                    op.then_inc(latent_normed, 1)
                elif kind == "rotary_key":
                    for t in range(TT):
                        link(tt(kr[:, t, :], kr[:, t, :], k_gain[:, l, DN:DQ], ALU.mult))
                        rope(kr[:, t, 0:HR], kr[:, t, HR:DR], cos_sin[:, t, 0, :], cos_sin[:, t, 1, :],
                             rs_a[:, 0:HR], rs_t[:, 0:HR])
                elif kind == "latent_turns":
                    for b in range(2):
                        turn_lo_parts(b0 + b, t1_hi, t1_lo, 2 * b, lambda k: qlat_g[:, l, k:k + 1])
                    turn_lo_parts(b0 + 2, t1_hi, t1_lo, KQ, lambda k: kvlat_g[:, l, k - KQ:k - KQ + 1])
                elif kind == "layer_stats":
                    wait_strip_read(dve, strip_at[l, "v", 1])
                    for t in range(TT):
                        for hf in range(2):
                            op = nc.vector.bn_stats(stats[:, t, hf, :], vbuf[:, t, hf * 512:(hf + 1) * 512])
                    link(op)
                    for t in range(TT):
                        op = nc.vector.bn_aggr(mean_var[:, t, :], stats[:, t, :, :])
                    link(op)
                    root(small[:, 14:16], mean_var[:, :, 1], 1.0, 4 * EPS, 2)
                elif kind == "layer_norm":
                    t = step[2]
                    dve.wait_ge(ln_landed, 32 * (l + 1))
                    v = vbuf[:, t, :]
                    link(ts(v, v, mean_var[:, t, 0:1], small[:, 14 + t:15 + t], ALU.subtract, ALU.mult))
                    link(tt(v, v, ln_rows[:, 0, :], ALU.mult))
                    tt(v, v, ln_rows[:, 1, :], ALU.add).then_inc(v_normed, 1)
                elif kind == "mix_tokens":
                    for b in range(4):
                        bb = b0 + b
                        dve.wait_ge(turn_done, bb + 1)
                        for g in range(2):
                            gg = 2 * b + g
                            op = ts(vbuf[:, :, gg * P:(gg + 1) * P],
                                    ps[:, 4 + bb % 2, g * S:(g + 1) * S].rearrange("p (t d) -> p t d", t=TT),
                                    b_sp[:, l, gg:gg + 1], 0.5, ALU.add, ALU.mult)
                        op.then_inc(turn_free[bb % 2], 1)
                elif kind == "a_turns":
                    for b in range(2):
                        bb = b0 + b
                        turn_lo_parts(bb, t1_hi, t1_lo, 4 * step[2] + 2 * b, lambda k: 1.0)
                elif kind == "merged_turns":
                    for b in range(2):
                        turn_lo_parts(b0 + b, act_hi, act_lo, 4 * step[2] + 2 * b, lambda k: 0.5)
                elif kind == "hidden_turn":
                    turn_lo_parts(b0, hid_hi, hid_lo, 2 * step[2], lambda k: 1.0)
                elif kind == "q_norm":
                    t = step[2]
                    if not l and not t:
                        dve.wait_ge(small_landed, 16 * 4 * L)
                        nc.vector.memset(qk_gain[DN:DQ, :], 1.0)
                        tt(qk_gain[0:DN, :], gain_q[0:DN, :], gain_k[0:DN, :], ALU.mult).then_inc(qk_gain_ready, 1)
                    for hf in range(2):
                        sum_squares(q_sum[:, t, 8 * hf:8 * hf + 8], DQ)
                    dve.wait_ge(head_sums, counts["heads"])
                    root(q_sum[:, t, :], q_sum[:, t, :], 1.0, DQ * EPS, H)
                    q = qb[:, t, :, :]
                    link(tt(q[:, :, DN:DQ], q[:, :, DN:DQ], each(q_gain[:, l, DN:DQ], H), ALU.mult))
                    s1, s2 = (prob[:, c:c + H * HR].rearrange("p (h r) -> p h r", h=H) for c in (0, H * HR))
                    rope(q[:, :, DN:DN + HR], q[:, :, DN + HR:DQ], each(cos_sin[:, t, 0, :], H),
                         each(cos_sin[:, t, 1, :], H), s1, s2, q_ready)
                elif kind == "branch":
                    j = step[2]
                    cols = slice(j * STRIP, (j + 1) * STRIP)
                    wait_strip_read(dve, strip_at[l, "u", j])
                    wait_turn_read(dve, last_turn["mix_tokens", l])
                    wait_turn_read(dve, last_turn["mix_tokens", l] - 1)
                    tt(vbuf[:, :, cols], tmp[:], vbuf[:, :, cols], ALU.mult).then_inc(branch_a, 1)
                elif kind == "k_norm":
                    t = step[2]
                    for hf in range(2):
                        sum_squares(k_sum[:, t, 8 * hf:8 * hf + 8], DN)
                    dve.wait_ge(head_sums, counts["heads"])
                    link(ts(k_sum[:, t, :], k_sum[:, t, :], small[:, 12 + t:13 + t], None, ALU.add))
                    root(k_sum[:, t, :], k_sum[:, t, :], 1.0 / DQ, EPS, H)
                    k = kb[:, t, :, 0:DN]
                    tt(k, k, over(k_sum[:, t, :], DN), ALU.mult)
                    tt(kb[:, t, :, DN:DQ], each(kr[:, t, :], H), over(k_sum[:, t, :], DR), ALU.mult).then_inc(k_ready, 1)
                elif kind == "attention":
                    s, b = step[2], b0
                    if s >= 3:
                        counts["split_turns"] += 1
                        dve.wait_ge(turn_hi, counts["split_turns"])
                        tt(bt_lo[:, s - 3, :], ps[:, 4 + b % 2, 0:S], bt_hi[:, s - 3, :].bitcast(F32),
                           ALU.subtract).then_inc(turn_free[b % 2], 1)
                        b += 1
                    if 1 <= s < PAIRS + 1:
                        n = PAIRS * l + s - 1
                        pr = probs[(s - 1) % 2]
                        p0 = pr[:, 0:2 * P].rearrange("p (h k) -> p h k", h=2)
                        p1 = pr[:, 2 * P:2 * P + 2 * S].rearrange("p (h k) -> p h k", h=2)
                        if s >= 3:
                            dve.wait_ge(turn_done, prob_turn[l, s - 3] + 2)
                        else:
                            dve.wait_ge(q_ready, TT * (l + 1))
                        dve.wait_ge(scores_done, n + 1)
                        for t, pt, w in ((0, p0, P), (1, p1, S)):
                            for hh in range(2):
                                h = 2 * (s - 1) + hh
                                op = stt(pt[:, hh, :], ps[:, 6 + t, hh * w:(hh + 1) * w], q_sum[:, t, h:h + 1],
                                         bias_mask[:, P:2 * P] if t == 0 else bias_mask[:, 0:S], ALU.mult, ALU.add)
                        op.then_inc(scores_read, 1)
                        dve.wait_ge(scores_read, n + 1)
                        nc.vector.tensor_reduce(soft[:, 2, 0:2], p0, AX.X, ALU.max)
                        link(nc.vector.tensor_reduce(soft[:, 2, 2:4], p1, AX.X, ALU.max))
                        ts(soft[:, 0, :], soft[:, 2, :], -1.0, None, ALU.mult).then_inc(max_ready, 1)
                        dve.wait_ge(exp_done, n + 1)
                        link(nc.vector.reciprocal(soft[:, 2, :], soft[:, 1, :]))
                        tt(p0, p0, over(soft[:, 2, 0:2], P), ALU.mult)
                        tt(p1, p1, over(soft[:, 2, 2:4], S), ALU.mult).then_inc(prob_ready, 1)
                elif kind == "mul":
                    splits(step[-1], step[-1] + 1)
                elif kind == "evac":
                    _, _, what, j = step
                    n, end = strip_at[l, what, j], chunk_end[l, what, j]
                    bank = ps[:, 2 * (n % 2):2 * (n % 2) + 2, :]
                    free = strip_free[n % 2]
                    cols = slice(j * STRIP, (j + 1) * STRIP)
                    if what in ("v", "u"):
                        m = 4 * l + (2 if what == "u" else 0) + j
                        dve.wait_ge(gelu_sq, m + 1)
                        stt(tmp[:], tmp[:], 1.0 / GELU_A, bank, ALU.add, ALU.mult).then_inc(gelu_arg, 1)
                        dve.wait_ge(gelu_tanh, m + 1)
                        if what == "v":
                            stt(vbuf[:, :, cols], tmp[:], 1.0, bank, ALU.add, ALU.mult).then_inc(free, 1)
                        else:
                            stt(tmp[:], tmp[:], 1.0, bank, ALU.add, ALU.mult).then_inc(free, 1)
                    elif what in ("pa", "pb"):
                        wait_strip_read(dve, strip_at[l, "g" + what[1], j])
                        dve.wait_ge(chunk_used, end)
                        if what == "pa":
                            stt(vbuf[:, :, cols], tmp[:], 1.0, bank, ALU.add, ALU.mult).then_inc(free, 1)
                        else:
                            stt(gate_b[j], gate_b[j], 1.0, bank, ALU.add, ALU.mult).then_inc(free, 1)
                            wait_strip_read(dve, n)
                            wait_strip_read(dve, strip_at[l, "pa", j])
                            tt(vbuf[:, :, cols], vbuf[:, :, cols], gate_b[j], ALU.add).then_inc(merged_b, 1)
                    elif what == "wo":
                        dve.wait_ge(chunk_used, end)
                        tt(xres[:, :, cols], xres[:, :, cols], bank, ALU.add).then_inc(free, 1)
                    elif what == "gu":
                        dve.wait_ge(sig_done, j + 1)
                        if j >= 2:
                            dve.wait_ge(turn_done, last_turn["hidden_turn", l, j - 2] + 1)
                        link(stt(sig[:], sig[:], 1.0, bank[:, :, 0:HC], ALU.add, ALU.mult))
                        stt(hid[:, j % 2, :, :], sig[:], 0.5, bank[:, :, HC:2 * HC], ALU.mult, ALU.mult).then_inc(free, 1)
                elif kind == "down":
                    a, b, n = step[2:5]
                    splits(a, b)
                    dve.wait_ge(chunk_used, b)
                    for t in range(TT):
                        at = (2 * n + 2 * t) % 4
                        tt(xres[:, t, :], xres[:, t, :], ps[:, at:at + 2, :].rearrange("p a b -> p (a b)"),
                           ALU.add).then_inc(strip_free[(n + t) % 2], 1)

            dve.wait_ge(wr_hi_done, 1)
            tt(wr_lo[:], wr[:], wr_hi[:].bitcast(F32), ALU.subtract).then_inc(wr_lo_done, 1)
            dve.wait_ge(xn_hi_done, 1)
            tt(xn_lo[:], xn[:], xn_hi[:].bitcast(F32), ALU.subtract).then_inc(xn_lo_done, 1)
            dve.wait_ge(logits_done, 1)
            link(tt(logit[:], ps[:, 4, 0:TT * E].rearrange("p (t e) -> p t e", t=TT), each(br[:], TT), ALU.add))
            for t in range(TT):
                link(nc.vector.max(top[:, t, :], logit[:, t, :]))
                link(nc.vector.max_index(top_i[:, t, :], top[:, t, :], logit[:, t, :]))
                link(nc.vector.tensor_copy(top_f[:, t, :], top_i[:, t, :]))
                ts(one_a[:, t, :], iota[:, 0:E], top_f[:, t, 0:1], None, ALU.is_equal)
                link(ts(one_b[:, t, :], iota[:, 0:E], top_f[:, t, 1:2], None, ALU.is_equal))
            tt(chosen[:], one_a[:], one_b[:], ALU.add).then_inc(chosen_ready, 1)
            dve.wait_ge(chosen_ready, 1)
            tt(rt[:, :, 0], top[:, :, 1], top[:, :, 0], ALU.subtract).then_inc(gap_ready, 1)
            dve.wait_ge(gap_exp, 1)
            link(ts(rt[:, :, 2], rt[:, :, 1], 1.0, None, ALU.add))
            link(nc.vector.reciprocal(rt[:, :, 3], rt[:, :, 2]))
            link(tt(rt[:, :, 2], rt[:, :, 1], rt[:, :, 3], ALU.mult))
            for t in range(TT):
                link(ts(combine[:, t, :], one_a[:, t, :], rt[:, t, 3:4], None, ALU.mult))
                link(stt(combine[:, t, :], one_b[:, t, :], rt[:, t, 2:3], combine[:, t, :], ALU.mult, ALU.add))
            dve.wait_ge(places_done, 1)
            link(ts(place[:], chosen[:], -4.0 * S, 4.0 * S, ALU.mult, ALU.add))
            link(tt(place[:], place[:], ps[:, 5, 0:TT * E].rearrange("p (t e) -> p t e", t=TT), ALU.add))
            link(nc.vector.tensor_reduce(most_f[:, 0:1], ps[:, 5, TT * E:(TT + 1) * E], AX.X, ALU.max))
            nc.vector.tensor_copy(most[:, 0:1], most_f[:, 0:1]).then_inc(counts_ready, 1)

            def moe_pass(r, z):
                def turn_part(e, j):
                    dve.wait_ge(z["hturn_hi"], GUS * e + j + 1)
                    tt(hid_lo[:, 2 * j:2 * j + 2, 0:P], ps[:, 4 + j % 2, 0:2 * P].rearrange("p (k s) -> p k s", k=2),
                       hid_hi[:, 2 * j:2 * j + 2, 0:P].bitcast(F32), ALU.subtract).then_inc(z[f"hturn_free{j % 2}"], 1)

                def gather_part(e, half):
                    dve.wait_ge(z["g_hi"], 1 + half if e is None else 2 * e + 3 + half)
                    for k in range(4):
                        kk = 4 * half + k
                        op = stt(act_lo[:, kk, 0:P], ps[:, 6 + half, k * P:(k + 1) * P], ffn_g[:, L - 1, kk:kk + 1],
                                 act_hi[:, kk, 0:P].bitcast(F32), ALU.mult, ALU.subtract)
                    op.then_inc(z[f"g_free{half}"], 1)

                def scattered(e, t, missing=0):
                    for hf in range(2):
                        dve.wait_ge(z["g_done"], g_done(e, 2 * t + hf) + 1 - missing)
                        xs = xres[:, t, hf * 512:(hf + 1) * 512]
                        op = tt(xs, xs, ps[:, 6 + hf, :], ALU.add)
                        if missing and t and hf:
                            op.then_inc(z["over"], 1)
                        else:
                            op.then_inc(z[f"g_free{hf}"], 1)

                def pick_tokens(e):
                    for t in range(TT):
                        at = place[:, t, e:e + 1] if isinstance(e, int) else place[:, t, bass.ds(e, 1)]
                        w = combine[:, t, e:e + 1] if isinstance(e, int) else combine[:, t, bass.ds(e, 1)]
                        ts(pick[:, t, :], iota, at, None, ALU.is_equal)
                        op = ts(pick_w[:, t:t + 1], w, 0.0, None, ALU.add)
                    op.then_inc(z["picked"], 1)

                def split(e, c, last):
                    if c < PER_EXPERT:
                        r.split_lo(dve, e, c, expert_size[c])
                    elif not last:
                        r.split_lo(dve, e + 1, c - PER_EXPERT, expert_size[c - PER_EXPERT])

                def body(e, last):
                    first = is_first(e)
                    for j in range(GUS):
                        if not first and j in (2, 4):
                            scattered(e, j // 2 - 1)
                        split(e, 2 * j + LEAD, last)
                        split(e, 2 * j + 1 + LEAD, last)
                        dve.wait_ge(z["sig_ready"], GUS * e + j + 1)
                        if j >= 2:
                            dve.wait_ge(z["hturn_done"], GUS * e + j - 1)
                        stt(sig[:, 0, :], sig[:, 0, :], 1.0, ps[:, j % 2, 0:HC], ALU.add, ALU.mult).then_inc(z["sig_half"], 1)
                        dve.wait_ge(z["sig_half"], GUS * e + j + 1)
                        stt(hid[:, j % 2, 0, :], sig[:, 0, :], 0.5, ps[:, j % 2, HC:2 * HC], ALU.mult,
                            ALU.mult).then_inc(z[f"gu_free{j % 2}"], 1)
                        if j >= 2:
                            turn_part(e, j - 2)
                        if not last and j == 8:
                            dve.wait_ge(z["g_done"], g_done(e, 5) + 1)
                            pick_tokens(e + 1)
                    for d in range(len(DOWN_K)):
                        split(e, GU_CHUNKS + d + LEAD, last)
                        if d == 1:
                            turn_part(e, GUS - 2)
                        if d == 3:
                            turn_part(e, GUS - 1)
                        if not last and d in (5, 7):
                            gather_part(e, (d - 5) // 2)
                    dve.wait_ge(z["y_hi_done"], e + 1)
                    stt(y_lo[:], ps[:, 2:4, :].rearrange("p a b -> p (a b)"), slot_w[:, 0:1], y_hi[:].bitcast(F32),
                        ALU.mult, ALU.subtract).then_inc(z["y_split"], 1)

                pick_tokens(0)
                gather_part(None, 0)
                gather_part(None, 1)
                body(0, False)
                with dve.Fori(1, E - 1) as e:
                    body(e, False)
                body(E - 1, True)
                scattered(E, 0, 2)
                scattered(E, 1, 2)

            moe_pass(Ring(N0, raw_landed, hi_done, lo_done, chunk_used), pass_sems[0])
            dve.wait_ge(counts_ready, 1)
            crowded = dve.value_load(most[0:1, 0:1], min_val=0, max_val=S)
            with dve.If(crowded > P):
                dve.wait_ge(pass_sems[0]["over"], 1)
                link(ts(place[:], place[:], -float(P), None, ALU.add))
                r2 = Ring(0, raw_landed2, hi_done2, lo_done2, chunk_used2)
                for c in range(LEAD):
                    r2.split_lo(dve, 0, c)
                moe_pass(r2, pass_sems[1])


def shape_tables(S, DR, theta):
    import numpy as np
    i = np.arange(P)
    eye = np.eye(P)
    before = (i[:, None] < i[None, :])
    ones = np.ones((P, P))
    iota = np.broadcast_to(i, (P, P))
    mask = np.concatenate([np.zeros((P, P)), np.where(i[None, :] <= i[:, None], 0.0, NEG)], 1)
    pos = np.arange(S, dtype=np.float32)
    inv = np.float32(theta) ** (-np.arange(0, DR, 2, dtype=np.float32) / np.float32(DR))
    ang = pos[:, None] * inv[None, :]
    cs = np.stack([np.cos(ang), np.sin(ang)], 1).reshape(S // P, P, DR).transpose(1, 0, 2).reshape(P, -1)
    return np.ascontiguousarray(np.concatenate([eye, before, ones, iota, mask, cs], 1).astype(np.float32))


_INS = ["x", "mix_norm_g", "w_in", "gm_v_norm_g", "gm_v_norm_b", "gm_w_spatial", "gm_b_spatial", "gm_w_proj",
        "mla_q_lat_g", "mla_w_uq", "mla_kv_lat_g", "mla_w_ukv", "mla_q_norm_g", "mla_k_norm_g", "mla_w_proj",
        "w_out", "ffn_norm_g", "dense_w_gu", "dense_w_down", "moe_w_router", "moe_b_router", "moe_w_gu",
        "moe_w_down"]


def kernel(**inputs):
    import numpy as np
    import concourse.bacc as bacc
    from concourse.bass_utils import run_bass_kernel_spmd

    nc = bacc.Bacc("TRN2", target_bir_lowering=False, num_devices=1)
    arrays, args = {}, []
    for name in _INS:
        a = np.ascontiguousarray(inputs[name])
        arrays[f"in_{name}"] = a
        args.append(nc.dram_tensor(f"in_{name}", a.shape, mybir.dt.from_np(a.dtype), kind="ExternalInput").ap())
    tables = shape_tables(256, 32, 10000.0)
    arrays["shape_consts"] = tables
    args.append(nc.dram_tensor("shape_consts", tables.shape, F32, kind="ExternalInput").ap())
    args.append(nc.dram_tensor("out", (1, 256, 1024), F32, kind="ExternalOutput").ap())
    decoder_trunk(nc, *args)
    r = run_bass_kernel_spmd(nc, [arrays], core_ids=[0])
    return r.results[0]["out"]
```

```python
from contextlib import ExitStack

import concourse.bass as bass
from concourse import mybir

F32 = mybir.dt.float32
F32R = mybir.dt.float32r
I32 = mybir.dt.int32
U32 = mybir.dt.uint32
ALU = mybir.AluOpType
ACT = mybir.ActivationFunctionType
AX = mybir.AxisListType

P = 128
EPS = 1e-6
RAW, RAW_MOE, SPLIT, LEAD = 4, 6, 3, 3
CHUNK = 2048
STRIP = 512
GELU_A = 0.044715
GELU_C = 0.7978845608028654
RSQRT_SEED = float(0x5F3759DF)
NEG = -1e30


class Chain:

    def __init__(self, eng, sem, base=0):
        self.eng, self.sem, self.base, self.n = eng, sem, base, 0

    def link(self, ins):
        self.n += 1
        ins.then_inc(self.sem, 1)
        self.eng.wait_ge(self.sem, self.base + self.n)


def decoder_trunk(nc, x, mix_norm_g, w_in, gm_v_norm_g, gm_v_norm_b, gm_w_spatial, gm_b_spatial, gm_w_proj,
                  mla_q_lat_g, mla_w_uq, mla_kv_lat_g, mla_w_ukv, mla_q_norm_g, mla_k_norm_g, mla_w_proj,
                  w_out, ffn_norm_g, dense_w_gu, dense_w_down, moe_w_router, moe_b_router, moe_w_gu,
                  moe_w_down, shape_consts, out):
    _, S, D = x.shape
    L = w_in.shape[0]
    TT = S // P
    KD = D // P
    NG = gm_w_spatial.shape[1]
    QL, KVL = mla_w_uq.shape[1], mla_w_ukv.shape[1]
    DQ = mla_q_norm_g.shape[1]
    H = mla_w_uq.shape[2] // DQ
    DV = mla_w_proj.shape[1] // H
    DN = mla_w_ukv.shape[2] // H - DV
    DR = DQ - DN
    HR = DR // 2
    E = moe_w_gu.shape[1]
    FF = moe_w_down.shape[2]
    KF = FF // P
    assert TT == 2 and D == 1024 and dense_w_down.shape[1] == FF and H * DV == D and 2 * DV == P
    OFF_V, OFF_CQ = D, 2 * D
    OFF_CKV = OFF_CQ + QL
    OFF_GATE = OFF_CKV + KVL + DR
    SCALE = float(DQ) ** -0.5
    KQ, KKV = QL // P, KVL // P
    HC = 256
    GUS = FF // HC
    PAIRS = H // 2
    HPS = STRIP // (DN + DV)
    UQS, UKVS = H * DQ // STRIP, H // HPS

    chunks = []

    DOWN_K = [2, 1] * 6 + [2, 2]
    assert sum(DOWN_K) == KF
    LAST_TURN = 2
    GU_CHUNKS = GUS * KD // 4
    PER_EXPERT = GU_CHUNKS + len(DOWN_K)

    def gu_pieces(w_gu, j, k0):
        v = w_gu.rearrange("(k p) n -> p k n", p=P)
        return [v[:, k0:k0 + 4, hh * FF + j * HC:hh * FF + (j + 1) * HC] for hh in range(2)]

    def down_pieces(w_down, d):
        k0, n = sum(DOWN_K[:d]), DOWN_K[d]
        v = w_down.rearrange("(k p) n -> p k n", p=P)
        if n == 2:
            return [v[:, k0, :], v[:, k0 + 1, :]]
        return [v[:, k0, 0:D // 2], v[:, k0, D // 2:D]]

    plan = []
    strip_no = 0
    strip_at, chunk_end = {}, {}

    def mul(l, what, j, k0=0, then=(), split=True):
        nonlocal strip_no
        w, c0 = {"cq": (w_in, OFF_CQ), "ckv": (w_in, OFF_CKV), "v": (w_in, OFF_V), "u": (w_in, 0),
                 "ga": (w_in, OFF_GATE), "gb": (w_in, OFF_GATE + D), "uq": (mla_w_uq, 0), "ukv": (mla_w_ukv, 0),
                 "pa": (gm_w_proj, 0), "pb": (mla_w_proj, 0), "wo": (w_out, 0), "gu": (None, 0)}[what]
        width = KVL + DR if what == "ckv" else STRIP
        if not k0:
            strip_at[l, what, j] = strip_no
            strip_no += 1
        if what == "gu":
            kt, n = KD, 4
            chunks.append((("gu", *gu_pieces(dense_w_gu[l // 2], j, k0)), n, width))
        else:
            v = w[l].rearrange("(k p) n -> p k n", p=P)[:, :, c0 + j * STRIP:c0 + j * STRIP + width]
            kt = v.shape[1]
            n = min(4, kt - k0)
            h = n // 2
            chunks.append(([(0, h, v[:, k0:k0 + h, :]), (h * width, n - h, v[:, k0 + h:k0 + n, :])], n, width))
        chunk_end[l, what, j] = len(chunks)
        plan.append(("mul", l, what, j, k0, n, k0 + n == kt, width, len(chunks) - 1))
        plan.extend(then)
        if split:
            plan.append(("split", l, len(chunks) - 1))

    for l in range(L):
        def evac(what, j=0):
            return "evac", l, what, j

        def slot(n):
            return "attention", l, n

        plan.append(("norm", l, 0, len(chunks) - 1))
        plan.append(("norm_turns", l, 0, 0))
        plan.append(("norm_turns", l, 0, 1))
        mul(l, "cq", 0)
        mul(l, "cq", 0, 4, [evac("cq")])
        mul(l, "ckv", 0)
        mul(l, "ckv", 0, 4, [evac("ckv"), ("latent_norm", l)])
        mul(l, "v", 0, 0, [("spatial_weights", l), ("latent_turns", l)])
        mul(l, "v", 0, 4, [evac("v", 0)])
        mul(l, "uq", 0, 0, [evac("uq", 0)])
        plan.append(("rotary_key", l))
        for j in range(1, UQS):
            mul(l, "uq", j, 0, [evac("uq", j)])
        for j in range(UKVS // 2):
            mul(l, "ukv", j, 0, [evac("ukv", j)])
        plan.append(("head_sums", l, "q"))
        mul(l, "gb", 0)
        plan.append(("q_rope", l))
        mul(l, "gb", 0, 4, [evac("gb", 0)])
        for j in range(UKVS // 2, UKVS):
            mul(l, "ukv", j, 0, [evac("ukv", j)])
        plan.append(("head_sums", l, "k"))
        mul(l, "v", 1)
        plan.append(("k_scale", l))
        mul(l, "v", 1, 4, [evac("v", 1)])
        mul(l, "ga", 0, 0, [slot(0)])
        plan.append(("layer_stats", l))
        mul(l, "ga", 0, 4, [evac("ga", 0)])
        mul(l, "u", 0, 0, [slot(1)])
        plan.append(("layer_norm", l, 0))
        mul(l, "u", 0, 4, [evac("u", 0)])
        plan.append(("layer_norm", l, 1))
        mul(l, "u", 1, 0, [slot(2)])
        mul(l, "u", 1, 4, [("mix_tokens", l), ("branch", l, 0), evac("u", 1)])
        plan.append(("branch", l, 1))
        mul(l, "gb", 1, 0, [slot(3)])
        mul(l, "gb", 1, 4, [("a_turns", l, 0), ("a_turns", l, 1), slot(4), evac("gb", 1)])
        mul(l, "pa", 0, 0, [slot(5)])
        mul(l, "pa", 0, 4, [slot(6), evac("pa", 0)])
        mul(l, "ga", 1, 0, [slot(7)])
        mul(l, "ga", 1, 4, [slot(8), evac("ga", 1)])
        mul(l, "pa", 1, 0, [slot(9)])
        mul(l, "pa", 1, 4, [evac("pa", 1)])
        mul(l, "pb", 0, 0, [slot(10)])
        mul(l, "pb", 0, 4, [evac("pb", 0)])
        mul(l, "pb", 1, 0, [("merged_turns", l, 0)])
        mul(l, "pb", 1, 4, [evac("pb", 1)])
        mul(l, "wo", 0, 0, [("merged_turns", l, 1)] + [("router", l)] * (l % 2))
        mul(l, "wo", 1)
        mul(l, "wo", 0, 4, [evac("wo", 0), ("squares", l, 0)])
        mul(l, "wo", 1, 4, [evac("wo", 1), ("norm_turns", l, 1, 0), ("squares", l, 1), ("norm_turns", l, 1, 1),
                            ("norm", l, 1, len(chunks))], split=False)
        if l % 2 == 0:
            for j in range(GUS):
                mul(l, "gu", j)
                after = [evac("gu", j)] + [("hidden_turn", l, j - 1)] * (j >= 1)
                if j < GUS - 1:
                    mul(l, "gu", j, 4)
                    plan += after
                else:
                    mul(l, "gu", j, 4, after)
            a = len(chunks)
            for d in range(len(DOWN_K)):
                chunks.append((("down", *down_pieces(dense_w_down[l // 2], d)), DOWN_K[d], D))
            plan.append(("down", l, a, len(chunks), strip_no))
            strip_at[l, "down", 0] = strip_no
            strip_no += 2
    assert PAIRS + 3 == 11
    N0 = len(chunks)
    assert N0 % SPLIT == 0 and PER_EXPERT % SPLIT == 0 and PER_EXPERT % RAW_MOE == 0

    with ExitStack() as ctx:
        def sb(name, shape, dt=F32, c=ctx):
            return c.enter_context(nc.sbuf_tensor(name, shape, dt))

        def sem(name):
            return ctx.enter_context(nc.semaphore(name))

        ps = ctx.enter_context(nc.psum_tensor("ps", [P, 8, 512], F32))

        raw = sb("raw", [P, RAW, CHUNK])
        w_hi = sb("w_hi", [P, SPLIT, CHUNK], F32R)
        w_lo = sb("w_lo", [P, SPLIT, CHUNK], F32R)
        act_hi = sb("act_hi", [P, KD, S], F32R)
        act_lo = sb("act_lo", [P, KD, S], F32R)
        xres = sb("xres", [P, TT, D])
        CW = shape_consts.shape[1] - 2 * P
        consts = sb("consts", [P, CW])
        o = 0

        def part(n):
            nonlocal o
            o += n
            return consts[:, o - n:o]

        ident, before, ones, iota, cos_sin = (part(n) for n in (P, P, P, P, TT * 2 * HR))
        cos_sin = cos_sin.rearrange("p (t c r) -> p t c r", t=TT, c=2)
        assert o == CW
        row_sizes = [L * KD, L * KD, L * KQ, L * KKV, L * NG]
        ROWS = sum(row_sizes)
        cols_t = sb("cols_t", [P, ROWS])
        row_at = [sum(row_sizes[:i]) for i in range(5)]
        mix_g, ffn_g, qlat_g, kvlat_g, b_sp = (
            cols_t[:, a:a + n].rearrange("p (l k) -> p l k", l=L) for a, n in zip(row_at, row_sizes))
        q_gain = sb("q_gain", [P, L, DQ])
        k_gain = sb("k_gain", [P, L, DQ])
        qk_gain = sb("qk_gain", [P, L])
        gain_q = sb("gain_q", [P, L])
        gain_k = sb("gain_k", [P, L])
        square_sum = sb("square_sum", [P, 2, TT])
        ident_r = sb("ident_r", [P, P], F32R)
        causal_r = sb("causal_r", [P, 2 * P], F32R)
        ffn_scale = sb("ffn_scale", [P, 2 * TT])
        small = sb("small", [P, 16])
        rs_a = sb("rs_a", [P, TT * H])
        rs_t = sb("rs_t", [P, TT * H])
        rs_y = sb("rs_y", [P, TT * H], I32)

        mixer = ExitStack()
        ln_memory = ExitStack()
        ln_rows = sb("ln_rows", [P, 2, D], F32, ln_memory)
        u_buf = sb("u_buf", [P, 2, TT, STRIP], F32, ln_memory)
        ln_memory.close()
        t1_hi = sb("t1_hi", [P, KD, S], F32R, mixer)
        t1_lo = sb("t1_lo", [P, KD, S], F32R, mixer)
        bt_hi = sb("bt_hi", [P, KD, S], F32R, mixer)
        bt_lo = sb("bt_lo", [P, KD, S], F32R, mixer)
        vbuf = sb("vbuf", [P, TT, D], F32, mixer)
        tmp = sb("tmp", [P, TT, STRIP], F32, mixer)
        qb = sb("qb", [P, TT, H, DQ], F32, mixer)
        kb = sb("kb", [P, TT, H, DQ], F32, mixer)
        vv = sb("vv", [P, TT, H, DV], F32, mixer)
        ws_t = sb("ws_t", [P, NG, P], F32, mixer)
        qk_t = sb("qk_t", [P, 2, 512], F32, mixer)
        prob = sb("prob", [P, 768], F32, mixer)
        prob_t = sb("prob_t", [P, 768], F32, mixer)
        kr = sb("kr", [P, TT, DR], F32, mixer)
        soft = sb("soft", [P, 3, 4], F32, mixer)
        ws_raw = sb("ws_raw", [P, NG, P], F32, mixer)
        sq = sb("sq", [P, 768], F32, mixer)
        q_sum = sb("q_sum", [P, TT, H], F32, mixer)
        k_sum = sb("k_sum", [P, TT, H], F32, mixer)
        stats = sb("stats", [P, TT, 2, 6], F32, mixer)
        mean_var = sb("mean_var", [P, TT, 2], F32, mixer)
        mixer.close()
        causal, rows = tmp[:, 0, 0:2 * P], tmp[0:ROWS, 1, 0:P]
        gate_b = [ws_raw[:].rearrange("p g t -> p (g t)").rearrange("p (t n) -> p t n", t=TT),
                  ws_t[:].rearrange("p g t -> p (g t)").rearrange("p (t n) -> p t n", t=TT)]
        probs = [prob, sq]
        square_of = [sq, prob]
        ffn = ExitStack()
        experts = ExitStack()
        ehid_hi = sb("ehid_hi", [P, KF, P], F32R, experts)
        ehid_lo = sb("ehid_lo", [P, KF, P], F32R, experts)
        raw_more = sb("raw_more", [P, RAW_MOE - RAW, CHUNK], F32, experts)
        experts.close()
        hid_hi = sb("hid_hi", [P, KF, S], F32R, ffn)
        hid_lo = sb("hid_lo", [P, KF, S], F32R, ffn)
        xn = sb("xn", [P, TT, D], F32, ffn)
        xn_hi = sb("xn_hi", [P, TT, D], F32R, ffn)
        xn_lo = sb("xn_lo", [P, TT, D], F32R, ffn)
        hid = sb("hid", [P, 2, TT, HC], F32, ffn)
        sig = sb("sig", [P, TT, HC], F32, ffn)
        y_hi = sb("y_hi", [P, D], F32R, ffn)
        y_lo = sb("y_lo", [P, D], F32R, ffn)
        pick = sb("pick", [P, TT, P], F32R, ffn)
        pick_w = sb("pick_w", [P, TT], F32, ffn)
        put = sb("put", [P, S], F32R, ffn)
        slot_w = sb("slot_w", [P, 1], F32, ffn)
        wr = sb("wr", [P, KD, E], F32, ffn)
        wr_hi = sb("wr_hi", [P, KD, E], F32R, ffn)
        wr_lo = sb("wr_lo", [P, KD, E], F32R, ffn)
        br = sb("br", [P, E], F32, ffn)
        logit_t = sb("logit_t", [E, S], F32, ffn)
        logit = sb("logit", [P, TT, E], F32, ffn)
        top = sb("top", [P, TT, 8], F32, ffn)
        top_i = sb("top_i", [P, TT, 8], U32, ffn)
        top_f = sb("top_f", [P, TT, 8], F32, ffn)
        one_a = sb("one_a", [P, TT, E], F32, ffn)
        one_b = sb("one_b", [P, TT, E], F32, ffn)
        chosen = sb("chosen", [P, TT, E], F32, ffn)
        combine = sb("combine", [P, TT, E], F32, ffn)
        place = sb("place", [P, TT, E], F32, ffn)
        rt = sb("rt", [P, TT, 4], F32, ffn)
        most = sb("most", [P, 2], I32, ffn)
        most_f = sb("most_f", [P, 2], F32, ffn)
        ffn.close()

        raw_landed = [sem(f"raw_landed{i}") for i in range(RAW)]
        raw_landed_moe = [sem(f"raw_landed_moe{i}") for i in range(RAW_MOE)]
        raw_landed2 = [sem(f"raw_landed2_{i}") for i in range(RAW_MOE)]
        hi_done, lo_done, chunk_used = sem("hi_done"), sem("lo_done"), sem("chunk_used")
        hi_done2, lo_done2, chunk_used2 = sem("hi_done2"), sem("lo_done2"), sem("chunk_used2")
        x_landed, small_landed, out_stored = sem("x_landed"), sem("small_landed"), sem("out_stored")
        x_added = sem("x_added")
        consts_landed, mask_ready = sem("consts_landed"), sem("mask_ready")
        rows_landed, rows_turned, gains_ready = sem("rows_landed"), sem("rows_turned"), sem("gains_ready")
        ws_landed, ln_landed, wr_landed, qk_gain_ready = sem("ws_landed"), sem("ln_landed"), sem("wr_landed"), sem("qk_gain_ready")
        strip_free = [sem("strip_free0"), sem("strip_free1")]
        turn_done, turn_hi = sem("turn_done"), sem("turn_hi")
        turn_free = [sem("turn_free0"), sem("turn_free1")]
        act_own, dve_own = sem("act_own"), sem("dve_own")
        squares_done, root_done = sem("squares_done"), sem("root_done")
        normed0_done, normed1_done = sem("normed0_done"), sem("normed1_done")
        latent_normed = sem("latent_normed")
        gelu_sq, gelu_arg, gelu_tanh = sem("gelu_sq"), sem("gelu_arg"), sem("gelu_tanh")
        v_normed, ws_masked, branch_a = sem("v_normed"), sem("ws_masked"), sem("branch_a")
        head_squares, head_sums = sem("head_squares"), sem("head_sums")
        q_ready, k_ready = sem("q_ready"), sem("k_ready")
        scores_done, max_ready, exp_done, prob_ready = (
            sem("scores_done"), sem("max_ready"), sem("exp_done"), sem("prob_ready"))
        merged_b, sig_done = sem("merged_b"), sem("sig_done")
        xn_hi_done, xn_lo_done, wr_hi_done, wr_lo_done = (
            sem("xn_hi_done"), sem("xn_lo_done"), sem("wr_hi_done"), sem("wr_lo_done"))
        ffn_scale_ready = sem("ffn_scale_ready")
        logits_copied, logits_turned = sem("logits_copied"), sem("logits_turned")
        logits_done, chosen_ready, gap_ready, gap_exp, places_done, counts_ready = (
            sem("logits_done"), sem("chosen_ready"), sem("gap_ready"), sem("gap_exp"), sem("places_done"),
            sem("counts_ready"))
        pass_sems = []
        for q in range(2):
            pass_sems.append({n: sem(f"{n}_{q}") for n in (
                "gu_free0", "gu_free1", "sig_ready", "sig_half", "hturn_done", "hturn_hi", "hturn_free0",
                "hturn_free1", "y_hi_done", "y_split", "g_done", "g_hi", "g_free0", "g_free1", "picked", "over")})

        class Ring:

            def __init__(self, n0, slots, landed, hi, lo, used):
                self.n0, self.slots, self.landed, self.hi, self.lo, self.used = n0, slots, landed, hi, lo, used

            def count(self, e, j):
                return self.n0 + j + PER_EXPERT * e

            def raw(self, j):
                return self.slots[j % len(self.slots)]

            def raw_view(self, j, n, w):
                return self.raw(j)[:, 0:n * w].rearrange("p (k n) -> p k n", k=n)

            def split_slot(self, j):
                return (self.n0 + j) % SPLIT

            def load(self, sp, e, j, pieces):
                r = len(self.slots)
                if j >= r or not isinstance(e, int) or e > 0:
                    sp.wait_ge(self.lo, self.count(e, j) - r + 1)
                elif self.n0 and j < RAW:
                    sp.wait_ge(self.lo, self.count(e, j) - RAW + 1)
                elif self.n0:
                    wait_turn_read(sp, last_turn["merged_turns", L - 1, 1])
                    wait_turn_read(sp, last_turn["merged_turns", L - 1, 1] - 1)
                for dst, src in pieces:
                    sp.dma_start(dst, src).then_inc(self.landed[j % r], 16)

            def split_hi(self, act, e, j, n=CHUNK):
                r = len(self.slots)
                act.wait_ge(self.landed[j % r], 32 * (j // r + 1) + 32 * (PER_EXPERT // r) * e)
                if self.n0 + j >= SPLIT or not isinstance(e, int) or e > 0:
                    act.wait_ge(self.used, self.count(e, j) - SPLIT + 1)
                nc.scalar.activation(w_hi[:, self.split_slot(j), 0:n], self.raw(j)[:, 0:n], ACT.Copy).then_inc(self.hi, 1)

            def split_lo(self, dve, e, j, n=CHUNK):
                dve.wait_ge(self.hi, self.count(e, j) + 1)
                c = self.split_slot(j)
                nc.vector.tensor_tensor(w_lo[:, c, 0:n], self.raw(j)[:, 0:n],
                                        w_hi[:, c, 0:n].bitcast(F32), ALU.subtract).then_inc(self.lo, 1)

            def take(self, pe, e, j):
                pe.wait_ge(self.lo, self.count(e, j) + 1)
                c = self.split_slot(j)
                return w_hi[:, c, :], w_lo[:, c, :]

        ring = Ring(0, [raw[:, i, :] for i in range(RAW)], raw_landed, hi_done, lo_done, chunk_used)
        moe_slots = [raw[:, (N0 + i) % RAW, :] for i in range(RAW)] + [raw_more[:, i, :] for i in range(RAW_MOE - RAW)]
        moe_ring = Ring(N0, moe_slots, raw_landed_moe, hi_done, lo_done, chunk_used)
        moe_ring2 = Ring(0, moe_slots, raw_landed2, hi_done2, lo_done2, chunk_used2)

        def ring_of(n):
            return (ring, n) if n < N0 else (moe_ring, n - N0)
        size = [n * w for _, n, w in chunks]
        DOWN_SIZE = [n * D for n in DOWN_K]
        expert_size = [CHUNK] * GU_CHUNKS + DOWN_SIZE

        def three(dst, a_hi, a_lo, b_hi, b_lo, start, stop):
            nc.tensor.matmul(dst, a_hi, b_hi, start=start, stop=False)
            nc.tensor.matmul(dst, a_lo, b_hi, start=False, stop=False)
            return nc.tensor.matmul(dst, a_hi, b_lo, start=False, stop=stop)

        def turns_in(step):
            if step[0] == "attention":
                s = step[2]
                return (2 if s < PAIRS else 0) + (2 if 2 <= s < PAIRS + 2 else 0) + (1 if 3 <= s else 0)
            return {"norm_turns": 2, "latent_turns": 3, "spatial_weights": 2, "mix_tokens": 4, "merged_turns": 2,
                    "a_turns": 2, "hidden_turn": 1, "down": 1}.get(step[0], 0)

        turn_at, ws_turn, t = [], [], 0
        last_turn = {}
        prob_turn, qk_turn = {}, {}
        for step in plan:
            if step[0] == "spatial_weights":
                ws_turn.append(t)
            turn_at.append(t)
            if step[0] == "attention":
                s, b = step[2], t + (1 if 3 <= step[2] else 0)
                if 2 <= s < PAIRS + 2:
                    prob_turn[step[1], s - 2] = b
                    b += 2
                if s < PAIRS:
                    qk_turn[step[1], s] = b
            t += turns_in(step)
            if turns_in(step):
                last_turn[step] = t - 1
        ALL_TURNS = t

        def wait_turn_read(eng, b):
            eng.wait_ge(turn_free[b % 2], b // 2 + 1)

        def operand_turns(l, what, k0):
            half = k0 // 4
            return {"cq": lambda: last_turn["norm_turns", l, 0, half],
                    "gu": lambda: last_turn["norm_turns", l, 1, half],
                    "uq": lambda: last_turn["latent_turns", l] - 1,
                    "ukv": lambda: last_turn["latent_turns", l],
                    "pa": lambda: last_turn["a_turns", l, half],
                    "pb": lambda: turn_at[plan.index(("attention", l, 4 * half + 3 + 3))],
                    "wo": lambda: last_turn["merged_turns", l, half]}.get(what, lambda: None)()

        def normed_before(l):
            return 2 * l + 2 * (l // 2)

        def wait_strip_read(eng, n):
            eng.wait_ge(strip_free[n % 2], n // 2 + 1)

        def is_first(e):
            return isinstance(e, int) and e == 0

        def strips_read(e, j):
            return ((GUS + 1) // 2 if j % 2 == 0 else GUS // 2) * e + j // 2

        def g_done(e, g):
            return 8 * e - 2 + g

        def g_read(e, g):
            return 4 * e - 1 + g // 2

        def layer_over(l):
            return strip_at[l, "down", 0] + 1

        block = ctx.enter_context(nc.Block())

        @block.sync
        def _(sp):
            for t in range(TT):
                sp.dma_start(xres[:, t, :], x[0, t * P:(t + 1) * P, :]).then_inc(x_landed, 16)
            sp.dma_start(consts[:], shape_consts[:, 0:CW]).then_inc(consts_landed, 16)
            sp.dma_start(causal, shape_consts[:, CW:CW + 2 * P]).then_inc(consts_landed, 16)
            for i, src in enumerate((mix_norm_g.rearrange("l (k p) -> (l k) p", p=P),
                                     ffn_norm_g.rearrange("l (k p) -> (l k) p", p=P),
                                     mla_q_lat_g.rearrange("l (k p) -> (l k) p", p=P),
                                     mla_kv_lat_g.rearrange("l (k p) -> (l k) p", p=P),
                                     gm_b_spatial.rearrange("l g p -> (l g) p"))):
                sp.dma_start(rows[row_at[i]:row_at[i] + row_sizes[i], :], src).then_inc(rows_landed, 16)

            def static_load(n):
                pieces, k, w = chunks[n]
                to, v = ring.raw(n), ring.raw_view(n, k, w)
                if pieces[0] == "gu":
                    ring.load(sp, 0, n, [(v[:, :, 0:HC], pieces[1]), (v[:, :, HC:2 * HC], pieces[2])])
                elif pieces[0] == "down":
                    half = k * w // 2
                    ring.load(sp, 0, n, [(to[:, 0:half], pieces[1]), (to[:, half:2 * half], pieces[2])])
                else:
                    ring.load(sp, 0, n, [(v[:, c // w:c // w + kk, :], src) for c, kk, src in pieces])

            for n in range(RAW):
                static_load(n)
            for n in range(RAW, N0):
                static_load(n)

            def expert_loads(r, e):
                for j in range(GU_CHUNKS):
                    v = r.raw_view(j, 4, STRIP)
                    g, u = gu_pieces(moe_w_gu[0, e], j // 2, 4 * (j % 2))
                    r.load(sp, e, j, [(v[:, :, 0:HC], g), (v[:, :, HC:2 * HC], u)])
                for d in range(len(DOWN_K)):
                    to = r.raw(GU_CHUNKS + d)
                    half = DOWN_SIZE[d] // 2
                    a, b = down_pieces(moe_w_down[0, e], d)
                    r.load(sp, e, GU_CHUNKS + d, [(to[:, 0:half], a), (to[:, half:2 * half], b)])

            expert_loads(moe_ring, 0)
            with sp.Fori(1, E) as e:
                expert_loads(moe_ring, e)
            sp.wait_ge(counts_ready, 1)
            crowded = sp.value_load(most[0:1, 0:1], min_val=0, max_val=S)
            sp.wait_ge(pass_sems[0]["over"], 1)
            with sp.If(crowded > P):
                expert_loads(moe_ring2, 0)
                with sp.Fori(1, E) as e:
                    expert_loads(moe_ring2, e)
                sp.wait_ge(pass_sems[1]["over"], 1)
            sp.dma_start(out[0].rearrange("(t p) d -> p t d", p=P), xres[:]).then_inc(out_stored, 16)
            sp.wait_ge(out_stored, 16)

        @block.gpsimd
        def _(pool):
            for l in range(L):
                for dst, src in ((q_gain, mla_q_norm_g), (k_gain, mla_k_norm_g)):
                    pool.dma_start(dst[:, l, :], src[l:l + 1, :].to_broadcast([P, DQ])).then_inc(small_landed, 16)
            with nc.allow_non_contiguous_dma(reason="gains as columns, 256 bytes each"):
                for l in range(L):
                    for dst, src in ((gain_q, mla_q_norm_g), (gain_k, mla_k_norm_g)):
                        pool.dma_start(dst[0:DN, l:l + 1], src[l:l + 1, 0:DN].rearrange("o d -> d o")
                                       ).then_inc(small_landed, 16)
            for l in range(L):
                if l:
                    wait_strip_read(pool, layer_over(l - 1) - 1)
                    wait_strip_read(pool, layer_over(l - 1))
                pool.dma_start(ws_raw[:], gm_w_spatial[l].rearrange("g t s -> t g s")).then_inc(ws_landed, 16)
                wait_turn_read(pool, ws_turn[l])
                wait_turn_read(pool, ws_turn[l] + 1)
                nc.gpsimd.affine_select(out=ws_t[:], in_=ws_t[:], compare_op=ALU.is_ge, fill=0.0, base=0,
                                        pattern=[[0, NG], [1, P]], channel_multiplier=-1).then_inc(ws_masked, 1)
                pool.wait_ge(chunk_used, chunk_end[l, "ukv", UKVS - 1])
                pool.dma_start(ln_rows[:, 0, :], gm_v_norm_g[l:l + 1, :].to_broadcast([P, D])).then_inc(ln_landed, 16)
                pool.dma_start(ln_rows[:, 1, :], gm_v_norm_b[l:l + 1, :].to_broadcast([P, D])).then_inc(ln_landed, 16)
            pool.wait_ge(merged_b, 2 * L)
            with nc.allow_non_contiguous_dma(reason="the router, 32 KiB"):
                pool.dma_start(wr[:], moe_w_router[0].rearrange("(k p) e -> p k e", p=P)).then_inc(wr_landed, 16)
            pool.dma_start(br[:], moe_b_router[0:1, :].to_broadcast([P, E])).then_inc(wr_landed, 16)
            pool.wait_ge(xn_hi_done, 1)
            nc.gpsimd.tensor_tensor(xn_lo[:], xn[:], xn_hi[:].bitcast(F32), ALU.subtract).then_inc(xn_lo_done, 1)
            pool.wait_ge(small_landed, 16 * 4 * L)
            pool.wait_ge(wr_landed, 32)

        @block.tensor
        def _(pe):
            def turn_bank(b):
                if b >= 2:
                    wait_turn_read(pe, b - 2)
                return ps[:, 4 + b % 2, :]

            def turn4(b, src):
                bank = turn_bank(b)
                for i in range(4):
                    mm = nc.tensor.transpose(bank[:, i * P:(i + 1) * P], src(i // TT, i % TT), ident)
                mm.then_inc(turn_done, 1)

            def twice(v):
                return v.rearrange("p (o n) -> p o n", o=1).to_broadcast([P, 2, v.shape[1]])

            def wait_turns_split(b):
                wait_turn_read(pe, b - 1)
                wait_turn_read(pe, b - 2)

            operands = {"cq": (act_hi, act_lo, 0), "ckv": (act_hi, act_lo, 0), "v": (act_hi, act_lo, 0),
                        "u": (act_hi, act_lo, 0), "ga": (act_hi, act_lo, 0), "gb": (act_hi, act_lo, 0),
                        "gu": (act_hi, act_lo, 0), "uq": (t1_hi, t1_lo, 0), "ukv": (t1_hi, t1_lo, KQ),
                        "pa": (t1_hi, t1_lo, 0), "pb": (bt_hi, bt_lo, 0), "wo": (act_hi, act_lo, 0)}
            latents = qb[:].rearrange("p t h d -> p (t h d)")
            CKV0, CKVW = TT * QL, KVL + DR

            pe.wait_ge(consts_landed, 32)
            pe.wait_ge(rows_landed, 80)
            nc.tensor.transpose(ps[:, 6, 0:ROWS], rows, ident[0:ROWS, 0:ROWS]).then_inc(rows_turned, 1)
            for i, step in enumerate(plan):
                kind, l, b0 = step[0], step[1], turn_at[i]
                if kind == "norm_turns":
                    half = step[3]
                    src = xres if step[2] else vbuf
                    if step[2]:
                        wait_strip_read(pe, strip_at[l, "wo", half])
                    else:
                        pe.wait_ge(normed0_done, normed_before(l) + half + 1)
                        pe.wait_ge(normed1_done, normed_before(l) + half + 1)
                    for b in range(2):
                        c = 4 * half + 2 * b
                        turn4(b0 + b, lambda k, t: src[:, t, (c + k) * P:(c + k + 1) * P])
                elif kind == "spatial_weights":
                    pe.wait_ge(ws_landed, 16 * (l + 1))
                    for b in range(2):
                        bank = turn_bank(b0 + b)
                        for g in range(4):
                            mm = nc.tensor.transpose(bank[:, g * P:(g + 1) * P], ws_raw[:, 4 * b + g, :], ident)
                        mm.then_inc(turn_done, 1)
                elif kind == "latent_turns":
                    pe.wait_ge(latent_normed, l + 1)
                    for b in range(2):
                        turn4(b0 + b, lambda k, t: latents[:, t * QL + (2 * b + k) * P:t * QL + (2 * b + k + 1) * P])
                    turn4(b0 + 2, lambda k, t: latents[:, CKV0 + t * CKVW + k * P:CKV0 + t * CKVW + (k + 1) * P])
                elif kind == "mix_tokens":
                    pe.wait_ge(v_normed, TT * (l + 1))
                    pe.wait_ge(ws_masked, l + 1)
                    for b in range(4):
                        bank = turn_bank(b0 + b)
                        for g in range(2):
                            c = (2 * b + g) * P
                            mm = nc.tensor.matmul(bank[:, g * S:(g + 1) * S].rearrange("p (t d) -> p t d", t=TT),
                                                  ws_t[:, 2 * b + g, :], vbuf[:, :, c:c + P], start=True, stop=True)
                        mm.then_inc(turn_done, 1)
                elif kind == "a_turns":
                    j = step[2]
                    pe.wait_ge(branch_a, 2 * l + j + 1)
                    for b in range(2):
                        turn4(b0 + b, lambda k, t: vbuf[:, t, (4 * j + 2 * b + k) * P:(4 * j + 2 * b + k + 1) * P])
                elif kind == "merged_turns":
                    half = step[2]
                    pe.wait_ge(merged_b, 2 * l + half + 1)
                    for b in range(2):
                        c = 4 * half + 2 * b
                        turn4(b0 + b, lambda k, t: vbuf[:, t, (c + k) * P:(c + k + 1) * P])
                elif kind == "hidden_turn":
                    j = step[2]
                    wait_strip_read(pe, strip_at[l, "gu", j])
                    turn4(b0, lambda k, t: hid[:, j % 2, t, k * P:(k + 1) * P])
                elif kind == "attention":
                    s, b = step[2], b0
                    if s >= 3:
                        n = s - 3
                        wait_turn_read(pe, prob_turn[l, n])
                        wait_turn_read(pe, prob_turn[l, n] + 1)
                        bank = turn_bank(b)
                        for hh in range(2):
                            dst = bank[hh * DV:(hh + 1) * DV, :]
                            v0, v1 = vv[:, 0, 2 * n + hh, :], vv[:, 1, 2 * n + hh, :]
                            t10, t11 = 2 + 2 * hh, 3 + 2 * hh
                            nc.tensor.matmul(dst[:, 0:P], v0, prob_t[:, hh * P:(hh + 1) * P], start=True, stop=True)
                            nc.tensor.matmul(dst[:, P:S], v0, prob_t[:, t10 * P:(t10 + 1) * P], start=True, stop=False)
                            mm = nc.tensor.matmul(dst[:, P:S], v1, prob_t[:, t11 * P:(t11 + 1) * P], start=False, stop=True)
                        mm.then_inc(turn_done, 1)
                        b += 1
                    if 1 <= s < PAIRS + 1:
                        n = PAIRS * l + s - 1
                        wait_turn_read(pe, qk_turn[l, s - 1])
                        wait_turn_read(pe, qk_turn[l, s - 1] + 1)
                        if n:
                            pe.wait_ge(exp_done, n)
                        else:
                            pe.wait_ge(mask_ready, 1)
                        nc.tensor.matmul(ps[:, 6, 0:2 * P].rearrange("p (h k) -> p h k", h=2), ident_r[:],
                                         twice(causal_r[:, P:2 * P]), start=True, stop=False)
                        nc.tensor.matmul(ps[:, 7, :].rearrange("p (h k) -> p h k", h=2), ident_r[:],
                                         twice(causal_r[:]), start=True, stop=False)
                        for hh in range(2):
                            q_t, k_t = qk_t[0:DQ, hh, 0:S], qk_t[0:DQ, hh, S:2 * S]
                            nc.tensor.matmul(ps[:, 6, hh * P:(hh + 1) * P], q_t[:, 0:P], k_t[:, 0:P], start=False, stop=hh == 1)
                            mm = nc.tensor.matmul(ps[:, 7, hh * S:(hh + 1) * S], q_t[:, P:S], k_t, start=False, stop=hh == 1)
                        mm.then_inc(scores_done, 1)
                    if 2 <= s < PAIRS + 2:
                        pe.wait_ge(prob_ready, PAIRS * l + s - 1)
                        for blocks in ((0, 1, 2, 3), (4, 5)):
                            bank = turn_bank(b)
                            for q, blk in enumerate(blocks):
                                mm = nc.tensor.transpose(bank[:, q * P:(q + 1) * P], probs[s % 2][:, blk * P:(blk + 1) * P], ident)
                            mm.then_inc(turn_done, 1)
                            b += 1
                    if s < PAIRS:
                        if s == 0:
                            pe.wait_ge(q_ready, l + 1)
                            pe.wait_ge(k_ready, l + 1)
                        for hh in range(2):
                            bank = turn_bank(b)
                            for q in range(4):
                                src = (qb, kb)[q // 2]
                                mm = nc.tensor.transpose(bank[0:DQ, q * P:(q + 1) * P], src[:, q % 2, 2 * s + hh, :], ident)
                            mm.then_inc(turn_done, 1)
                            b += 1
                elif kind == "mul":
                    _, _, what, j, k0, kt, ends, width, c = step
                    hi, lo, k_at = operands[what]
                    n = strip_at[l, what, j]
                    turned = operand_turns(l, what, k0)
                    if j == 0 and turned is not None:
                        wait_turns_split(turned + 1)
                    if n >= 2 and k0 == 0:
                        wait_strip_read(pe, n - 2)
                    ch, cl = ring.take(pe, 0, c)
                    for t in range(TT):
                        for k in range(kt):
                            kk = k_at + k0 + k
                            mm = three(ps[:, 2 * (n % 2) + t, 0:width], hi[:, kk, t * P:(t + 1) * P],
                                       lo[:, kk, t * P:(t + 1) * P], ch[:, k * width:(k + 1) * width],
                                       cl[:, k * width:(k + 1) * width], k0 + k == 0, ends and k == kt - 1)
                    mm.then_inc(chunk_used, 1)
                elif kind == "down":
                    a, n = step[2], step[4]
                    wait_turns_split(b0)
                    wait_strip_read(pe, n - 2)
                    k_at = 0
                    for d, kt in enumerate(DOWN_K):
                        if d == len(DOWN_K) - 1:
                            wait_turns_split(b0 + 1)
                        ch, cl = ring.take(pe, 0, a + d)
                        for t in range(TT):
                            if t and not d:
                                wait_strip_read(pe, n - 1)
                            for k in range(kt):
                                kk = k_at + k
                                for hf in range(2):
                                    c = k * D + hf * 512
                                    mm = three(ps[:, (2 * n + 2 * t) % 4 + hf, :], hid_hi[:, kk, t * P:(t + 1) * P],
                                               hid_lo[:, kk, t * P:(t + 1) * P], ch[:, c:c + 512], cl[:, c:c + 512],
                                               kk == 0, kk == KF - 1)
                        mm.then_inc(chunk_used, 1)
                        k_at += kt
                        if d == LAST_TURN:
                            wait_strip_read(pe, n - 1)
                            turn4(b0, lambda k, t: hid[:, (GUS - 1) % 2, t, k * P:(k + 1) * P])

            wait_turns_split(ALL_TURNS)
            pe.wait_ge(wr_lo_done, 1)
            for k in range(KD):
                mm = three(ps[0:E, 4, 0:S], wr_hi[:, k, :], wr_lo[:, k, :], act_hi[:, k, :], act_lo[:, k, :],
                           k == 0, k == KD - 1)
            mm.then_inc(logits_done, 1)
            pe.wait_ge(logits_copied, 1)
            for t in range(TT):
                mm = nc.tensor.transpose(ps[:, 5, t * E:(t + 1) * E], logit_t[:, t * P:(t + 1) * P], ident[0:E, 0:E])
            mm.then_inc(logits_turned, 1)
            pe.wait_ge(chosen_ready, 1)
            nc.tensor.matmul(ps[:, 4, 0:E], before, chosen[:, 0, :], start=True, stop=True)
            nc.tensor.matmul(ps[:, 4, E:2 * E], before, chosen[:, 1, :], start=True, stop=False)
            nc.tensor.matmul(ps[:, 4, E:2 * E], ones, chosen[:, 0, :], start=False, stop=True)
            nc.tensor.matmul(ps[:, 4, 2 * E:3 * E], ones, chosen[:, 0, :], start=True, stop=False)
            nc.tensor.matmul(ps[:, 4, 2 * E:3 * E], ones, chosen[:, 1, :], start=False, stop=True).then_inc(places_done, 1)

            def moe_pass(r, z):
                def gather(half):
                    bank = ps[:, 6 + half, :]
                    for k in range(4):
                        c = (4 * half + k) * P
                        for t in range(TT):
                            nc.tensor.matmul(bank[:, k * P:(k + 1) * P], xn_hi[:, t, c:c + P], pick[:, t, :],
                                             start=t == 0, stop=False)
                            mm = nc.tensor.matmul(bank[:, k * P:(k + 1) * P], xn_lo[:, t, c:c + P], pick[:, t, :],
                                                  start=False, stop=t == TT - 1)
                    mm.then_inc(z["g_done"], 1)

                def scatter(t, g_read):
                    for hf in range(2):
                        pe.wait_ge(z[f"g_free{hf}"], g_read)
                        nc.tensor.matmul(ps[:, 6 + hf, :], put[:, t * P:(t + 1) * P], y_hi[:, hf * 512:(hf + 1) * 512],
                                         start=True, stop=False)
                        nc.tensor.matmul(ps[:, 6 + hf, :], put[:, t * P:(t + 1) * P], y_lo[:, hf * 512:(hf + 1) * 512],
                                         start=False, stop=True).then_inc(z["g_done"], 1)

                def hidden_turn(e, j):
                    pe.wait_ge(z[f"gu_free{j % 2}"], strips_read(e, j) + 1)
                    if j >= 2 or not is_first(e):
                        pe.wait_ge(z[f"hturn_free{j % 2}"], strips_read(e, j))
                    for k in range(2):
                        mm = nc.tensor.transpose(ps[:, 4 + j % 2, k * P:(k + 1) * P], hid[:, j % 2, 0, k * P:(k + 1) * P], ident)
                    mm.then_inc(z["hturn_done"], 1)

                def body(e, last):
                    first = is_first(e)
                    for j in range(GUS):
                        if j >= 2 or not first:
                            pe.wait_ge(z[f"gu_free{j % 2}"], strips_read(e, j))
                        for c in range(2):
                            if j == 0:
                                pe.wait_ge(z[f"g_free{c}"], 1 if first else g_read(e, 0))
                            ch, cl = r.take(pe, e, 2 * j + c)
                            for k in range(4):
                                kk = 4 * c + k
                                mm = three(ps[:, j % 2, :], act_hi[:, kk, 0:P], act_lo[:, kk, 0:P],
                                           ch[:, k * STRIP:(k + 1) * STRIP], cl[:, k * STRIP:(k + 1) * STRIP],
                                           kk == 0, kk == KD - 1)
                            mm.then_inc(r.used, 1)
                            if c == 0 and j >= 2:
                                hidden_turn(e, j - 2)
                        if not first and j == 1:
                            pe.wait_ge(z["y_split"], e)
                            scatter(0, g_read(e, 0))
                        if not first and j == 3:
                            scatter(1, g_read(e, 2))
                        if j == 5:
                            pe.wait_ge(z["g_free0"], g_read(e, 4))
                            for t in range(TT):
                                mm = nc.tensor.transpose(ps[:, 6, t * P:(t + 1) * P], pick[:, t, :].bitcast(F32), ident)
                            mm.then_inc(z["g_done"], 1)
                            pe.wait_ge(z["g_free1"], g_read(e, 4))
                            for t in range(TT):
                                mm = nc.tensor.matmul(ps[:, 7, 0:1], pick[:, t, :].bitcast(F32), pick_w[:, t:t + 1],
                                                      start=t == 0, stop=t == TT - 1)
                            mm.then_inc(z["g_done"], 1)
                    k_at = 0
                    for d, kt in enumerate(DOWN_K):
                        if d == 0 and not first:
                            pe.wait_ge(z["y_split"], e)
                        ch, cl = r.take(pe, e, GU_CHUNKS + d)
                        s = (k_at + kt - 1) // 2
                        if s > (k_at - 1) // 2 or not k_at:
                            pe.wait_ge(z[f"hturn_free{s % 2}"], strips_read(e, s) + 1)
                        for k in range(kt):
                            kk = k_at + k
                            for hf in range(2):
                                c = k * D + hf * 512
                                mm = three(ps[:, 2 + hf, :], ehid_hi[:, kk, :], ehid_lo[:, kk, :], ch[:, c:c + 512],
                                           cl[:, c:c + 512], kk == 0, kk == KF - 1)
                        mm.then_inc(r.used, 1)
                        k_at += kt
                        if d == 0:
                            hidden_turn(e, GUS - 2)
                        if d == 2:
                            hidden_turn(e, GUS - 1)
                        if not last and d in (4, 6):
                            if d == 4:
                                pe.wait_ge(z["picked"], e + 2)
                            pe.wait_ge(z[f"g_free{(d - 4) // 2}"], g_read(e, 6))
                            gather((d - 4) // 2)

                pe.wait_ge(z["picked"], 1)
                gather(0)
                gather(1)
                body(0, False)
                with pe.Fori(1, E - 1) as e:
                    body(e, False)
                body(E - 1, True)
                pe.wait_ge(z["y_split"], E)
                scatter(0, g_read(E, 0) - 1)
                scatter(1, g_read(E, 2) - 1)

            pe.wait_ge(xn_lo_done, 1)
            moe_pass(moe_ring, pass_sems[0])
            pe.wait_ge(counts_ready, 1)
            crowded = pe.value_load(most[0:1, 0:1], min_val=0, max_val=S)
            with pe.If(crowded > P):
                pe.wait_ge(pass_sems[0]["over"], 1)
                moe_pass(moe_ring2, pass_sems[1])

        @block.scalar
        def _(act):
            own = Chain(act, act_own)
            latents = qb[:].rearrange("p t h d -> p (t h d)")
            CKV0, CKVW = TT * QL, KVL + DR
            counts = {"split_turns": 0, "head_sums": 0}

            def copy(dst, src, scale=1.0):
                return nc.scalar.activation(dst, src, ACT.Copy, scale=scale)

            def splits(a, b):
                for n in range(a + LEAD, b + LEAD):
                    r, j = ring_of(n)
                    r.split_hi(act, 0, j, size[n] if n < N0 else CHUNK)

            def turn_hi_parts(b, hi, k0, scale):
                act.wait_ge(turn_done, b + 1)
                for k in range(2):
                    op = copy(hi[:, k0 + k, :], ps[:, 4 + b % 2, k * S:(k + 1) * S], scale(k0 + k))
                op.then_inc(turn_hi, 1)

            act.wait_ge(x_landed, 32)
            for i, step in enumerate(plan):
                kind, l, b0 = step[0], step[1], turn_at[i]
                if kind == "squares":
                    half = step[2]
                    cols = slice(half * STRIP, (half + 1) * STRIP)
                    for t in range(TT):
                        if t:
                            wait_strip_read(act, strip_at[l, "wo", half])
                        else:
                            act.wait_ge(x_added, 2 * l + half + 1)
                        nc.scalar.activation(xn[:, t, cols], xres[:, t, cols], ACT.Square,
                                             accum_out=square_sum[:, half, t:t + 1]).then_inc(squares_done, 1)
                elif kind == "norm":
                    dst = xn if step[2] else vbuf
                    m = 2 * l + step[2]
                    if not step[2]:
                        for t in range(TT):
                            if l:
                                wait_strip_read(act, layer_over(l - 1) - 1 + t)
                            nc.scalar.activation(dst[:, t, :], xres[:, t, :], ACT.Square,
                                                 accum_out=square_sum[:, 0, t:t + 1]).then_inc(squares_done, 1)
                    if not m:
                        act.wait_ge(consts_landed, 32)
                        copy(ident_r[:], ident)
                        copy(causal_r[:], causal).then_inc(mask_ready, 1)
                        act.wait_ge(rows_turned, 1)
                        copy(cols_t[:], ps[:, 6, 0:ROWS]).then_inc(gains_ready, 1)
                        act.wait_ge(gains_ready, 1)
                    splits(step[3], step[3] + 1) if m else ring.split_hi(act, 0, 0, size[0])
                    if step[2] and l % 2 == 0:
                        continue
                    act.wait_ge(root_done, m + 1)
                    for half in range(2):
                        cols = slice(half * STRIP, (half + 1) * STRIP)
                        copy(dst[:, 0, cols], xres[:, 0, cols], small[:, 2:3]).then_inc(normed0_done, 1)
                elif kind == "norm_turns":
                    g = ffn_g if step[2] else mix_g
                    for b in range(2):
                        turn_hi_parts(b0 + b, act_hi, 4 * step[3] + 2 * b, lambda k: g[:, l, k:k + 1])
                    if (l, step[2], step[3]) == (0, 0, 1):
                        for n in range(1, LEAD):
                            ring.split_hi(act, 0, n, size[n])
                elif kind == "spatial_weights":
                    for b in range(2):
                        act.wait_ge(turn_done, b0 + b + 1)
                        copy(ws_t[:, 4 * b:4 * b + 4, :], ps[:, 4 + (b0 + b) % 2, :].rearrange("p (g s) -> p g s", g=4)
                             ).then_inc(turn_free[(b0 + b) % 2], 1)
                elif kind == "latent_turns":
                    for b in range(2):
                        turn_hi_parts(b0 + b, t1_hi, 2 * b, lambda k: qlat_g[:, l, k:k + 1])
                    turn_hi_parts(b0 + 2, t1_hi, KQ, lambda k: kvlat_g[:, l, k - KQ:k - KQ + 1])
                elif kind == "a_turns":
                    for b in range(2):
                        turn_hi_parts(b0 + b, t1_hi, 4 * step[2] + 2 * b, lambda k: 1.0)
                elif kind == "merged_turns":
                    for b in range(2):
                        turn_hi_parts(b0 + b, act_hi, 4 * step[2] + 2 * b, lambda k: 0.5)
                elif kind == "hidden_turn":
                    turn_hi_parts(b0, hid_hi, 2 * step[2], lambda k: 1.0)
                elif kind == "head_sums":
                    src, w, last = (qb, DQ, ("uq", UQS - 1)) if step[2] == "q" else (kb, DN, ("ukv", UKVS - 1))
                    wait_strip_read(act, strip_at[l, last[0], last[1]])
                    for t in range(TT):
                        for hf in range(2):
                            n = counts["head_sums"]
                            if n >= 2:
                                act.wait_ge(head_sums, n - 1)
                            counts["head_sums"] += 1
                            nc.scalar.activation(square_of[n % 2][:, 0:8 * w].rearrange("p (h d) -> p h d", h=8),
                                                 src[:, t, 8 * hf:8 * hf + 8, 0:w], ACT.Square).then_inc(head_squares, 1)
                elif kind == "mix_tokens":
                    for b in range(4):
                        bb = b0 + b
                        act.wait_ge(turn_done, bb + 1)
                        for g in range(2):
                            gg = 2 * b + g
                            op = nc.scalar.activation(vbuf[:, :, gg * P:(gg + 1) * P],
                                                      ps[:, 4 + bb % 2, g * S:(g + 1) * S].rearrange(
                                                          "p (t d) -> p t d", t=TT),
                                                      ACT.Identity, bias=b_sp[:, l, gg:gg + 1], scale=0.5)
                        op.then_inc(turn_free[bb % 2], 1)
                elif kind == "attention":
                    s, b = step[2], b0
                    if s >= 3:
                        act.wait_ge(turn_done, b + 1)
                        copy(bt_hi[:, s - 3, :], ps[:, 4 + b % 2, 0:S]).then_inc(turn_hi, 1)
                        b += 1
                    if 2 <= s < PAIRS + 2:
                        for c, w in ((0, 512), (512, 256)):
                            act.wait_ge(turn_done, b + 1)
                            copy(prob_t[:, c:c + w], ps[:, 4 + b % 2, 0:w]).then_inc(turn_free[b % 2], 1)
                            b += 1
                    if s < PAIRS:
                        if s >= 1:
                            act.wait_ge(scores_done, PAIRS * l + s)
                        for hh in range(2):
                            act.wait_ge(turn_done, b + 1)
                            if not l and not s and not hh:
                                act.wait_ge(qk_gain_ready, 1)
                            copy(qk_t[0:DQ, hh, 0:S], ps[0:DQ, 4 + b % 2, 0:S], qk_gain[0:DQ, l:l + 1])
                            copy(qk_t[0:DQ, hh, S:2 * S], ps[0:DQ, 4 + b % 2, S:2 * S]).then_inc(turn_free[b % 2], 1)
                            b += 1
                    if 1 <= s < PAIRS + 1:
                        act.wait_ge(max_ready, PAIRS * l + s)
                        pr = probs[(s - 1) % 2]
                        for q in range(4):
                            t, hh, w = q // 2, q % 2, S if q >= 2 else P
                            c, h = (hh * P, 2 * P + hh * S)[t], 2 * (s - 1) + hh
                            op = nc.scalar.activation(pr[:, c:c + w], ps[:, 6 + t, hh * w:(hh + 1) * w], ACT.Exp,
                                                      bias=soft[:, 0, q:q + 1], scale=q_sum[:, t, h:h + 1],
                                                      accum_out=soft[:, 1, q:q + 1])
                        op.then_inc(exp_done, 1)
                elif kind == "split":
                    splits(step[2], step[2] + 1)
                elif kind == "evac":
                    _, _, what, j = step
                    n, end = strip_at[l, what, j], chunk_end[l, what, j]
                    bank = ps[:, 2 * (n % 2):2 * (n % 2) + 2, :]
                    free = strip_free[n % 2]
                    if what in ("wo", "pa", "pb"):
                        continue
                    act.wait_ge(chunk_used, end)
                    if what == "cq":
                        for t in range(TT):
                            own.link(nc.scalar.activation(sq[:, 0:QL], bank[:, t, 0:QL], ACT.Square,
                                                          accum_out=small[:, 4 + t:5 + t]))
                        op = copy(latents[:, 0:TT * QL].rearrange("p (t c) -> p t c", t=TT), bank[:, :, 0:QL])
                    elif what == "ckv":
                        for t in range(TT):
                            own.link(nc.scalar.activation(sq[:, 0:KVL], bank[:, t, 0:KVL], ACT.Square,
                                                          accum_out=small[:, 6 + t:7 + t]))
                            own.link(nc.scalar.activation(sq[:, 0:DR], bank[:, t, KVL:KVL + DR], ACT.Square,
                                                          accum_out=small[:, 12 + t:13 + t]))
                        copy(kr[:, :, :], bank[:, :, KVL:KVL + DR])
                        op = copy(latents[:, CKV0:CKV0 + TT * CKVW].rearrange("p (t c) -> p t c", t=TT),
                                  bank[:, :, 0:CKVW])
                    elif what in ("v", "u"):
                        m = 4 * l + (2 if what == "u" else 0) + j
                        if (what, j) == ("v", 0):
                            if l:
                                wait_strip_read(act, strip_at[l - 1, "pa", 1])
                        elif what == "u":
                            act.wait_ge(chunk_used, chunk_end[l, "ukv", UKVS - 1])
                        else:
                            wait_strip_read(act, strip_at[l, "v", 0])
                        dst = u_buf[:, j] if what == "u" else tmp[:]
                        nc.scalar.activation(dst, bank, ACT.Square).then_inc(gelu_sq, 1)
                        act.wait_ge(gelu_arg, m + 1)
                        nc.scalar.activation(dst, dst, ACT.Tanh, scale=GELU_A * GELU_C).then_inc(gelu_tanh, 1)
                        continue
                    elif what == "uq":
                        if j == 0:
                            act.wait_ge(turn_done, last_turn["latent_turns", l] + 1)
                        flat = qb[:].rearrange("p t h d -> p t (h d)")
                        op = copy(flat[:, :, j * STRIP:(j + 1) * STRIP], bank)
                    elif what == "ukv":
                        for t in range(TT):
                            heads = bank[:, t, :].rearrange("p (h c) -> p h c", h=HPS)
                            copy(kb[:, t, HPS * j:HPS * (j + 1), 0:DN], heads[:, :, 0:DN])
                            op = copy(vv[:, t, HPS * j:HPS * (j + 1), :], heads[:, :, DN:DN + DV])
                    elif what in ("ga", "gb"):
                        dst = tmp[:] if what == "ga" else gate_b[j]
                        if what == "ga" and j == 0:
                            wait_strip_read(act, strip_at[l, "v", 1])
                        elif what == "ga":
                            wait_strip_read(act, strip_at[l, "pa", 0])
                        elif j:
                            act.wait_ge(turn_done, last_turn["mix_tokens", l] + 1)
                        op = nc.scalar.activation(dst, bank, ACT.Tanh, scale=0.5)
                    elif what == "gu":
                        if j:
                            wait_strip_read(act, n - 1)
                        else:
                            act.wait_ge(ffn_scale_ready, l // 2 + 1)
                        for t in range(TT):
                            op = nc.scalar.activation(sig[:, t, :], bank[:, t, 0:HC], ACT.Tanh,
                                                      scale=ffn_scale[:, t:t + 1])
                        free = sig_done
                    op.then_inc(free, 1)
                elif kind == "router":
                    act.wait_ge(wr_landed, 32)
                    copy(wr_hi[:], wr[:]).then_inc(wr_hi_done, 1)
                elif kind == "down":
                    splits(step[2], step[2] + LAST_TURN)
                    turn_hi_parts(b0, hid_hi, 2 * (GUS - 1), lambda k: 1.0)
                    splits(step[2] + LAST_TURN, step[3] - 1)

            act.wait_ge(normed0_done, normed_before(L))
            act.wait_ge(normed1_done, normed_before(L))
            copy(xn_hi[:], xn[:]).then_inc(xn_hi_done, 1)
            act.wait_ge(gap_ready, 1)
            nc.scalar.activation(rt[:, :, 1], rt[:, :, 0], ACT.Exp).then_inc(gap_exp, 1)

            def moe_pass(r, z):
                def turn_part(e, j):
                    act.wait_ge(z["hturn_done"], GUS * e + j + 1)
                    copy(ehid_hi[:, 2 * j:2 * j + 2, :], ps[:, 4 + j % 2, 0:2 * P].rearrange("p (k s) -> p k s", k=2)
                         ).then_inc(z["hturn_hi"], 1)

                def gather_part(e, half):
                    act.wait_ge(z["g_done"], 1 + half if e is None else g_done(e, 6 + half) + 1)
                    for k in range(4):
                        kk = 4 * half + k
                        op = copy(act_hi[:, kk, 0:P], ps[:, 6 + half, k * P:(k + 1) * P], ffn_g[:, L - 1, kk:kk + 1])
                    op.then_inc(z["g_hi"], 1)

                def split(e, c, last):
                    if c < PER_EXPERT:
                        r.split_hi(act, e, c, expert_size[c])
                    elif not last:
                        r.split_hi(act, e + 1, c - PER_EXPERT, expert_size[c - PER_EXPERT])

                def body(e, last):
                    first = is_first(e)
                    for j in range(GUS):
                        split(e, 2 * j + LEAD, last)
                        split(e, 2 * j + 1 + LEAD, last)
                        act.wait_ge(r.used, r.count(e, 2 * j + 2))
                        if j or not first:
                            q = j - 1 if j else GUS - 1
                            act.wait_ge(z[f"gu_free{q % 2}"], strips_read(e if j else e - 1, q) + 1)
                        nc.scalar.activation(sig[:, 0, :], ps[:, j % 2, 0:HC], ACT.Tanh, scale=0.5).then_inc(z["sig_ready"], 1)
                        if j >= 2:
                            turn_part(e, j - 2)
                        if j == 6:
                            act.wait_ge(z["g_done"], g_done(e, 4) + 1)
                            copy(put[:], ps[:, 6, 0:S]).then_inc(z["g_free0"], 1)
                            act.wait_ge(z["g_done"], g_done(e, 5) + 1)
                            copy(slot_w[:], ps[:, 7, 0:1]).then_inc(z["g_free1"], 1)
                    for d in range(len(DOWN_K)):
                        split(e, GU_CHUNKS + d + LEAD, last)
                        if d == 1:
                            turn_part(e, GUS - 2)
                        if d == 3:
                            turn_part(e, GUS - 1)
                        if not last and d in (5, 7):
                            gather_part(e, (d - 5) // 2)
                    act.wait_ge(r.used, r.count(e, PER_EXPERT))
                    act.wait_ge(z["g_free1"], g_read(e, 4) + 1)
                    copy(y_hi[:], ps[:, 2:4, :].rearrange("p a b -> p (a b)"), slot_w[:, 0:1]).then_inc(z["y_hi_done"], 1)

                gather_part(None, 0)
                gather_part(None, 1)
                body(0, False)
                with act.Fori(1, E - 1) as e:
                    body(e, False)
                body(E - 1, True)

            moe_pass(moe_ring, pass_sems[0])
            act.wait_ge(counts_ready, 1)
            crowded = act.value_load(most[0:1, 0:1], min_val=0, max_val=S)
            with act.If(crowded > P):
                act.wait_ge(pass_sems[0]["over"], 1)
                for c in range(LEAD):
                    moe_ring2.split_hi(act, 0, c)
                moe_pass(moe_ring2, pass_sems[1])

        @block.vector
        def _(dve):
            own = Chain(dve, dve_own)
            link = own.link
            latents = qb[:].rearrange("p t h d -> p (t h d)")
            CKV0, CKVW = TT * QL, KVL + DR
            counts = {"split_turns": 0, "heads": 0}
            tt, ts, stt = nc.vector.tensor_tensor, nc.vector.tensor_scalar, nc.vector.scalar_tensor_tensor

            def splits(a, b):
                for n in range(a + LEAD, b + LEAD):
                    r, j = ring_of(n)
                    r.split_lo(dve, 0, j, size[n] if n < N0 else CHUNK)

            def turn_lo_parts(b, hi, lo, k0, scale):
                counts["split_turns"] += 1
                dve.wait_ge(turn_hi, counts["split_turns"])
                for k in range(2):
                    op = stt(lo[:, k0 + k, :], ps[:, 4 + b % 2, k * S:(k + 1) * S], scale(k0 + k),
                             hi[:, k0 + k, :].bitcast(F32), ALU.mult, ALU.subtract)
                op.then_inc(turn_free[b % 2], 1)

            def root(dst, src, scale, eps, n, last=None):
                a, t_, yi = rs_a[:, 0:n], rs_t[:, 0:n], rs_y[:, 0:n]
                y = yi.bitcast(F32)
                link(ts(a, src, scale, eps, ALU.mult, ALU.add))
                link(ts(yi, a.bitcast(I32), 1, None, ALU.logical_shift_right))
                link(ts(yi, yi, -1.0, RSQRT_SEED, ALU.mult, ALU.add))
                for it in range(3):
                    link(tt(t_, y, y, ALU.mult))
                    link(stt(t_, t_, -0.5, a, ALU.mult, ALU.mult))
                    op = stt(dst if it == 2 else y, t_, 1.5, y, ALU.add, ALU.mult)
                    if it == 2 and last is not None:
                        op.then_inc(last, 1)
                        return
                    link(op)

            def rope(x1, x2, cos, sin, s1, s2, last=None):
                link(tt(s1, x2, sin, ALU.mult))
                link(tt(s2, x1, sin, ALU.mult))
                link(tt(x1, x1, cos, ALU.mult))
                link(tt(x1, x1, s1, ALU.subtract))
                link(tt(x2, x2, cos, ALU.mult))
                op = tt(x2, x2, s2, ALU.add)
                if last is None:
                    link(op)
                else:
                    op.then_inc(last, 1)

            def sum_squares(dst, w):
                counts["heads"] += 1
                dve.wait_ge(head_squares, counts["heads"])
                nc.vector.tensor_reduce(dst, square_of[(counts["heads"] - 1) % 2][:, 0:8 * w].rearrange("p (h d) -> p h d", h=8), AX.X,
                                        ALU.add).then_inc(head_sums, 1)

            def over(v, n):
                return v.rearrange("p (m o) -> p m o", o=1).to_broadcast([P, v.shape[1], n])

            def each(v, m):
                return v.rearrange("p (o n) -> p o n", o=1).to_broadcast([P, m, v.shape[1]])

            def each_head(v):
                return v.rearrange("p t (o n) -> p t o n", o=1).to_broadcast([P, TT, H, v.shape[2]])

            dve.wait_ge(x_landed, 32)
            for i, step in enumerate(plan):
                kind, l, b0 = step[0], step[1], turn_at[i]
                if kind == "norm":
                    dst = xn if step[2] else vbuf
                    m = 2 * l + step[2]
                    dve.wait_ge(squares_done, 6 * l + (6 if step[2] else 2))
                    if step[2]:
                        link(tt(square_sum[:, 0, :], square_sum[:, 0, :], square_sum[:, 1, :], ALU.add))
                    root(small[:, 2:4], square_sum[:, 0, :], 1.0 / D, EPS, 2, root_done)
                    dve.wait_ge(root_done, m + 1)
                    if step[2] and l % 2 == 0:
                        link(ts(ffn_scale[:, 0:TT], small[:, 2:4], 0.5, None, ALU.mult))
                        tt(ffn_scale[:, TT:2 * TT], ffn_scale[:, 0:TT], small[:, 2:4], ALU.mult).then_inc(ffn_scale_ready, 1)
                    else:
                        for half in range(2):
                            cols = slice(half * STRIP, (half + 1) * STRIP)
                            ts(dst[:, 1, cols], xres[:, 1, cols], small[:, 3:4], None, ALU.mult).then_inc(normed1_done, 1)
                    if step[2] and l == L - 1:
                        pass
                    elif m:
                        splits(step[3], step[3] + 1)
                    else:
                        dve.wait_ge(gains_ready, 1)
                        ring.split_lo(dve, 0, 0, size[0])
                elif kind == "norm_turns":
                    g = ffn_g if step[2] else mix_g
                    for b in range(2):
                        turn_lo_parts(b0 + b, act_hi, act_lo, 4 * step[3] + 2 * b, lambda k: g[:, l, k:k + 1])
                    if (l, step[2], step[3]) == (0, 0, 1):
                        for n in range(1, LEAD):
                            ring.split_lo(dve, 0, n, size[n])
                elif kind == "latent_norm":
                    wait_strip_read(dve, strip_at[l, "cq", 0])
                    wait_strip_read(dve, strip_at[l, "ckv", 0])
                    link(ts(small[:, 4:6], small[:, 4:6], 1.0 / QL, None, ALU.mult))
                    link(ts(small[:, 6:8], small[:, 6:8], 1.0 / KVL, None, ALU.mult))
                    root(small[:, 8:12], small[:, 4:8], 1.0, EPS, 4)
                    for t in range(TT):
                        q, c = latents[:, t * QL:(t + 1) * QL], latents[:, CKV0 + t * CKVW:CKV0 + t * CKVW + KVL]
                        ts(q, q, small[:, 8 + t:9 + t], None, ALU.mult)
                        op = ts(c, c, small[:, 10 + t:11 + t], None, ALU.mult)
                    op.then_inc(latent_normed, 1)
                elif kind == "rotary_key":
                    s1, s2 = (v[:, 0:TT * HR].rearrange("p (t r) -> p t r", t=TT) for v in (rs_a, rs_t))
                    link(tt(kr[:], kr[:], each(k_gain[:, l, DN:DQ], TT), ALU.mult))
                    rope(kr[:, :, 0:HR], kr[:, :, HR:DR], cos_sin[:, :, 0, :], cos_sin[:, :, 1, :], s1, s2)
                elif kind == "latent_turns":
                    for b in range(2):
                        turn_lo_parts(b0 + b, t1_hi, t1_lo, 2 * b, lambda k: qlat_g[:, l, k:k + 1])
                    turn_lo_parts(b0 + 2, t1_hi, t1_lo, KQ, lambda k: kvlat_g[:, l, k - KQ:k - KQ + 1])
                elif kind == "layer_stats":
                    wait_strip_read(dve, strip_at[l, "v", 1])
                    for t in range(TT):
                        for hf in range(2):
                            op = nc.vector.bn_stats(stats[:, t, hf, :], vbuf[:, t, hf * 512:(hf + 1) * 512])
                    link(op)
                    for t in range(TT):
                        op = nc.vector.bn_aggr(mean_var[:, t, :], stats[:, t, :, :])
                    link(op)
                    root(small[:, 14:16], mean_var[:, :, 1], 1.0, 4 * EPS, 2)
                elif kind == "layer_norm":
                    t = step[2]
                    dve.wait_ge(ln_landed, 32 * (l + 1))
                    v = vbuf[:, t, :]
                    link(ts(v, v, mean_var[:, t, 0:1], small[:, 14 + t:15 + t], ALU.subtract, ALU.mult))
                    link(tt(v, v, ln_rows[:, 0, :], ALU.mult))
                    tt(v, v, ln_rows[:, 1, :], ALU.add).then_inc(v_normed, 1)
                elif kind == "a_turns":
                    for b in range(2):
                        bb = b0 + b
                        turn_lo_parts(bb, t1_hi, t1_lo, 4 * step[2] + 2 * b, lambda k: 1.0)
                elif kind == "merged_turns":
                    for b in range(2):
                        turn_lo_parts(b0 + b, act_hi, act_lo, 4 * step[2] + 2 * b, lambda k: 0.5)
                elif kind == "hidden_turn":
                    turn_lo_parts(b0, hid_hi, hid_lo, 2 * step[2], lambda k: 1.0)
                elif kind == "head_sums":
                    if not l and step[2] == "q":
                        dve.wait_ge(small_landed, 16 * 4 * L)
                        nc.vector.memset(qk_gain[DN:DQ, :], 1.0)
                        tt(qk_gain[0:DN, :], gain_q[0:DN, :], gain_k[0:DN, :], ALU.mult)
                        ts(b_sp, b_sp, 0.5, None, ALU.mult).then_inc(qk_gain_ready, 1)
                    v, w = (q_sum, DQ) if step[2] == "q" else (k_sum, DN)
                    for t in range(TT):
                        for hf in range(2):
                            sum_squares(v[:, t, 8 * hf:8 * hf + 8], w)
                    dve.wait_ge(head_sums, counts["heads"])
                    flat = v[:].rearrange("p t h -> p (t h)")
                    if step[2] == "q":
                        root(flat, flat, 1.0, DQ * EPS, TT * H)
                    else:
                        link(tt(v[:], v[:], over(small[:, 12:14], H), ALU.add))
                        root(flat, flat, 1.0 / DQ, EPS, TT * H)
                elif kind == "q_rope":
                    q = qb[:].rearrange("p t h d -> p (t h) d")[:, :, DN:DQ]
                    link(tt(q, q, each(q_gain[:, l, DN:DQ], TT * H), ALU.mult))
                    s1, s2 = (v.rearrange("p (t h r) -> p t h r", t=TT, h=H) for v in (prob_t[:, 0:TT * H * HR], qk_t[:, 0, :]))
                    rope(qb[:, :, :, DN:DN + HR], qb[:, :, :, DN + HR:DQ], each_head(cos_sin[:, :, 0, :]),
                         each_head(cos_sin[:, :, 1, :]), s1, s2, q_ready)
                elif kind == "k_scale":
                    k = kb[:].rearrange("p t h d -> p (t h) d")[:, :, 0:DN]
                    ks = k_sum[:].rearrange("p t h -> p (t h)")
                    tt(k, k, over(ks, DN), ALU.mult)
                    tt(kb[:, :, :, DN:DQ], each_head(kr[:]), k_sum[:].rearrange("p t (h o) -> p t h o", o=1)
                       .to_broadcast([P, TT, H, DR]), ALU.mult).then_inc(k_ready, 1)
                elif kind == "branch":
                    j = step[2]
                    cols = slice(j * STRIP, (j + 1) * STRIP)
                    wait_strip_read(dve, strip_at[l, "u", j])
                    wait_turn_read(dve, last_turn["mix_tokens", l])
                    wait_turn_read(dve, last_turn["mix_tokens", l] - 1)
                    tt(vbuf[:, :, cols], u_buf[:, j], vbuf[:, :, cols], ALU.mult).then_inc(branch_a, 1)
                elif kind == "attention":
                    s, b = step[2], b0
                    if s >= 3:
                        counts["split_turns"] += 1
                        dve.wait_ge(turn_hi, counts["split_turns"])
                        tt(bt_lo[:, s - 3, :], ps[:, 4 + b % 2, 0:S], bt_hi[:, s - 3, :].bitcast(F32),
                           ALU.subtract).then_inc(turn_free[b % 2], 1)
                        b += 1
                    if 1 <= s < PAIRS + 1:
                        n = PAIRS * l + s - 1
                        pr = probs[(s - 1) % 2]
                        p0 = pr[:, 0:2 * P].rearrange("p (h k) -> p h k", h=2)
                        p1 = pr[:, 2 * P:2 * P + 2 * S].rearrange("p (h k) -> p h k", h=2)
                        if s >= 3:
                            dve.wait_ge(turn_done, prob_turn[l, s - 3] + 2)
                        else:
                            dve.wait_ge(head_sums, counts["heads"])
                        if n:
                            dve.wait_ge(prob_ready, n)
                        dve.wait_ge(scores_done, n + 1)
                        nc.vector.tensor_reduce(soft[:, 2, 0:2], ps[:, 6, 0:2 * P].rearrange("p (h k) -> p h k", h=2),
                                                AX.X, ALU.max)
                        link(nc.vector.tensor_reduce(soft[:, 2, 2:4], ps[:, 7, :].rearrange("p (h k) -> p h k", h=2),
                                                     AX.X, ALU.max))
                        soft4 = soft[:].rearrange("p a (t h) -> p a t h", t=TT)
                        stt(soft4[:, 0], soft4[:, 2], -1.0, q_sum[:, :, 2 * (s - 1):2 * s], ALU.mult,
                            ALU.mult).then_inc(max_ready, 1)
                        dve.wait_ge(exp_done, n + 1)
                        link(nc.vector.reciprocal(soft[:, 2, :], soft[:, 1, :]))
                        tt(p0, p0, over(soft[:, 2, 0:2], P), ALU.mult)
                        tt(p1, p1, over(soft[:, 2, 2:4], S), ALU.mult).then_inc(prob_ready, 1)
                elif kind == "split":
                    splits(step[2], step[2] + 1)
                elif kind == "evac":
                    _, _, what, j = step
                    n, end = strip_at[l, what, j], chunk_end[l, what, j]
                    bank = ps[:, 2 * (n % 2):2 * (n % 2) + 2, :]
                    free = strip_free[n % 2]
                    cols = slice(j * STRIP, (j + 1) * STRIP)
                    if what in ("v", "u"):
                        m = 4 * l + (2 if what == "u" else 0) + j
                        dve.wait_ge(gelu_sq, m + 1)
                        g = u_buf[:, j] if what == "u" else tmp[:]
                        stt(g, g, 1.0 / GELU_A, bank, ALU.add, ALU.mult).then_inc(gelu_arg, 1)
                        dve.wait_ge(gelu_tanh, m + 1)
                        if what == "v":
                            stt(vbuf[:, :, cols], tmp[:], 1.0, bank, ALU.add, ALU.mult).then_inc(free, 1)
                        else:
                            stt(g, g, 1.0, bank, ALU.add, ALU.mult).then_inc(free, 1)
                    elif what in ("pa", "pb"):
                        wait_strip_read(dve, strip_at[l, "g" + what[1], j])
                        dve.wait_ge(chunk_used, end)
                        if what == "pa":
                            stt(vbuf[:, :, cols], tmp[:], 1.0, bank, ALU.add, ALU.mult).then_inc(free, 1)
                        else:
                            stt(gate_b[j], gate_b[j], 1.0, bank, ALU.add, ALU.mult).then_inc(free, 1)
                            wait_strip_read(dve, n)
                            wait_strip_read(dve, strip_at[l, "pa", j])
                            tt(vbuf[:, :, cols], vbuf[:, :, cols], gate_b[j], ALU.add).then_inc(merged_b, 1)
                    elif what == "wo":
                        dve.wait_ge(chunk_used, end)
                        for t in range(TT):
                            tt(xres[:, t, cols], xres[:, t, cols], bank[:, t, :], ALU.add).then_inc(free if t else x_added, 1)
                    elif what == "gu":
                        dve.wait_ge(sig_done, j + 1)
                        if j >= 2:
                            dve.wait_ge(turn_done, last_turn["hidden_turn", l, j - 2] + 1)
                        if not j:
                            dve.wait_ge(ffn_scale_ready, l // 2 + 1)
                        link(stt(sig[:], sig[:], 1.0, bank[:, :, 0:HC], ALU.add, ALU.mult))
                        for t in range(TT):
                            op = stt(hid[:, j % 2, t, :], sig[:, t, :], ffn_scale[:, TT + t:TT + t + 1],
                                     bank[:, t, HC:2 * HC], ALU.mult, ALU.mult)
                        op.then_inc(free, 1)
                elif kind == "router":
                    dve.wait_ge(wr_hi_done, 1)
                    tt(wr_lo[:], wr[:], wr_hi[:].bitcast(F32), ALU.subtract).then_inc(wr_lo_done, 1)
                elif kind == "down":
                    a, b, n = step[2:5]
                    splits(a, a + LAST_TURN)
                    turn_lo_parts(b0, hid_hi, hid_lo, 2 * (GUS - 1), lambda k: 1.0)
                    splits(a + LAST_TURN, b - 1)
                    dve.wait_ge(chunk_used, b)
                    for t in range(TT):
                        at = (2 * n + 2 * t) % 4
                        tt(xres[:, t, :], xres[:, t, :], ps[:, at:at + 2, :].rearrange("p a b -> p (a b)"),
                           ALU.add).then_inc(strip_free[(n + t) % 2], 1)

            dve.wait_ge(logits_done, 1)
            nc.vector.tensor_copy(logit_t[:], ps[0:E, 4, 0:S]).then_inc(logits_copied, 1)
            dve.wait_ge(logits_turned, 1)
            for t in range(TT):
                link(stt(logit[:, t, :], ps[:, 5, t * E:(t + 1) * E], small[:, 2 + t:3 + t], br[:], ALU.mult, ALU.add))
                link(nc.vector.max(top[:, t, :], logit[:, t, :]))
                link(nc.vector.max_index(top_i[:, t, :], top[:, t, :], logit[:, t, :]))
                link(nc.vector.tensor_copy(top_f[:, t, :], top_i[:, t, :]))
                ts(one_a[:, t, :], iota[:, 0:E], top_f[:, t, 0:1], None, ALU.is_equal)
                link(ts(one_b[:, t, :], iota[:, 0:E], top_f[:, t, 1:2], None, ALU.is_equal))
            tt(chosen[:], one_a[:], one_b[:], ALU.add).then_inc(chosen_ready, 1)
            dve.wait_ge(chosen_ready, 1)
            tt(rt[:, :, 0], top[:, :, 1], top[:, :, 0], ALU.subtract).then_inc(gap_ready, 1)
            dve.wait_ge(gap_exp, 1)
            link(ts(rt[:, :, 2], rt[:, :, 1], 1.0, None, ALU.add))
            link(nc.vector.reciprocal(rt[:, :, 3], rt[:, :, 2]))
            link(tt(rt[:, :, 2], rt[:, :, 1], rt[:, :, 3], ALU.mult))
            for t in range(TT):
                link(ts(combine[:, t, :], one_a[:, t, :], rt[:, t, 3:4], None, ALU.mult))
                link(stt(combine[:, t, :], one_b[:, t, :], rt[:, t, 2:3], combine[:, t, :], ALU.mult, ALU.add))
            dve.wait_ge(places_done, 1)
            link(ts(place[:], chosen[:], -4.0 * S, 4.0 * S, ALU.mult, ALU.add))
            link(tt(place[:], place[:], ps[:, 4, 0:TT * E].rearrange("p (t e) -> p t e", t=TT), ALU.add))
            link(nc.vector.tensor_reduce(most_f[:, 0:1], ps[:, 4, TT * E:(TT + 1) * E], AX.X, ALU.max))
            nc.vector.tensor_copy(most[:, 0:1], most_f[:, 0:1]).then_inc(counts_ready, 1)

            def moe_pass(r, z, held=None):
                def turn_part(e, j):
                    dve.wait_ge(z["hturn_hi"], GUS * e + j + 1)
                    tt(ehid_lo[:, 2 * j:2 * j + 2, :], ps[:, 4 + j % 2, 0:2 * P].rearrange("p (k s) -> p k s", k=2),
                       ehid_hi[:, 2 * j:2 * j + 2, :].bitcast(F32), ALU.subtract).then_inc(z[f"hturn_free{j % 2}"], 1)

                def gather_part(e, half):
                    dve.wait_ge(z["g_hi"], 1 + half if e is None else 2 * e + 3 + half)
                    for k in range(4):
                        kk = 4 * half + k
                        op = stt(act_lo[:, kk, 0:P], ps[:, 6 + half, k * P:(k + 1) * P], ffn_g[:, L - 1, kk:kk + 1],
                                 act_hi[:, kk, 0:P].bitcast(F32), ALU.mult, ALU.subtract)
                    op.then_inc(z[f"g_free{half}"], 1)

                def scattered(e, t, missing=0):
                    for hf in range(2):
                        dve.wait_ge(z["g_done"], g_done(e, 2 * t + hf) + 1 - missing)
                        xs = xres[:, t, hf * 512:(hf + 1) * 512]
                        op = tt(xs, xs, ps[:, 6 + hf, :], ALU.add)
                        if missing and t and hf:
                            op.then_inc(z["over"], 1)
                        else:
                            op.then_inc(z[f"g_free{hf}"], 1)

                def pick_tokens(e):
                    for t in range(TT):
                        at = place[:, t, e:e + 1] if isinstance(e, int) else place[:, t, bass.ds(e, 1)]
                        w = combine[:, t, e:e + 1] if isinstance(e, int) else combine[:, t, bass.ds(e, 1)]
                        ts(pick[:, t, :], iota, at, None, ALU.is_equal)
                        op = ts(pick_w[:, t:t + 1], w, 0.0, None, ALU.add)
                    op.then_inc(z["picked"], 1)

                def split(e, c, last):
                    if c < PER_EXPERT:
                        r.split_lo(dve, e, c, expert_size[c])
                    elif not last:
                        r.split_lo(dve, e + 1, c - PER_EXPERT, expert_size[c - PER_EXPERT])

                def body(e, last):
                    first = is_first(e)
                    for j in range(GUS):
                        if not first and j in (2, 4):
                            scattered(e, j // 2 - 1)
                        split(e, 2 * j + LEAD, last)
                        split(e, 2 * j + 1 + LEAD, last)
                        dve.wait_ge(z["sig_ready"], GUS * e + j + 1)
                        if j >= 2:
                            dve.wait_ge(z["hturn_done"], GUS * e + j - 1)
                        stt(sig[:, 0, :], sig[:, 0, :], 1.0, ps[:, j % 2, 0:HC], ALU.add, ALU.mult).then_inc(z["sig_half"], 1)
                        dve.wait_ge(z["sig_half"], GUS * e + j + 1)
                        stt(hid[:, j % 2, 0, :], sig[:, 0, :], 0.5, ps[:, j % 2, HC:2 * HC], ALU.mult,
                            ALU.mult).then_inc(z[f"gu_free{j % 2}"], 1)
                        if j >= 2:
                            turn_part(e, j - 2)
                        if not last and j == 8:
                            dve.wait_ge(z["g_done"], g_done(e, 5) + 1)
                            pick_tokens(e + 1)
                    for d in range(len(DOWN_K)):
                        split(e, GU_CHUNKS + d + LEAD, last)
                        if d == 1:
                            turn_part(e, GUS - 2)
                        if d == 3:
                            turn_part(e, GUS - 1)
                        if not last and d in (5, 7):
                            gather_part(e, (d - 5) // 2)
                    dve.wait_ge(z["y_hi_done"], e + 1)
                    stt(y_lo[:], ps[:, 2:4, :].rearrange("p a b -> p (a b)"), slot_w[:, 0:1], y_hi[:].bitcast(F32),
                        ALU.mult, ALU.subtract).then_inc(z["y_split"], 1)

                pick_tokens(0)
                if held is not None:
                    moe_ring.split_lo(dve, 0, held)
                gather_part(None, 0)
                gather_part(None, 1)
                body(0, False)
                with dve.Fori(1, E - 1) as e:
                    body(e, False)
                body(E - 1, True)
                scattered(E, 0, 2)
                scattered(E, 1, 2)

            moe_pass(moe_ring, pass_sems[0], LEAD - 1)
            dve.wait_ge(counts_ready, 1)
            crowded = dve.value_load(most[0:1, 0:1], min_val=0, max_val=S)
            with dve.If(crowded > P):
                dve.wait_ge(pass_sems[0]["over"], 1)
                link(ts(place[:], place[:], -float(P), None, ALU.add))
                for c in range(LEAD):
                    moe_ring2.split_lo(dve, 0, c)
                moe_pass(moe_ring2, pass_sems[1])


def shape_tables(S, DR, theta):
    import numpy as np
    i = np.arange(P)
    eye = np.eye(P)
    before = (i[:, None] < i[None, :])
    ones = np.ones((P, P))
    iota = np.broadcast_to(i, (P, P))
    mask = np.concatenate([np.zeros((P, P)), np.where(i[None, :] <= i[:, None], 0.0, NEG)], 1)
    pos = np.arange(S, dtype=np.float32)
    inv = np.float32(theta) ** (-np.arange(0, DR, 2, dtype=np.float32) / np.float32(DR))
    ang = pos[:, None] * inv[None, :]
    cs = np.stack([np.cos(ang), np.sin(ang)], 1).reshape(S // P, P, DR).transpose(1, 0, 2).reshape(P, -1)
    return np.ascontiguousarray(np.concatenate([eye, before, ones, iota, cs, mask], 1).astype(np.float32))


_INS = ["x", "mix_norm_g", "w_in", "gm_v_norm_g", "gm_v_norm_b", "gm_w_spatial", "gm_b_spatial", "gm_w_proj",
        "mla_q_lat_g", "mla_w_uq", "mla_kv_lat_g", "mla_w_ukv", "mla_q_norm_g", "mla_k_norm_g", "mla_w_proj",
        "w_out", "ffn_norm_g", "dense_w_gu", "dense_w_down", "moe_w_router", "moe_b_router", "moe_w_gu",
        "moe_w_down"]


def kernel(**inputs):
    import numpy as np
    import concourse.bacc as bacc
    from concourse.bass_utils import run_bass_kernel_spmd

    nc = bacc.Bacc("TRN2", target_bir_lowering=False, num_devices=1)
    arrays, args = {}, []
    for name in _INS:
        a = np.ascontiguousarray(inputs[name])
        arrays[f"in_{name}"] = a
        args.append(nc.dram_tensor(f"in_{name}", a.shape, mybir.dt.from_np(a.dtype), kind="ExternalInput").ap())
    tables = shape_tables(256, 32, 10000.0)
    arrays["shape_consts"] = tables
    args.append(nc.dram_tensor("shape_consts", tables.shape, F32, kind="ExternalInput").ap())
    args.append(nc.dram_tensor("out", (1, 256, 1024), F32, kind="ExternalOutput").ap())
    decoder_trunk(nc, *args)
    r = run_bass_kernel_spmd(nc, [arrays], core_ids=[0])
    return r.results[0]["out"]
```
